# Optimizing a Trainium2 kernel written in Bass

```python
import math
import jax
import jax.numpy as jnp
from jax import lax
import numpy as np

D_MODEL = 1024
BATCH = 1
SEQ = 1024
DEPTH = 1
DEC_BATCH = 8
DEC_SEQ = 4
PAST_LEN = 1024
PAGE_SIZE = 128

HEAD_DIM = 64
MIX_W = D_MODEL
N_HEADS = MIX_W // HEAD_DIM
H_FOX = N_HEADS // 2
H_NSA = N_HEADS - H_FOX
NSA_KV = 2
NSA_GH = H_NSA // NSA_KV
FOX_W = H_FOX * HEAD_DIM
NSA_W = H_NSA * HEAD_DIM
KV_W = NSA_KV * HEAD_DIM
CMP_LEN = 32
CMP_STRIDE = 16
CMP_HID = 4 * HEAD_DIM
SEL_LEN = 64
N_SELECT = 16
WINDOW = 512
Q_BLOCK = 128
N_BUCKETS = 32
MAX_DISTANCE = 128
D_FF = ((8 * D_MODEL // 3 + 127) // 128) * 128
CONV_W = 3
FORGET_BIAS = 4.0
IN_COLS = 3 * FOX_W + H_FOX + NSA_W + 6 * KV_W + 3 * H_NSA
EPS = 1e-6
NEG = -1e30
TINY = 1e-30
FORCE_SCORE = 1e4
SCALE = HEAD_DIM ** -0.5

kernel_name = 'hymba_fox_nsa_convffn_step'

def rmsnorm(x, g):
    xf = x.astype(jnp.float32)
    r = lax.rsqrt(jnp.mean(xf * xf, axis=-1, keepdims=True) + EPS)
    return (xf * r).astype(x.dtype) * g

def masked_softmax(s, mask):
    s = jnp.where(mask, s, NEG)
    m = jnp.max(s, axis=-1, keepdims=True)
    p = jnp.where(mask, jnp.exp(s - m), 0.0)
    return p / jnp.maximum(jnp.sum(p, axis=-1, keepdims=True), TINY)

def rel_bucket(dist):
    n = jnp.maximum(dist, 0)
    exact = N_BUCKETS // 2
    nf = jnp.maximum(n, 1).astype(jnp.float32)
    far = exact + (jnp.log(nf / exact) / math.log(MAX_DISTANCE / exact) * (N_BUCKETS - exact)).astype(jnp.int32)
    return jnp.where(n < exact, n, jnp.minimum(far, N_BUCKETS - 1))

def project(h, w_in, b_forget):
    B, T = h.shape[:2]
    z = h @ w_in
    sizes = (FOX_W, FOX_W, FOX_W, H_FOX, NSA_W) + (KV_W,) * 6 + (3 * H_NSA,)
    parts = jnp.split(z, np.cumsum(sizes)[:-1].tolist(), axis=-1)
    fox = [p.reshape(B, T, H_FOX, HEAD_DIM) for p in parts[0:3]]
    kvs = [p.reshape(B, T, NSA_KV, HEAD_DIM) for p in parts[5:11]]
    return {
        'q_fox': fox[0],
        'fox_kv': jnp.stack([fox[1], fox[2]], axis=2),
        'logf': jax.nn.log_sigmoid((parts[3] + b_forget).astype(jnp.float32)),
        'q_nsa': parts[4].reshape(B, T, NSA_KV, NSA_GH, HEAD_DIM),
        'nsa_kv': jnp.stack(kvs[0:4], axis=2),
        'win_kv': jnp.stack(kvs[4:6], axis=2),
        'gates': jax.nn.sigmoid(parts[11].reshape(B, T, 3, NSA_KV, NSA_GH)),
    }

def fox_attend(q, q_cum, q_pos, k, v, k_cum, k_pos):
    s = jnp.einsum('bqhd,bkhd->bhqk', q, k).astype(jnp.float32) * SCALE
    s = s + (q_cum.transpose(0, 2, 1)[:, :, :, None] - k_cum.transpose(0, 2, 1)[:, :, None, :])
    p = masked_softmax(s, k_pos[None, :] <= q_pos[:, None])
    return jnp.einsum('bhqk,bkhd->bqhd', p.astype(v.dtype), v)

def fox_prompt(q, fox_kv, logf):
    B, S = q.shape[:2]
    cum = jnp.cumsum(logf, axis=1)
    k, v = fox_kv[:, :, 0], fox_kv[:, :, 1]
    pos = jnp.arange(S)

    def block(i):
        qs = i * Q_BLOCK
        return fox_attend(lax.dynamic_slice_in_dim(q, qs, Q_BLOCK, 1),
                          lax.dynamic_slice_in_dim(cum, qs, Q_BLOCK, 1),
                          qs + jnp.arange(Q_BLOCK), k, v, cum, pos)

    o = lax.map(block, jnp.arange(S // Q_BLOCK))
    return o.transpose(1, 0, 2, 3, 4).reshape(B, S, FOX_W)

def fox_sample(q, kv_new, logf_new, kv_past, logf_past):
    B, Tq = q.shape[:2]
    past = kv_past.shape[1]
    kv = jnp.concatenate([kv_past, kv_new.astype(kv_past.dtype)], axis=1)
    lf = jnp.concatenate([logf_past.astype(jnp.float32), logf_new.astype(jnp.float32)], axis=1)
    cum = jnp.cumsum(lf, axis=1)
    o = fox_attend(q, cum[:, past:], past + jnp.arange(Tq), kv[:, :, 0], kv[:, :, 1], cum,
                   jnp.arange(past + Tq))
    return o.reshape(B, Tq, FOX_W)

def compress(rows, pos, w1, b1, w2):
    B, T = rows.shape[:2]
    c = rows.reshape(B, T // CMP_STRIDE, CMP_STRIDE, NSA_KV, HEAD_DIM)
    blocks = jnp.concatenate([c[:, :-1], c[:, 1:]], axis=2) + pos[None, None, :, None, :]
    n_cmp = blocks.shape[1]
    flat = blocks.transpose(0, 1, 3, 2, 4).reshape(B, n_cmp, NSA_KV, CMP_LEN * HEAD_DIM)
    return jax.nn.gelu(flat @ w1 + b1) @ w2

def nsa_branch_keys(rows, cmp_l):
    pos, w1, b1, w2 = cmp_l
    B, T = rows.shape[:2]
    kc = compress(rows[:, :, 0], pos[0], w1[0], b1[0], w2[0])
    vc = compress(rows[:, :, 1], pos[1], w1[1], b1[1], w2[1])
    sel = rows[:, :, 2:4].reshape(B, T // SEL_LEN, SEL_LEN, 2, NSA_KV, HEAD_DIM).transpose(3, 0, 4, 1, 2, 5)
    return kc, vc, sel[0], sel[1]

def cmp_to_sel(n_cmp, n_sel):
    start = jnp.arange(n_cmp) * CMP_STRIDE
    js = jnp.arange(n_sel) * SEL_LEN
    return ((start[:, None] < js[None, :] + SEL_LEN) & (start[:, None] + CMP_LEN > js[None, :])).astype(jnp.float32)

def nsa_attend(q, q_pos, kc, vc, ks_b, vs_b, kw, vw, kw_pos, gates, rel_bias):
    B, Tq = q.shape[:2]
    rb = rel_bias.reshape(N_BUCKETS, NSA_KV, NSA_GH)
    n_cmp = kc.shape[1]
    dist_c = q_pos[:, None] - (jnp.arange(n_cmp) * CMP_STRIDE + (CMP_LEN - 1))[None, :]
    s_c = jnp.einsum('bqghd,bngd->bghqn', q, kc).astype(jnp.float32) * SCALE
    s_c = s_c + rb[rel_bucket(dist_c)].transpose(2, 3, 0, 1)
    p_c = masked_softmax(s_c, dist_c >= 0)
    o_c = jnp.einsum('bghqn,bngd->bqghd', p_c.astype(vc.dtype), vc)
    n_sel = ks_b.shape[2]
    k_eff = min(N_SELECT, n_sel)
    p_slc = jnp.einsum('bghqn,nj->bqgj', p_c, cmp_to_sel(n_cmp, n_sel))
    jb = jnp.arange(n_sel)[None, :]
    qblk = (q_pos // SEL_LEN)[:, None]
    valid = jb * SEL_LEN <= q_pos[:, None]
    forced = (jb == 0) | (jb == qblk) | (jb == qblk - 1)
    score = jnp.where(forced[None, :, None, :], FORCE_SCORE, jnp.where(valid[None, :, None, :], p_slc, -1.0))
    top_s, idx = lax.top_k(score, k_eff)
    idx_t = idx.transpose(0, 2, 1, 3).reshape(B, NSA_KV, Tq * k_eff)
    bi = jnp.arange(B)[:, None, None]
    gi = jnp.arange(NSA_KV)[None, :, None]
    n_s = k_eff * SEL_LEN
    kg = ks_b[bi, gi, idx_t].reshape(B, NSA_KV, Tq, n_s, HEAD_DIM)
    vg = vs_b[bi, gi, idx_t].reshape(B, NSA_KV, Tq, n_s, HEAD_DIM)
    s_pos = (idx_t[..., None] * SEL_LEN + jnp.arange(SEL_LEN)).reshape(B, NSA_KV, Tq, n_s)
    dist_s = q_pos[None, None, :, None] - s_pos
    ok = jnp.repeat(top_s.transpose(0, 2, 1, 3) >= 0, SEL_LEN, axis=-1)
    bias_s = rb.transpose(1, 0, 2)[gi[..., None], rel_bucket(dist_s)].transpose(0, 1, 4, 2, 3)
    s_s = jnp.einsum('bqghd,bgqsd->bghqs', q, kg).astype(jnp.float32) * SCALE + bias_s
    p_s = masked_softmax(s_s, (ok & (dist_s >= 0))[:, :, None])
    o_s = jnp.einsum('bghqs,bgqsd->bqghd', p_s.astype(vg.dtype), vg)
    dist_w = q_pos[:, None] - kw_pos[None, :]
    mask_w = (dist_w >= 0) & (dist_w < WINDOW) & (kw_pos[None, :] >= 0)
    s_w = jnp.einsum('bqghd,bkgd->bghqk', q, kw).astype(jnp.float32) * SCALE
    s_w = s_w + rb[rel_bucket(dist_w)].transpose(2, 3, 0, 1)
    p_w = masked_softmax(s_w, mask_w)
    o_w = jnp.einsum('bghqk,bkgd->bqghd', p_w.astype(vw.dtype), vw)
    o = gates[:, :, 0][..., None] * o_c + gates[:, :, 1][..., None] * o_s + gates[:, :, 2][..., None] * o_w
    return o.reshape(B, Tq, NSA_W)

def nsa_prompt(q, nsa_kv, win_kv, gates, cmp_l, rel_bias):
    B, S = q.shape[:2]
    kc, vc, ks_b, vs_b = nsa_branch_keys(nsa_kv, cmp_l)
    kwp = jnp.pad(win_kv, ((0, 0), (WINDOW, 0), (0, 0), (0, 0), (0, 0)))

    def block(i):
        qs = i * Q_BLOCK
        kw = lax.dynamic_slice_in_dim(kwp, qs, WINDOW + Q_BLOCK, 1)
        kw_pos = qs - WINDOW + jnp.arange(WINDOW + Q_BLOCK)
        return nsa_attend(lax.dynamic_slice_in_dim(q, qs, Q_BLOCK, 1), qs + jnp.arange(Q_BLOCK),
                          kc, vc, ks_b, vs_b, kw[:, :, 0], kw[:, :, 1], kw_pos,
                          lax.dynamic_slice_in_dim(gates, qs, Q_BLOCK, 1), rel_bias)

    o = lax.map(block, jnp.arange(S // Q_BLOCK))
    return o.transpose(1, 0, 2, 3).reshape(B, S, NSA_W)

def nsa_sample(q, nsa_new, win_new, gates, nsa_past, win_buf, cmp_l, rel_bias):
    B, Tq = q.shape[:2]
    past = nsa_past.shape[1]
    t_all = past + Tq
    t_pad = -(-t_all // SEL_LEN) * SEL_LEN
    rows = jnp.concatenate([nsa_past, nsa_new.astype(nsa_past.dtype)], axis=1)
    rows = jnp.pad(rows, ((0, 0), (0, t_pad - t_all), (0, 0), (0, 0), (0, 0)))
    kc, vc, ks_b, vs_b = nsa_branch_keys(rows, cmp_l)
    w_buf = win_buf.shape[1]
    kw = jnp.concatenate([win_buf, win_new.astype(win_buf.dtype)], axis=1)
    kw_pos = past - w_buf + jnp.arange(w_buf + Tq)
    o = nsa_attend(q, past + jnp.arange(Tq), kc, vc, ks_b, vs_b, kw[:, :, 0], kw[:, :, 1], kw_pos, gates, rel_bias)
    return o, kw[:, -w_buf:]

def merge_heads(o_fox, o_nsa, g, w_out):
    o = jnp.concatenate([rmsnorm(o_fox, g[:FOX_W]), rmsnorm(o_nsa, g[FOX_W:])], axis=-1)
    return o @ w_out

def conv_ffn(x, hist, g_norm, w_gu, conv_w, conv_b, w_down):
    T = x.shape[1]
    gu = rmsnorm(x, g_norm) @ w_gu
    g, u = gu[..., :D_FF], gu[..., D_FF:]
    g_ext = jnp.concatenate([hist.astype(g.dtype), g], axis=1)
    gc = conv_b
    for i in range(CONV_W):
        gc = gc + conv_w[i] * g_ext[:, i:i + T]
    y = (jax.nn.silu(gc) * u) @ w_down
    return x + y, g_ext[:, -(CONV_W - 1):]

def setup_inputs(seed: int = 0) -> dict:
    key = jax.random.key(seed)
    ks = jax.random.split(key, 24)
    n_pages = PAST_LEN // PAGE_SIZE
    n_used = DEC_BATCH * n_pages
    n_pool = n_used + max(1, n_used // 4)
    w_buf = min(WINDOW, PAST_LEN)

    def nrm(k, shape, s=1.0):
        return s * jax.random.normal(k, shape, jnp.float32)

    page_table = jax.random.permutation(ks[0], n_pool)[:n_used].reshape(DEC_BATCH, n_pages).astype(jnp.int32)
    return {
        'x_prompt': nrm(ks[1], (BATCH, SEQ, D_MODEL)),
        'x_sample': nrm(ks[2], (DEC_BATCH, DEC_SEQ, D_MODEL)),
        'cache_fox_kv': nrm(ks[3], (DEPTH, n_pool, PAGE_SIZE, 2, H_FOX, HEAD_DIM)),
        'cache_fox_logf': jax.nn.log_sigmoid(FORGET_BIAS + nrm(ks[4], (DEPTH, n_pool, PAGE_SIZE, H_FOX))),
        'cache_nsa_kv': nrm(ks[5], (DEPTH, n_pool, PAGE_SIZE, 4, NSA_KV, HEAD_DIM)),
        'state_win_kv': nrm(ks[6], (DEPTH, DEC_BATCH, w_buf, 2, NSA_KV, HEAD_DIM)),
        'state_conv': nrm(ks[7], (DEPTH, DEC_BATCH, CONV_W - 1, D_FF)),
        'page_table': page_table,
        'norm1_g': 1.0 + nrm(ks[8], (DEPTH, D_MODEL), 0.05),
        'w_in': nrm(ks[9], (DEPTH, D_MODEL, IN_COLS), D_MODEL ** -0.5),
        'b_forget': FORGET_BIAS + nrm(ks[10], (DEPTH, H_FOX), 0.1),
        'cmp_pos': nrm(ks[11], (DEPTH, 2, CMP_LEN, HEAD_DIM), 0.1),
        'cmp_w1': nrm(ks[12], (DEPTH, 2, CMP_LEN * HEAD_DIM, CMP_HID), (CMP_LEN * HEAD_DIM) ** -0.5),
        'cmp_b1': nrm(ks[13], (DEPTH, 2, CMP_HID), 0.01),
        'cmp_w2': nrm(ks[14], (DEPTH, 2, CMP_HID, HEAD_DIM), CMP_HID ** -0.5),
        'out_norm_g': 1.0 + nrm(ks[15], (DEPTH, MIX_W), 0.05),
        'w_out': nrm(ks[16], (DEPTH, MIX_W, D_MODEL), MIX_W ** -0.5),
        'norm2_g': 1.0 + nrm(ks[17], (DEPTH, D_MODEL), 0.05),
        'w_gu': nrm(ks[18], (DEPTH, D_MODEL, 2 * D_FF), D_MODEL ** -0.5),
        'conv_w': nrm(ks[19], (DEPTH, CONV_W, D_FF), CONV_W ** -0.5),
        'conv_b': nrm(ks[20], (DEPTH, D_FF), 0.01),
        'w_down': nrm(ks[21], (DEPTH, D_FF, D_MODEL), D_FF ** -0.5),
        'rel_bias': nrm(ks[22], (N_BUCKETS, H_NSA), 0.3),
        'final_norm_g': 1.0 + nrm(ks[23], (D_MODEL,), 0.05),
    }

def reference(x_prompt, x_sample, cache_fox_kv, cache_fox_logf, cache_nsa_kv, state_win_kv, state_conv,
              page_table, norm1_g, w_in, b_forget, cmp_pos, cmp_w1, cmp_b1, cmp_w2, out_norm_g, w_out,
              norm2_g, w_gu, conv_w, conv_b, w_down, rel_bias, final_norm_g):
    n_dec, n_pages = page_table.shape
    past = n_pages * PAGE_SIZE
    bp, sp = x_prompt.shape[:2]
    xp, xs = x_prompt, x_sample
    fkv_p, fkv_s, flf_p, flf_s, nkv_p, nkv_s, win_p, win_s, cv_p, cv_s = ([] for _ in range(10))
    for l in range(DEPTH):
        cmp_l = (cmp_pos[l], cmp_w1[l], cmp_b1[l], cmp_w2[l])
        pp = project(rmsnorm(xp, norm1_g[l]), w_in[l], b_forget[l])
        o_fox = fox_prompt(pp['q_fox'], pp['fox_kv'], pp['logf'])
        o_nsa = nsa_prompt(pp['q_nsa'], pp['nsa_kv'], pp['win_kv'], pp['gates'], cmp_l, rel_bias)
        xp = xp + merge_heads(o_fox, o_nsa, out_norm_g[l], w_out[l])
        xp, conv_new_p = conv_ffn(xp, jnp.zeros((bp, CONV_W - 1, D_FF), xp.dtype), norm2_g[l], w_gu[l],
                                  conv_w[l], conv_b[l], w_down[l])
        ps = project(rmsnorm(xs, norm1_g[l]), w_in[l], b_forget[l])
        fox_past = cache_fox_kv[l, page_table].reshape(n_dec, past, 2, H_FOX, HEAD_DIM)
        logf_past = cache_fox_logf[l, page_table].reshape(n_dec, past, H_FOX)
        nsa_past = cache_nsa_kv[l, page_table].reshape(n_dec, past, 4, NSA_KV, HEAD_DIM)
        o_fox_s = fox_sample(ps['q_fox'], ps['fox_kv'], ps['logf'], fox_past, logf_past)
        o_nsa_s, win_new_s = nsa_sample(ps['q_nsa'], ps['nsa_kv'], ps['win_kv'], ps['gates'], nsa_past,
                                        state_win_kv[l], cmp_l, rel_bias)
        xs = xs + merge_heads(o_fox_s, o_nsa_s, out_norm_g[l], w_out[l])
        xs, conv_new_s = conv_ffn(xs, state_conv[l], norm2_g[l], w_gu[l], conv_w[l], conv_b[l], w_down[l])
        fkv_p.append(pp['fox_kv'])
        fkv_s.append(ps['fox_kv'])
        flf_p.append(pp['logf'])
        flf_s.append(ps['logf'])
        nkv_p.append(pp['nsa_kv'])
        nkv_s.append(ps['nsa_kv'])
        win_p.append(pp['win_kv'][:, -min(WINDOW, sp):])
        win_s.append(win_new_s)
        cv_p.append(conv_new_p)
        cv_s.append(conv_new_s)
    y_prompt = rmsnorm(xp, final_norm_g)
    y_sample = rmsnorm(xs, final_norm_g)
    return (y_prompt, y_sample,
            jnp.stack(fkv_p), jnp.stack(fkv_s),
            jnp.stack(flf_p), jnp.stack(flf_s),
            jnp.stack(nkv_p), jnp.stack(nkv_s),
            jnp.stack(win_p), jnp.stack(win_s),
            jnp.stack(cv_p), jnp.stack(cv_s))


_drawn_inputs = setup_inputs


def setup_inputs(seed=0):
    import zlib

    import numpy as np

    out = dict(_drawn_inputs(seed))
    spreads = {}
    factors = {'cmp_b1': 6.128, 'conv_b': 8.0}
    for name, (base, spread) in spreads.items():
        noise = np.random.default_rng([zlib.crc32(name.encode()), seed]).standard_normal(out[name].shape)
        drawn = base * np.exp(spread * noise) if base else spread * noise
        out[name] = jnp.asarray(drawn.astype(out[name].dtype))
    for name, factor in factors.items():
        out[name] = (out[name] * factor).astype(out[name].dtype)
    return out
```

```python
import math
from contextlib import ExitStack

import numpy as np

import concourse.bass as bass
from concourse import mybir

F32 = mybir.dt.float32
BF16 = mybir.dt.bfloat16
FR = mybir.dt.float32r
I32 = mybir.dt.int32
ALU = mybir.AluOpType
ACT = mybir.ActivationFunctionType
AX = mybir.AxisListType.X
ds = bass.ds

P = 128
D = 1024
T = 1024
NB, NQ = 8, 4
NS = NB * NQ
TT = T + NS
NT = T // P
KD = D // P
HD = 64
H = 8
G = 2
GH = H // G
HQ = H * NQ
PAGES = 8
NSTR, CLEN = 16, 32
NC = T // NSTR - 1
NSEL = T // HD + 1
WIN = 512
NBK = 32
FF = 2816
NF = FF // P
EPS = 1e-6
NEG = -1e30
C_QF, C_KF, C_VF, C_F, C_QN, C_NSA, C_WIN, C_GATE, C_END = 0, 512, 1024, 1536, 1544, 2056, 2568, 2824, 2848
ROWS = [P] * NT + [NS]
CH = TT // 3


class Chain:

    def __init__(self, eng, sem):
        self.eng, self.sem, self.done, self.at = eng, sem, 0, 0

    def enter(self, i, per):
        self.at, self.k, self.per = self.done + i * per, 0, per

    def leave(self, n):
        assert self.k == self.per, (self.k, self.per)
        self.done += n * self.per
        self.at, self.k = self.done, 0

    k = 0

    def __call__(self, ins):
        ins.then_inc(self.sem, 1)
        self.k += 1
        self.eng.wait_ge(self.sem, self.at + self.k)


class Ctx:

    def __init__(self, nc, dram):
        self.nc, self.d = nc, dram


class Phase:

    def __init__(self, nc):
        self.nc, self.stack, self.sems = nc, ExitStack(), []

    def __enter__(self):
        self.stack.__enter__()
        return self

    def __exit__(self, *a):
        done = self.stack.__exit__(*a)
        if self.sems:
            self.nc.clear_and_free_semaphores(self.sems)
            self.nc.all_engine_barrier()
        return done

    def sb(self, name, shape, dt=F32):
        return self.stack.enter_context(self.nc.sbuf_tensor(name, shape, dt))

    def ps(self, name, shape, dt=F32):
        return self.stack.enter_context(self.nc.psum_tensor(name, shape, dt))

    def sem(self, name):
        self.sems.append(self.nc.alloc_semaphore(name))
        return self.sems[-1]

    def block(self):
        return self.stack.enter_context(self.nc.Block())


def split(ph, name, shape):
    return ph.sb(f"{name}_hi", shape, FR), ph.sb(f"{name}_lo", shape, FR)


def split_products(pe, out, a, b, at, bt, start, stop):
    pe.matmul(out, a[0][at], b[0][bt], start=start, stop=False)
    pe.matmul(out, a[0][at], b[1][bt], start=False, stop=False)
    return pe.matmul(out, a[1][at], b[0][bt], start=False, stop=stop)


def settled(eng, c):
    eng.sem_inc(c.passed, 1)


def norm_transpose(c, name, source, gain, groups, out):
    nc = c.nc
    W = D // groups
    with Phase(nc) as ph:
        x = ph.sb(f"{name}_x", [P, 2, D])
        xn = ph.sb(f"{name}_xn", [P, 2, D])
        sq = ph.sb(f"{name}_sq", [P, 2, D])
        g = ph.sb(f"{name}_gain", [P, D])
        ss = ph.sb(f"{name}_ss", [P, 9, groups])
        ms = ph.sb(f"{name}_ms", [P, 9, groups])
        rt = ph.sb(f"{name}_rt", [P, 9, groups])
        rr = ph.sb(f"{name}_rr", [P, 9, groups])
        tp = [ph.ps(f"{name}_tp{i}", [P, D]) for i in range(2)]
        s_x = [ph.sem(f"{name}_x_loaded{i}") for i in range(2)]
        s_g = ph.sem(f"{name}_gain_loaded")
        s_ss = ph.sem(f"{name}_squares")
        s_ms = ph.sem(f"{name}_mean")
        s_rt = ph.sem(f"{name}_root")
        s_rr = ph.sem(f"{name}_inverse")
        s_xn = ph.sem(f"{name}_normed")
        s_tr = ph.sem(f"{name}_transposed")
        s_ev = ph.sem(f"{name}_copied")
        s_lo = ph.sem(f"{name}_rest_kept")
        block = ph.block()

        @block.sync
        def _(sp):
            sp.dma_start(g[:, :], gain).then_inc(s_g, 16)
            for t, rows in enumerate(ROWS):
                if t >= 2:
                    sp.wait_ge(s_xn, t - 1)
                sp.dma_start(x[0:rows, t % 2, :], source(t)).then_inc(s_x[t % 2], 16)

        @block.scalar
        def _(act):
            def squares(t):
                rows = ROWS[t]
                act.wait_ge(s_x[t % 2], 16 * (t // 2 + 1))
                if t >= 2:
                    act.wait_ge(s_ss, groups * (t - 1))
                for k in range(groups):
                    act.activation(sq[0:rows, t % 2, k * W:(k + 1) * W], x[0:rows, t % 2, k * W:(k + 1) * W], ACT.Square,
                                   accum_out=ss[0:rows, t, k:k + 1]).then_inc(s_ss, 1)

            def root(t):
                rows = ROWS[t]
                act.wait_ge(s_ms, t + 1)
                act.activation(rt[0:rows, t, :], ms[0:rows, t, :], ACT.Sqrt).then_inc(s_rt, 1)

            def copy(t):
                rows = ROWS[t]
                act.wait_ge(s_tr, t + 1)
                act.activation(out[0][:, :, t * P:t * P + rows],
                               tp[t % 2][:, :].rearrange("p (k n) -> p k n", k=KD)[:, :, 0:rows],
                               ACT.Copy).then_inc(s_ev, 1)

            n = len(ROWS)
            squares(0)
            for t in range(n):
                if t + 1 < n:
                    squares(t + 1)
                root(t)
                if t >= 1:
                    copy(t - 1)
            copy(n - 1)

        @block.vector
        def _(dve):
            def mean(t):
                dve.wait_ge(s_ss, groups * (t + 1))
                dve.tensor_scalar(ms[0:ROWS[t], t, :], ss[0:ROWS[t], t, :], 1.0 / W, EPS, ALU.mult, ALU.add).then_inc(s_ms, 1)

            def rest(t):
                rows = ROWS[t]
                dve.wait_ge(s_ev, t + 1)
                dve.tensor_tensor(out[1][:, :, t * P:t * P + rows],
                                  tp[t % 2][:, :].rearrange("p (k n) -> p k n", k=KD)[:, :, 0:rows],
                                  out[0][:, :, t * P:t * P + rows], ALU.subtract).then_inc(s_lo, 1)

            mean(0)
            for t, rows in enumerate(ROWS):
                if t + 1 < len(ROWS):
                    mean(t + 1)
                dve.wait_ge(s_rt, t + 1)
                dve.reciprocal(rr[0:rows, t, :], rt[0:rows, t, :]).then_inc(s_rr, 1)
                dve.wait_ge(s_rr, t + 1)
                if t == 0:
                    dve.wait_ge(s_g, 16)
                if t >= 2:
                    dve.wait_ge(s_tr, t - 1)
                for k in range(groups):
                    ins = dve.scalar_tensor_tensor(
                        out=xn[0:rows, t % 2, k * W:(k + 1) * W], in0=x[0:rows, t % 2, k * W:(k + 1) * W],
                        scalar=rr[0:rows, t, k:k + 1], in1=g[0:rows, k * W:(k + 1) * W], op0=ALU.mult, op1=ALU.mult)
                ins.then_inc(s_xn, 1)
                if t >= 1:
                    rest(t - 1)
            rest(len(ROWS) - 1)

        @block.tensor
        def _(pe):
            for t, rows in enumerate(ROWS):
                pe.wait_ge(s_xn, t + 1)
                if t >= 2:
                    pe.wait_ge(s_lo, t - 1)
                for k in range(KD):
                    ins = pe.transpose(tp[t % 2][:, k * P:k * P + rows], xn[0:rows, t % 2, k * P:(k + 1) * P],
                                       c.ident[0:rows, 0:rows])
                ins.then_inc(s_tr, 1)


def setup(c):
    nc, d = c.nc, c.d
    with Phase(nc) as ph:
        ro = ph.sb("ro_rows", [H, 383])
        oh = ph.sb("oh_prompt", [NBK + 1, 383])
        ohc = ph.sb("oh_cmp", [NBK + 1, 16, P])
        ohs = ph.sb("oh_sample", [NBK + 1, NQ, 451])
        rel = ph.sb("rel_diff", [NBK, NBK + 1])
        one_last = ph.sb("one_last", [NBK + 1, 1])
        rb = ph.sb("rb", [NBK, H])
        rba = ph.sb("rba", [NBK + 1, H])
        rbx = ph.sb("rbx", [NBK + 1, NQ, H, NQ])
        ps_r = ph.ps("ps_r", [P, 512])
        ps_row = ph.ps("ps_row", [P, 512])
        ps_c = ph.ps("ps_c", [P, 16, H])
        ps_s = ph.ps("ps_s", [P, 512])
        s_ld = ph.sem("tables_loaded")
        s_id = ph.sem("fills")
        s_pe = ph.sem("table_products")
        s_v = ph.sem("table_copies")
        s_st = ph.sem("rows_stored")
        s_tb = ph.sem("toeplitz_stored")
        block = ph.block()

        @block.sync
        def _(sp):
            for dst, src in ((oh[:, :], d["c_oh"]), (ohc[:, :, :], d["c_cmp"]), (ohs[:, :, :], d["c_smp"]),
                             (rel[:, :], d["c_rel"]), (one_last[:, :], d["c_one"]), (rb[:, :], d["rel_bias"]),
                             (c.misc[:, :], d["c_misc"]), (c.pt[:, :], d["page_table"].rearrange("b p -> (b p)").rearrange("(a n) -> a n", a=1))):
                sp.dma_start(dst, src).then_inc(s_ld, 16)
            sp.wait_ge(s_v, 6)
            sp.dma_start(d["rep_d"], ro[:, :].rearrange("h (a n) -> h a n", a=1).to_broadcast([H, P, 383])).then_inc(s_st, 16)
            sp.wait_ge(s_st, 16)
            for h in range(H):
                sp.dma_start(d["tb_d"][h, :, :], bass.AP(d["rep_d"].tensor, h * P * 383 + 127, [[382, P], [1, 256]])).then_inc(s_tb, 16)
            sp.wait_ge(s_tb, 16 * H)

        @block.gpsimd
        def _(pool):
            pool.memset(c.ident[:, :], 0.0).then_inc(s_id, 1)
            pool.memset(c.ident16[:, :], 0.0).then_inc(s_id, 1)
            pool.memset(c.causal16[:, :], 0.0).then_inc(s_id, 1)
            pool.memset(c.cb[:, :, 0:47], 0.0).then_inc(s_id, 1)
            pool.memset(c.cb[:, :, 63:119], NEG).then_inc(s_id, 1)
            pool.memset(rbx[:, :, :, :], 0.0).then_inc(s_id, 1)
            pool.wait_ge(s_id, 6)
            for m in (c.ident, c.ident16):
                pool.affine_select(out=m[:, :], in_=m[:, :], compare_op=ALU.not_equal, fill=1.0, base=0,
                                   pattern=[[-1, P]], channel_multiplier=1).then_inc(s_id, 1)
            pool.affine_select(out=c.causal16[:, :], in_=c.causal16[:, :], compare_op=ALU.is_ge, fill=NEG, base=0,
                               pattern=[[-1, P]], channel_multiplier=1).then_inc(s_id, 1)
            pool.wait_ge(s_id, 9)
            pool.memset(c.one[:, :], 1.0)
            pool.memset(c.zero[:, :], 0.0)

        @block.tensor
        def _(pe):
            pe.wait_ge(s_ld, 16 * 8)
            pe.matmul(ps_r[0:NBK + 1, 0:H], rel[:, :], rb[:, :], start=True, stop=True).then_inc(s_pe, 1)
            pe.wait_ge(s_v, 1)
            pe.matmul(ps_row[0:H, 0:383], rba[:, :], oh[:, :], start=True, stop=True).then_inc(s_pe, 1)
            for m in range(16):
                ins = pe.matmul(ps_c[:, m, :], ohc[:, m, :], rba[:, :], start=True, stop=True)
            ins.then_inc(s_pe, 1)
            pe.wait_ge(s_v, 5)
            for q in range(NQ):
                ins = pe.matmul(ps_s[0:HQ, 0:451], rbx[:, q, :, :].rearrange("p h q -> p (h q)"), ohs[:, q, :],
                                start=(q == 0), stop=(q == NQ - 1))
            ins.then_inc(s_pe, 1)

        @block.vector
        def _(dve):
            dve.wait_ge(s_pe, 1)
            dve.tensor_scalar(rba[:, :], ps_r[0:NBK + 1, 0:H], one_last[:, 0:1], None, ALU.add).then_inc(s_v, 1)
            dve.wait_ge(s_v, 1)
            dve.wait_ge(s_id, 6)
            for q in range(NQ):
                dve.tensor_copy(rbx[:, q, :, q], rba[:, :]).then_inc(s_v, 1)
            dve.wait_ge(s_pe, 2)
            dve.tensor_copy(ro[:, :], ps_row[0:H, 0:383]).then_inc(s_v, 1)
            dve.wait_ge(s_pe, 3)
            dve.tensor_copy(c.cb[:, :, 47:63], ps_c[:, :, :].rearrange("p m h -> p h m")).then_inc(s_v, 1)
            dve.wait_ge(s_pe, 4)
            dve.tensor_copy(c.bias_s[:, :], ps_s[0:HQ, 0:451]).then_inc(s_v, 1)


def project_transposed(c):
    nc, d = c.nc, c.d
    w_in = d["w_in"][0].rearrange("(k p) n -> p k n", p=P)
    with Phase(nc) as ph:
        w = [ph.sb(f"wq{i}", [P, KD, P]) for i in range(2)]
        ws = [split(ph, f"wq_split{i}", [P, KD, P]) for i in range(2)]
        z = [ph.sb(f"qt{i}", [P, TT]) for i in range(2)]
        zs = [split(ph, f"qt_split{i}", [P, T]) for i in range(2)]
        acc = [ph.ps(f"q_acc{i}", [P, 3, 512]) for i in range(2)]
        s_w = [ph.sem(f"wq_loaded{i}") for i in range(2)]
        s_hi = ph.sem("wq_rounded")
        s_lo = ph.sem("wq_split")
        s_pe = ph.sem("q_products")
        s_z = ph.sem("q_copied")
        s_zh = ph.sem("q_rounded")
        s_zs = ph.sem("q_split")
        s_st = [ph.sem(f"q_stored{i}") for i in range(2)]
        s_free = ph.sem("q_store_ended")
        block = ph.block()

        @block.sync
        def _(sp):
            sp.sem_inc(s_lo, 2)
            with sp.Fori(0, 4) as i:
                for b, col in enumerate((C_QF, C_QN)):
                    sp.wait_ge(s_lo, 2 * i + b + 1)
                    sp.dma_start(w[b][:, :, :], w_in[:, :, ds(i * P + col, P)]).then_inc(s_w[b], 16)

        @block.vector
        def _(dve):
            def weights(i, b):
                dve.wait_ge(s_w[b], 16 * i + 16)
                dve.wait_ge(s_pe, 2 * i + b + 1)
                dve.tensor_copy(ws[b][0][:, :, :], w[b][:, :, :]).then_inc(s_hi, 1)
                dve.wait_ge(s_hi, 2 * i + b + 1)
                dve.tensor_tensor(ws[b][1][:, :, :], w[b][:, :, :], ws[b][0][:, :, :], ALU.subtract).then_inc(s_lo, 1)

            def queries(i, b):
                dve.wait_ge(s_z, 2 * i + b + 3)
                dve.tensor_copy(zs[b][0][:, :], z[b][:, 0:T]).then_inc(s_zh, 1)
                dve.wait_ge(s_zh, 2 * i + b + 1)
                dve.tensor_tensor(zs[b][1][:, :], z[b][:, 0:T], zs[b][0][:, :], ALU.subtract).then_inc(s_zs, 1)

            dve.sem_inc(s_pe, 2)
            weights(0, 0)
            with dve.Fori(0, 3) as i:
                weights(i, 1)
                queries(i, 0)
                weights(i + 1, 0)
                queries(i, 1)
            weights(3, 1)
            queries(3, 0)
            queries(3, 1)

        @block.tensor
        def _(pe):
            pe.sem_inc(s_z, 2)
            with pe.Fori(0, 4) as i:
                for b in range(2):
                    pe.wait_ge(s_lo, 2 * i + b + 3)
                    pe.wait_ge(s_z, 2 * i + b + 1)
                    for n in range(3):
                        for k in range(KD):
                            ins = split_products(pe, acc[b][:, n, 0:CH], ws[b], c.hT, np.s_[:, k, :], np.s_[:, k, n * CH:(n + 1) * CH],
                                                 k == 0, k == KD - 1)
                    ins.then_inc(s_pe, 1)

        @block.scalar
        def _(act):
            with act.Fori(0, 4) as i:
                for b in range(2):
                    act.wait_ge(s_pe, 2 * i + b + 3)
                    act.wait_ge(s_free, 2 * i + b + 1)
                    act.activation(z[b][:, :].rearrange("p (a n) -> p a n", a=3), acc[b][:, :, 0:CH], ACT.Copy, scale=HD ** -0.5)
                    act.activation(c.q_smp[:, b, ds(i, 1), :].rearrange("p a n -> p (a n)"), acc[b][:, 2, CH - NS:CH], ACT.Copy,
                                   scale=HD ** -0.5).then_inc(s_z, 1)

        @block.gpsimd
        def _(pool):
            pool.sem_inc(s_free, 2)
            with pool.Fori(0, 4) as i:
                for b, dst in enumerate(("qfs_d", "qns_d")):
                    pool.wait_ge(s_zs, 2 * i + b + 1)
                    settled(pool, c)
                    for w_ in range(2):
                        pool.dma_start(d[dst][w_].rearrange("h d n -> (h d) n")[ds(i * P, P), :], zs[b][w_][:, :]).then_inc(s_st[b], 16)
                    if b == 1:
                        pool.dma_start(d["qn_d"].rearrange("h d n -> (h d) n")[ds(i * P, P), :], z[b][:, 0:T]).then_inc(s_st[b], 16)
                    pool.wait_ge(s_st[b], (32 + 16 * b) * (i + 1))
                    pool.sem_inc(s_free, 1)


def project_rows(c):
    nc, d = c.nc, c.d
    w_in = d["w_in"][0].rearrange("(k p) n -> p k n", p=P)
    chunks = [("k_fox", C_KF, 512), ("v_fox", C_VF, 512), ("nsa", C_NSA, 512), ("win", C_WIN, 288)]
    out = {
        "k_fox": lambda t, n: d["fox_kv_p"][0, 0, t * P:t * P + P, 0, :, :].rearrange("n h d -> n (h d)") if t < NT
        else d["fox_kv_s"][0, :, :, 0, :, :].rearrange("b q h d -> (b q) (h d)"),
        "v_fox": lambda t, n: d["fox_kv_p"][0, 0, t * P:t * P + P, 1, :, :].rearrange("n h d -> n (h d)") if t < NT
        else d["fox_kv_s"][0, :, :, 1, :, :].rearrange("b q h d -> (b q) (h d)"),
        "nsa": lambda t, n: d["nsa_kv_p"][0, 0, t * P:t * P + P].rearrange("n a g d -> n (a g d)") if t < NT
        else d["nsa_kv_s"][0].rearrange("b q a g d -> (b q) (a g d)"),
        "win": lambda t, n: d["win_kv_p"][0, 0, t * P - WIN:t * P - WIN + P].rearrange("n a g d -> n (a g d)") if t < NT
        else d["win_kv_s"][0, :, WIN - NQ:WIN].rearrange("b q a g d -> b q (a g d)"),
    }
    steps = [(ci, t) for ci in range(4) for t in range(9)]
    KP = 2
    PIECES = KD // KP
    blocks_of = {"k_fox": (0, 4), "v_fox": (0, 0), "nsa": (256, 1), "win": (0, 1)}
    tsteps = [s for s, (ci, t) in enumerate(steps) if blocks_of[chunks[ci][0]][1]]

    def stored(s):
        ci, t = steps[s]
        return 1 if chunks[ci][0] != "win" else (t < NT) + (t >= NT - WIN // P)

    def stores(s):
        return sum(stored(m) for m in range(min(s, len(steps))) if m % 3 == s % 3)

    def uses(s):
        return sum(1 for ci, t in steps[:s] if chunks[ci][0] == "win")

    with Phase(nc) as ph:
        w = [ph.sb(f"w_rows{i}", [P, KD, 512]) for i in range(2)]
        ws = [split(ph, f"w_rows_split{i}", [P, KD, 512]) for i in range(2)]
        z = [ph.sb(f"z{i}", [P, 512]) for i in range(3)]
        kt = [split(ph, f"kt{i}", [P, 4, P]) for i in range(2)]
        fl = ph.sb("fl", [P, 9, 4, H])
        bf = ph.sb("bf", [P, H])
        lt = ph.sb("lt", [H, 9, P])
        cum = ph.sb("cum", [H, T])
        acc = [ph.ps(f"z_acc{i}", [P, 512]) for i in range(2)]
        tp = [ph.ps(f"z_tp{i}", [P, 4, P]) for i in range(2)]
        lp = [ph.ps(f"lf_tp{i}", [P, 4, P]) for i in range(3)]
        s_w = [ph.sem(f"w_rows_loaded{i}") for i in range(4)]
        s_hi = ph.sem("w_rows_rounded")
        s_lo = ph.sem("w_rows_split")
        s_b = ph.sem("b_forget_loaded")
        s_acc = ph.sem("z_products")
        s_z = ph.sem("z_copied")
        s_use = ph.sem("z_kept")
        s_tr = ph.sem("z_transposed")
        s_kh = ph.sem("kt_rounded")
        s_kt = ph.sem("kt_copied")
        s_o = [ph.sem(f"z_stored{i}") for i in range(3)]
        s_ks = [ph.sem(f"kt_stored{i}") for i in range(2)]
        s_lf = ph.sem("logf_steps")
        s_la = ph.sem("logf_table_steps")
        s_lt = ph.sem("logf_transposed")
        s_wc = ph.sem("window_carried")
        s_fo = ph.sem("logf_stored")
        s_gd = ph.sem("gates_stored")
        s_zero = ph.sem("zeroed")
        block = ph.block()

        @block.sync
        def _(sp):
            sp.dma_start(bf[:, :], d["b_forget"][0:1, :].to_broadcast([P, H])).then_inc(s_b, 16)
            sp.dma_start(d["win_kv_s"][0, :, 0:WIN - NQ], d["state_win_kv"][0, :, NQ:WIN]).then_inc(s_wc, 16)
            for ci, (kind, col, n) in enumerate(chunks):
                if ci >= 2:
                    sp.wait_ge(s_lo, PIECES * (ci - 1))
                if kind == "win":
                    sp.dma_start(w[ci % 2][:, :, 0:280], w_in[:, :, C_WIN:C_END]).then_inc(s_w[ci], 16)
                    sp.dma_start(w[ci % 2][:, :, 280:288], w_in[:, :, C_F:C_F + H]).then_inc(s_w[ci], 16)
                else:
                    sp.dma_start(w[ci % 2][:, :, :], w_in[:, :, col:col + n]).then_inc(s_w[ci], 16)
            sp.wait_ge(s_wc, 16)

        @block.tensor
        def _(pe):
            def transposes(n):
                s = tsteps[n]
                ci, t = steps[s]
                c0, nb = blocks_of[chunks[ci][0]]
                rows = ROWS[t]
                pe.wait_ge(s_z, s + 1)
                if n >= 2:
                    pe.wait_ge(s_kt, n - 1)
                for j in range(nb):
                    ins = pe.transpose(tp[n % 2][:, j, 0:rows], z[s % 3][0:rows, c0 + j * P:c0 + (j + 1) * P],
                                       c.ident[0:rows, 0:rows])
                ins.then_inc(s_tr, 1)

            n = 0
            for s, (ci, t) in enumerate(steps):
                rows = ROWS[t]
                width = chunks[ci][2]
                if s >= 2:
                    pe.wait_ge(s_z, s - 1)
                for k in range(KD):
                    if t == 0 and k % KP == 0:
                        pe.wait_ge(s_lo, PIECES * ci + k // KP + 1)
                    ins = split_products(pe, acc[s % 2][0:rows, 0:width], c.hT, ws[ci % 2], np.s_[:, k, t * P:t * P + rows],
                                         np.s_[:, k, 0:width], k == 0, k == KD - 1)
                ins.then_inc(s_acc, 1)
                if n < len(tsteps) and tsteps[n] < s:
                    transposes(n)
                    n += 1
            while n < len(tsteps):
                transposes(n)
                n += 1
            pe.wait_ge(s_lf, 2)
            for t, rows in enumerate(ROWS):
                ins = pe.transpose(lp[t // 4][0:H, t % 4, 0:rows], fl[0:rows, t, 3, :], c.ident[0:rows, 0:rows])
            ins.then_inc(s_lt, 1)

        def width(ci):
            return chunks[ci][2]

        @block.scalar
        def _(act):
            def rounded(ci):
                act.wait_ge(s_w[ci], 32 if ci == 3 else 16)
                if ci >= 2:
                    act.wait_ge(s_acc, 9 * (ci - 1))
                for k in range(0, KD, KP):
                    act.activation(ws[ci % 2][0][:, k:k + KP, 0:width(ci)], w[ci % 2][:, k:k + KP, 0:width(ci)], ACT.Copy).then_inc(s_hi, 1)

            rounded(0)
            for s, (ci, t) in enumerate(steps):
                rows = ROWS[t]
                if t == 1 and ci + 1 < len(chunks):
                    rounded(ci + 1)
                act.wait_ge(s_acc, s + 1)
                if s >= 3:
                    if stores(s):
                        act.wait_ge(s_o[s % 3], 16 * stores(s))
                    if uses(s - 2):
                        act.wait_ge(s_use, uses(s - 2))
                    m = sum(1 for q in tsteps if q <= s - 3)
                    if m:
                        act.wait_ge(s_tr, m)
                act.activation(z[s % 3][0:rows, 0:chunks[ci][2]], acc[s % 2][0:rows, 0:chunks[ci][2]], ACT.Copy).then_inc(s_z, 1)
            act.wait_ge(s_use, uses(len(steps)))
            act.activation(fl[:, :, 1, :], fl[:, :, 0, :], ACT.Abs).then_inc(s_la, 1)
            act.wait_ge(s_la, 1)
            act.activation(fl[:, :, 2, :], fl[:, :, 1, :], ACT.Exp, scale=-1.0).then_inc(s_la, 1)
            act.wait_ge(s_la, 2)
            act.activation(fl[:, :, 1, :], fl[:, :, 2, :], ACT.Ln, bias=1.0).then_inc(s_la, 1)
            act.activation(c.gates[:, :, :], c.gates[:, :, :], ACT.Exp, scale=-1.0).then_inc(s_la, 1)

        def stores_before(n):
            return sum(1 for m in range(n) if m % 2 == n % 2 and steps[tsteps[m]][1] < NT)

        @block.vector
        def _(dve):
            dve.memset(fl[:, NT, :, :], 0.0).then_inc(s_zero, 1)
            dve.memset(c.gates[:, NT, :], 0.0).then_inc(s_zero, 1)
            dve.wait_ge(s_zero, 2)
            n = 0

            def rests(ci):
                for k in range(0, KD, KP):
                    dve.wait_ge(s_hi, PIECES * ci + k // KP + 1)
                    dve.tensor_tensor(ws[ci % 2][1][:, k:k + KP, 0:width(ci)], w[ci % 2][:, k:k + KP, 0:width(ci)],
                                      ws[ci % 2][0][:, k:k + KP, 0:width(ci)], ALU.subtract).then_inc(s_lo, 1)

            rests(0)

            def key_copies(n):
                s = tsteps[n]
                ci, t = steps[s]
                kind = chunks[ci][0]
                rows, nb = ROWS[t], blocks_of[kind][1]
                dve.wait_ge(s_tr, n + 1)
                if t < NT:
                    if n >= 2:
                        dve.wait_ge(s_ks[n % 2], 32 * stores_before(n))
                    dve.tensor_copy(kt[n % 2][0][:, 0:nb, :], tp[n % 2][:, 0:nb, :]).then_inc(s_kh, 1)
                    dve.wait_ge(s_kh, sum(1 for m in tsteps[:n + 1] if steps[m][1] < NT))
                    dve.tensor_tensor(kt[n % 2][1][:, 0:nb, :], tp[n % 2][:, 0:nb, :], kt[n % 2][0][:, 0:nb, :],
                                      ALU.subtract).then_inc(s_kt, 1)
                else:
                    dst = {"k_fox": c.kf_new[:, :, :], "nsa": c.ks_new[:, :, :], "win": c.kw_new[:, :, :]}[kind]
                    dve.tensor_copy(dst, tp[n % 2][:, 0:nb, 0:rows]).then_inc(s_kt, 1)

            for s, (ci, t) in enumerate(steps):
                kind = chunks[ci][0]
                rows = ROWS[t]
                zz = z[s % 3]
                if t == 2 and ci + 1 < len(chunks):
                    rests(ci + 1)
                if kind == "win":
                    dve.wait_ge(s_z, s + 1)
                    if t == 0:
                        dve.wait_ge(s_b, 16)
                    dve.tensor_tensor(fl[0:rows, t, 0, :], zz[0:rows, 280:288], bf[0:rows, :], ALU.add)
                    dve.tensor_copy(c.gates[0:rows, t, :], zz[0:rows, 256:280]).then_inc(s_use, 1)
                if n < len(tsteps) and tsteps[n] < s:
                    key_copies(n)
                    n += 1
            while n < len(tsteps):
                key_copies(n)
                n += 1
            dve.wait_ge(s_use, uses(len(steps)))
            dve.wait_ge(s_la, 3)
            dve.tensor_scalar(fl[:, :, 0, :], fl[:, :, 0, :], 0.0, None, ALU.min).then_inc(s_lf, 1)
            dve.wait_ge(s_lf, 1)
            dve.tensor_tensor(fl[:, :, 3, :], fl[:, :, 0, :], fl[:, :, 1, :], ALU.subtract).then_inc(s_lf, 1)
            dve.wait_ge(s_la, 4)
            dve.tensor_scalar(c.gates[:, :, :], c.gates[:, :, :], 1.0, None, ALU.add).then_inc(s_lf, 1)
            dve.wait_ge(s_lf, 3)
            dve.reciprocal(c.gates[:, :, :], c.gates[:, :, :]).then_inc(s_lf, 1)
            dve.wait_ge(s_lt, 1)
            for a in range(2):
                dve.tensor_copy(lt[:, 4 * a:4 * a + 4, :], lp[a][0:H, :, :]).then_inc(s_lf, 1)
            dve.tensor_copy(c.lf_new[:, :], lp[2][0:H, 0, 0:NS]).then_inc(s_lf, 1)
            dve.wait_ge(s_lf, 7)
            dve.tensor_tensor_scan(cum[:, :], c.one[:, :].to_broadcast([H, T]), lt[:, 0:8, :].rearrange("h t n -> h (t n)"), 0.0,
                                   op0=ALU.mult, op1=ALU.add).then_inc(s_lf, 1)
            dve.wait_ge(s_lf, 8)
            dve.tensor_scalar(cum[:, :], cum[:, :], -1.0, None, ALU.mult).then_inc(s_lf, 1)

        @block.gpsimd
        def _(pool):
            def key_store(n):
                s = tsteps[n]
                ci, t = steps[s]
                kind = chunks[ci][0]
                if t >= NT:
                    return
                pool.wait_ge(s_kt, n + 1)
                for w_ in range(2):
                    if kind == "k_fox":
                        dst = d["kf_d"][w_].rearrange("(j s) d n -> (s d) j n", s=2)[:, :, t * P:(t + 1) * P]
                        pool.dma_start(dst, kt[n % 2][w_][:, :, :]).then_inc(s_ks[n % 2], 16)
                    else:
                        dst = d["ks_d" if kind == "nsa" else "kw_d"][w_].rearrange("g d n -> (g d) n")[:, t * P:(t + 1) * P]
                        pool.dma_start(dst, kt[n % 2][w_][:, 0, :]).then_inc(s_ks[n % 2], 16)

            n = 0
            for s, (ci, t) in enumerate(steps):
                kind = chunks[ci][0]
                rows = ROWS[t]
                pool.wait_ge(s_z, s + 1)
                if kind == "win" and t < NT:
                    pool.dma_start(d["vw_d"][t * P:(t + 1) * P, :], z[s % 3][:, P:2 * P]).then_inc(s_o[s % 3], 16)
                if kind != "win" or t >= NT - WIN // P:
                    width = 256 if kind == "win" else 512
                    pool.dma_start(out[kind](t, width), z[s % 3][0:rows, 0:width]).then_inc(s_o[s % 3], 16)
                if n < len(tsteps) and tsteps[n] < s:
                    key_store(n)
                    n += 1
            while n < len(tsteps):
                key_store(n)
                n += 1
            pool.wait_ge(s_lf, 2)
            pool.dma_start(d["logf_p"][0, 0].rearrange("(t p) h -> p t h", p=P), fl[:, 0:NT, 3, :]).then_inc(s_fo, 16)
            pool.dma_start(d["logf_s"][0].rearrange("b q h -> (b q) h"), fl[0:NS, NT, 3, :]).then_inc(s_fo, 16)
            pool.wait_ge(s_lf, 4)
            pool.dma_start(d["gs_d"], c.gates[0:NS, NT, :]).then_inc(s_gd, 16)
            pool.wait_ge(s_lf, 9)
            pool.dma_start(d["nc_d"], cum[:, :]).then_inc(s_fo, 16)
            for i in range(3):
                pool.wait_ge(s_o[i], 16 * stores(len(steps) + i))
            for i in range(2):
                pool.wait_ge(s_ks[i], 32 * sum(1 for m, s in enumerate(tsteps) if m % 2 == i and steps[s][1] < NT))
            pool.wait_ge(s_fo, 48)
            pool.wait_ge(s_gd, 16)


def compress_weights(c, mix):
    nc, d = c.nc, c.d
    c.w1 = mix.sb("cmp_w1_sb", [P, 2, 16, 256])
    c.w2 = mix.sb("cmp_w2_sb", [P, 2, 2, HD])
    c.b1 = mix.sb("cmp_b1_sb", [P, 2, 2])
    with Phase(nc) as ph:
        pos = ph.sb("cmp_pos_sb", [P, 2, 16])
        b1 = ph.sb("cmp_b1_raw", [P, 2, 2])
        acc = ph.ps("b1_acc", [P, 4])
        s_ld = ph.sem("cmp_weights_loaded")
        s_pe = ph.sem("pos_products")
        s_v = ph.sem("b1_summed")
        block = ph.block()

        @block.sync
        def _(sp):
            for k in range(2):
                sp.dma_start(c.w1[:, k, :, :], d["cmp_w1"][0, k].rearrange("(j p) n -> p j n", p=P)).then_inc(s_ld, 16)
                sp.dma_start(c.w2[:, k, :, :], d["cmp_w2"][0, k].rearrange("(a p) n -> p a n", p=P)).then_inc(s_ld, 16)
                sp.dma_start(pos[:, k, :], d["cmp_pos"][0, k].rearrange("(j r) e -> (r e) j", r=2)).then_inc(s_ld, 16)
                sp.dma_start(b1[:, k, :], d["cmp_b1"][0, k].rearrange("(a p) -> p a", p=P)).then_inc(s_ld, 16)

        @block.tensor
        def _(pe):
            pe.wait_ge(s_ld, 16 * 8)
            for k in range(2):
                for a in range(2):
                    for j in range(16):
                        ins = pe.matmul(acc[:, 2 * k + a:2 * k + a + 1], c.w1[:, k, j, a * P:(a + 1) * P], pos[:, k, j:j + 1],
                                        start=(j == 0), stop=(j == 15))
            ins.then_inc(s_pe, 1)

        @block.vector
        def _(dve):
            dve.wait_ge(s_ld, 16 * 8)
            dve.wait_ge(s_pe, 1)
            dve.tensor_tensor(c.b1[:, :, :].rearrange("p k a -> p (k a)"), acc[:, :], b1[:, :, :].rearrange("p k a -> p (k a)"),
                              ALU.add).then_inc(s_v, 1)


def misc(c, name, rows, a=None, b=None):
    lo, hi = MISC[name]
    return c.misc[0:rows, lo if a is None else lo + a:hi if b is None else lo + b]


def compress_products(pe, c, xt, hid):
    for k in range(2):
        for a in range(2):
            for j in range(16):
                rhs = xt[:, 2 * k:2 * k + 2, j:j + 8 * (NC - 1) + 1:8]
                ins = pe.matmul(hid[:, (2 * k + a) * 2 * NC:(2 * k + a + 1) * 2 * NC].rearrange("p (g n) -> p g n", g=2),
                                c.w1[:, k, j, a * P:(a + 1) * P], rhs, start=(j == 0), stop=(j == 15))
    return ins


def compress_outputs(pe, c, hs, kc_ps, vc_ps):
    for g in range(G):
        for a in range(2):
            pe.matmul(kc_ps[g * HD:(g + 1) * HD, 0:NC], c.w2[:, 0, a, :], hs[:, a, g * NC:(g + 1) * NC],
                      start=(a == 0), stop=(a == 1))
    for g in range(G):
        for a in range(2):
            ins = pe.matmul(vc_ps[0:NC, g * HD:(g + 1) * HD], hs[:, 2 + a, g * NC:(g + 1) * NC], c.w2[:, 1, a, :],
                            start=(a == 0), stop=(a == 1))
    return ins


def sample_attention(c):
    nc, d = c.nc, c.d
    with Phase(nc) as ph:
        kv = [ph.sb(f"fox_pages{i}", [P, PAGES, 2 * H * HD]) for i in range(2)]
        lf = [ph.sb(f"logf_pages{i}", [P, PAGES, H]) for i in range(2)]
        nc_ = [ph.sb(f"cmp_pages{i}", [P, PAGES // 2, 4, 2, HD]) for i in range(2)]
        ns = [ph.sb(f"sel_pages{i}", [P, PAGES // 2, 2, 256]) for i in range(2)]
        wn = [ph.sb(f"window{i}", [P, 4, 256]) for i in range(2)]
        vfn = [ph.sb(f"vf_new{i}", [NQ, H * HD]) for i in range(2)]
        vsn = [ph.sb(f"vs_new{i}", [NQ, 2, G * HD]) for i in range(2)]
        qbd = ph.sb("q_fox_blocks", [P, NB, 4, HQ])
        qnd = ph.sb("q_nsa_blocks", [P, NB, HQ])
        qb = ph.sb("q_fox_now", [P, 4, HQ])
        qn = ph.sb("q_nsa_now", [P, HQ])
        gt = ph.sb("gates_hq", [HQ, NB, 3])
        kT = ph.sb("k_fox_T", [P, 4, T])
        ksT = ph.sb("k_sel_T", [P, T])
        kwT = ph.sb("k_win_T", [P, WIN])
        xt = ph.sb("cmp_rows_T", [P, 4, 512])
        hs = ph.sb("cmp_hidden", [P, 4, 2 * NC])
        kcT = ph.sb("kc_T", [P, NC])
        vc = ph.sb("vc", [NC, G * HD])
        cum = ph.sb("cum_s", [H, T + NQ])
        pr = ph.sb("probs", [HQ, T + NQ])
        pc = ph.sb("probs_cmp", [HQ, NC])
        sc = ph.sb("scores_cmp", [HQ, NC])
        pT = ph.sb("probs_T", [P, PAGES * HQ])
        pTn = ph.sb("probs_T_new", [NQ, HQ])
        pcT = ph.sb("probs_cmp_T", [NC, HQ])
        blk = ph.sb("blk", [HQ, NSEL])
        sel = ph.sb("sel", [HQ, 4, 14])
        pen = ph.sb("penalty", [HQ, 16])
        ofo = ph.sb("o_fox_s", [HQ, HD])
        on = ph.sb("o_nsa_wide", [HQ, G * HD])
        ono = ph.sb("o_nsa_s", [HQ, HD])
        sm = ph.sb("small", [HQ, 20])
        tr = [ph.ps(f"tr{i}", [P, 512]) for i in range(2)]
        S = ph.ps("s_ps", [P, 3 * 512])
        PT = ph.ps("pt_ps", [P, 512])
        O = ph.ps("o_ps", [P, 512])
        M = ph.ps("m_ps", [P, 512])
        s_init = ph.sem("queries_spread")
        s_initd = ph.sem("small_rows_loaded")
        s_kv = [ph.sem(f"fox_pages_loaded{i}") for i in range(2)]
        s_ns = [ph.sem(f"nsa_pages_loaded{i}") for i in range(2)]
        s_wn = [ph.sem(f"window_loaded{i}") for i in range(2)]
        s_tr = ph.sem("group_transposed")
        s_tc = ph.sem("group_copied")
        s_dve = ph.sem("dve_chain")
        s_fs = ph.sem("o_fox_stored")
        s_nst = ph.sem("o_nsa_stored")
        s_ff = ph.sem("o_fox_free")
        s_nf = ph.sem("o_nsa_free")
        once = {n: ph.sem(n) for n in (
            "q_staged", "lf_transposed", "cum_ready", "f_scores", "f_max", "f_probs", "f_probs_turned", "f_pT", "f_values",
            "f_read", "f_out", "hidden", "gelu", "kc_products", "kc_copied", "c_scores", "c_read", "c_max", "c_exp", "c_probs",
            "c_probs_turned", "c_pT", "c_values", "slc_heads", "slc_copied", "slc_sums", "s_scores", "s_max", "s_probs",
            "s_probs_turned", "s_pT", "s_values", "w_scores", "w_max", "w_probs", "w_probs_turned", "w_pT", "w_values",
            "n_read", "n_out")}
        block = ph.block()
        os_v = d["os_d"].rearrange("(b q) (w h e) -> b w h q e", q=NQ, w=2, h=H)

        def waits(eng, b):
            return (lambda n: eng.wait_ge(once[n], b + 3)), (lambda n: eng.wait_ge(once[n], b + 2))

        def start(eng, names):
            for n in names.split():
                eng.sem_inc(once[n], 2)

        @block.sync
        def _(sp):
            for br in range(3):
                for h in range(H):
                    sp.dma_start(gt[h * NQ:(h + 1) * NQ, :, br:br + 1],
                                 d["gs_d"].rearrange("(b q) n -> q b n", q=NQ)[:, :, br * H + h:br * H + h + 1]).then_inc(s_initd, 16)
            with sp.Fori(0, NB // 2) as i:
                for u in range(2):
                    b = 2 * i + u
                    sp.wait_ge(once["w_values"], b + 1)
                    settled(sp, c)
                    for p in range(PAGES):
                        v = sp.value_load(c.pt[0:1, ds(i * (2 * PAGES) + (u * PAGES + p), 1)], min_val=0,
                                          max_val=d["cache_fox_kv"].shape[1] - 1)
                        sp.dma_start(kv[u][:, p, :], d["cache_fox_kv"][0, ds(v, 1)].rearrange("a n w h e -> n (a w h e)")).then_inc(s_kv[u], 16)
                        sp.dma_start(lf[u][:, p, :], d["cache_fox_logf"][0, ds(v, 1)].rearrange("a n h -> n (a h)")).then_inc(s_kv[u], 16)
                        half = slice((p % 2) * 64, (p % 2) * 64 + 64)
                        rows = d["cache_nsa_kv"][0, ds(v, 1)].rearrange("a (n r) w g e -> (a n) r (w g e)", r=2)
                        for r in range(2):
                            sp.dma_start(nc_[u][half, p // 2, :, r, :], rows[:, r, 0:256].rearrange("n (w e) -> n w e", e=HD)).then_inc(s_ns[u], 16)
                        sp.dma_start(ns[u][half, p // 2, :, :], rows[:, :, 256:512]).then_inc(s_ns[u], 16)
                    sp.dma_start(wn[u][:, :, :], d["state_win_kv"][0, ds(b, 1)].rearrange("a (t n) w g e -> n (a t) (w g e)", n=P)).then_inc(s_wn[u], 16)
                    sp.dma_start(vfn[u][:, :], d["fox_kv_s"][0, ds(b, 1), :, 1].rearrange("a q h e -> (a q) (h e)")).then_inc(s_wn[u], 16)
                    sp.dma_start(vsn[u][:, 0, :], d["nsa_kv_s"][0, ds(b, 1), :, 3].rearrange("a q g e -> (a q) (g e)")).then_inc(s_wn[u], 16)
                    sp.dma_start(vsn[u][:, 1, :], d["win_kv_s"][0, ds(b, 1), WIN - NQ:WIN, 1].rearrange("a q g e -> (a q) (g e)")).then_inc(s_wn[u], 16)

        NG = 15

        def group_blocks(u, m):
            if m < 8:
                return [kv[u][:, m, j * P:(j + 1) * P] for j in range(4)]
            if m < 12:
                return [nc_[u][:, m - 8, j, :, :].rearrange("p r e -> p (r e)") for j in range(4)]
            if m < 14:
                return [ns[u][:, 2 * (m - 12) + j // 2, j % 2, 0:128] for j in range(4)]
            return [wn[u][:, j, 0:P] for j in range(4)]

        def group_target(m):
            if m < 8:
                return kT[:, :, m * P:(m + 1) * P]
            if m < 12:
                return xt[:, :, (m - 8) * P:(m - 7) * P]
            if m < 14:
                return ksT[:, (m - 12) * 512:(m - 11) * 512].rearrange("p (j m) -> p j m", j=4)
            return kwT[:, :].rearrange("p (j m) -> p j m", j=4)

        @block.tensor
        def _(pe):
            start(pe, "lf_transposed f_scores f_probs_turned f_values hidden kc_products c_scores c_probs_turned c_values "
                      "slc_heads slc_sums s_scores s_probs_turned s_values w_scores w_probs_turned w_values")
            pe.sem_inc(s_tc, 2)
            pe.wait_ge(s_init, 18)
            with pe.Fori(0, NB // 2) as i:
                for u in range(2):
                    b = 2 * i + u
                    now, prev = waits(pe, b)

                    def group(m):
                        pe.wait_ge(s_tc, b * NG + m + 1)
                        for j, src in enumerate(group_blocks(u, m)):
                            ins = pe.transpose(tr[(u + m) % 2][:, j * P:(j + 1) * P], src, c.ident[:, :])
                        ins.then_inc(s_tr, 1)

                    def copied(m):
                        pe.wait_ge(s_tc, b * NG + m + 3)

                    def turn(src, tiles, name):
                        settled(pe, c)
                        for p in range(tiles):
                            pe.transpose(PT[:, p * HQ:(p + 1) * HQ], pr[:, p * P:(p + 1) * P], c.ident[0:HQ, 0:HQ])
                        pe.transpose(PT[0:NQ, 256:256 + HQ], pr[:, tiles * P:tiles * P + NQ],
                                     c.ident[0:HQ, 0:HQ]).then_inc(once[name], 1)

                    pe.wait_ge(s_kv[u], i * (2 * PAGES * 16) + 2 * PAGES * 16)
                    prev("w_probs")
                    for p in range(PAGES):
                        ins = pe.transpose(S[0:H, p * P:(p + 1) * P], lf[u][:, p, :], c.ident[:, :])
                    ins.then_inc(once["lf_transposed"], 1)
                    for m in range(8):
                        group(m)
                    pe.wait_ge(s_ns[u], i * (3 * PAGES * 16) + 3 * PAGES * 16)
                    pe.wait_ge(s_wn[u], i * 64 + 64)
                    for m in range(8, 12):
                        group(m)
                    now("q_staged")
                    now("cum_ready")
                    copied(7)
                    for n in range(2):
                        cols = slice(n * 512, (n + 1) * 512)
                        for j in range(4):
                            pe.matmul(S[0:HQ, cols], qb[:, j, :], kT[:, j, cols], start=(j == 0), stop=False)
                        pe.matmul(S[0:HQ, cols], misc(c, "neg_head", H), cum[:, cols], start=False, stop=True)
                    for j in range(4):
                        pe.matmul(S[0:HQ, T:T + NQ], qb[:, j, :], c.kf_new[:, j, ds(b * NQ, NQ)], start=(j == 0), stop=False)
                    pe.matmul(S[0:HQ, T:T + NQ], misc(c, "neg_head", H), cum[:, T:T + NQ],
                              start=False, stop=True).then_inc(once["f_scores"], 1)
                    copied(11)
                    prev("n_read")
                    compress_products(pe, c, xt, M).then_inc(once["hidden"], 1)
                    for m in range(12, 15):
                        group(m)
                    now("f_probs")
                    prev("w_pT")
                    turn(pr, PAGES, "f_probs_turned")
                    now("gelu")
                    prev("f_read")
                    compress_outputs(pe, c, hs, O[:, 0:P], O[:, P:2 * P]).then_inc(once["kc_products"], 1)
                    now("kc_copied")
                    pe.matmul(O[0:HQ, 256:256 + NC], qn[:, :], kcT[:, :], start=True, stop=True).then_inc(once["c_scores"], 1)
                    now("f_pT")
                    now("c_read")
                    for p in range(PAGES):
                        pe.matmul(O[0:HQ, :], pT[:, p * HQ:(p + 1) * HQ], kv[u][:, p, 512:1024], start=(p == 0), stop=False)
                    pe.matmul(O[0:HQ, :], pTn[:, :], vfn[u][:, :], start=False, stop=True).then_inc(once["f_values"], 1)
                    now("c_probs")
                    settled(pe, c)
                    pe.transpose(PT[0:NC, 0:HQ], pc[:, :], c.ident[0:HQ, 0:HQ]).then_inc(once["c_probs_turned"], 1)
                    copied(13)
                    for n in range(2):
                        cols = slice(n * 512, (n + 1) * 512)
                        pe.matmul(S[0:HQ, cols], qn[:, :], ksT[:, cols], start=True, stop=True)
                    pe.matmul(S[0:HQ, T:T + NQ], qn[:, :], c.ks_new[:, 0, ds(b * NQ, NQ)],
                              start=True, stop=True).then_inc(once["s_scores"], 1)
                    now("c_pT")
                    settled(pe, c)
                    pe.matmul(PT[0:HQ, 0:NSEL], pcT[:, :], misc(c, "to_sel", NC), start=True, stop=True).then_inc(once["slc_heads"], 1)
                    pe.matmul(M[0:HQ, 0:G * HD], pcT[:, :], vc[:, :], start=True, stop=True).then_inc(once["c_values"], 1)
                    now("slc_copied")
                    settled(pe, c)
                    pe.matmul(PT[0:HQ, 0:NSEL], misc(c, "group_sum", HQ), blk[:, :], start=True, stop=True).then_inc(once["slc_sums"], 1)
                    now("s_probs")
                    turn(pr, PAGES, "s_probs_turned")
                    copied(14)
                    pe.matmul(S[0:HQ, 0:WIN], qn[:, :], kwT[:, :], start=True, stop=True)
                    pe.matmul(S[0:HQ, WIN:WIN + NQ], qn[:, :], c.kw_new[:, 0, ds(b * NQ, NQ)],
                              start=True, stop=True).then_inc(once["w_scores"], 1)
                    now("s_pT")
                    for p in range(PAGES):
                        pe.matmul(M[0:HQ, 128:256], pT[:, p * HQ:(p + 1) * HQ], ns[u][:, p // 2, p % 2, 128:256],
                                  start=(p == 0), stop=False)
                    pe.matmul(M[0:HQ, 128:256], pTn[:, :], vsn[u][:, 0, :], start=False, stop=True).then_inc(once["s_values"], 1)
                    now("w_probs")
                    turn(pr, WIN // P, "w_probs_turned")
                    now("w_pT")
                    for p in range(WIN // P):
                        pe.matmul(M[0:HQ, 256:384], pT[:, p * HQ:(p + 1) * HQ], wn[u][:, p, P:2 * P], start=(p == 0), stop=False)
                    pe.matmul(M[0:HQ, 256:384], pTn[:, :], vsn[u][:, 1, :], start=False, stop=True).then_inc(once["w_values"], 1)

        @block.scalar
        def _(act):
            start(act, "f_probs gelu f_pT c_exp s_probs s_pT w_probs w_pT")
            with act.Fori(0, NB // 2) as i:
                for u in range(2):
                    b = 2 * i + u
                    now, prev = waits(act, b)

                    def probs(name, out, src, col):
                        now(f"{name}_max")
                        act.activation(out, src, ACT.Exp, bias=sm[:, col:col + 1], accum_out=sm[:, col + 1:col + 2])\
                           .then_inc(once[{"c": "c_exp"}.get(name, f"{name}_probs")], 1)

                    def turned(name, before):
                        now(f"{name}_probs_turned")
                        before()
                        n = (WIN // P if name == "w" else PAGES) * HQ
                        act.activation(pT[:, 0:n], PT[:, 0:n], ACT.Copy)
                        act.activation(pTn[:, :], PT[0:NQ, 256:256 + HQ], ACT.Copy).then_inc(once[f"{name}_pT"], 1)

                    prev("w_probs_turned")
                    probs("f", pr[:, :], S[0:HQ, 0:T + NQ], 0)
                    now("hidden")
                    prev("kc_products")
                    for k in range(4):
                        ins = act.activation(hs[:, k, :], M[:, k * 2 * NC:(k + 1) * 2 * NC], ACT.Gelu_apprx_tanh,
                                             bias=c.b1[:, k // 2, k % 2:k % 2 + 1])
                    ins.then_inc(once["gelu"], 1)
                    turned("f", lambda: prev("w_values"))
                    probs("c", pc[:, :], sc[:, :], 3)
                    probs("s", pr[:, :], S[0:HQ, 0:T + NQ], 6)
                    turned("s", lambda: now("f_values"))
                    probs("w", pr[:, 0:WIN + NQ], S[0:HQ, 0:WIN + NQ], 9)
                    turned("w", lambda: now("s_values"))

        @block.vector
        def _(dve):
            start(dve, "q_staged cum_ready f_max f_read f_out kc_copied c_read c_max c_probs c_pT slc_copied s_max w_max "
                       "n_read n_out")
            dve.memset(qbd[:, :, :, :], 0.0).then_inc(s_init, 1)
            dve.memset(qnd[:, :, :], 0.0).then_inc(s_init, 1)
            dve.wait_ge(s_init, 2)
            for h in range(H):
                j, s, g = h // 2, h % 2, h // GH
                q_of = lambda k: c.q_smp[s * HD:(s + 1) * HD, k, j, :].rearrange("p (b q) -> p b q", q=NQ)
                dve.tensor_copy(qbd[s * HD:(s + 1) * HD, :, j, h * NQ:(h + 1) * NQ], q_of(0)).then_inc(s_init, 1)
                dve.tensor_copy(qnd[g * HD:(g + 1) * HD, :, h * NQ:(h + 1) * NQ], q_of(1)).then_inc(s_init, 1)
            dve.wait_ge(s_init, 18)
            chain = Chain(dve, s_dve)
            chain(dve.memset(pen[:, :], 0.0))
            chain.done, chain.k = 1, 0
            dve.wait_ge(s_initd, 16 * 24)
            with dve.Fori(0, NB // 2) as i:
                chain.enter(i, 2 * PER_SEQ)
                for u in range(2):
                    b = 2 * i + u
                    now, prev = waits(dve, b)
                    k0 = chain.k

                    def copy_group(m):
                        dve.wait_ge(s_tr, b * NG + m + 1)
                        dve.tensor_copy(group_target(m), tr[(u + m) % 2][:, :].rearrange("p (j m) -> p j m", j=4)).then_inc(s_tc, 1)

                    prev("f_scores")
                    dve.tensor_copy(qb[:, :, :], qbd[:, ds(b, 1), :, :].rearrange("p a j n -> p (a j) n"))
                    prev("w_scores")
                    dve.tensor_copy(qn[:, :], qnd[:, ds(b, 1), :].rearrange("p a n -> p (a n)")).then_inc(once["q_staged"], 1)
                    now("lf_transposed")
                    chain(dve.tensor_tensor_scan(cum[:, 0:T], c.one[:, :].to_broadcast([H, T]), S[0:H, 0:T], 0.0, op0=ALU.mult, op1=ALU.add))
                    dve.tensor_tensor_scan(cum[:, T:T + NQ], c.one[:, :].to_broadcast([H, NQ]), c.lf_new[:, ds(b * NQ, NQ)],
                                           cum[:, T - 1:T], op0=ALU.mult, op1=ALU.add).then_inc(once["cum_ready"], 1)
                    for m in range(8):
                        copy_group(m)
                    prev("hidden")
                    for m in range(8, 12):
                        copy_group(m)
                    now("f_scores")
                    chain(dve.tensor_tensor(S[0:HQ, T:T + NQ], S[0:HQ, T:T + NQ], misc(c, "causal_new", HQ), ALU.add))
                    dve.tensor_reduce(sm[:, 0:1], S[0:HQ, 0:T + NQ], AX, ALU.max, negate=True).then_inc(once["f_max"], 1)
                    prev("s_scores")
                    for m in range(12, 15):
                        copy_group(m)
                    now("kc_products")
                    dve.tensor_copy(kcT[:, :], O[:, 0:NC])
                    prev("c_values")
                    dve.tensor_copy(vc[:, :], O[0:NC, P:2 * P]).then_inc(once["kc_copied"], 1)
                    now("c_scores")
                    dve.tensor_tensor(sc[:, :], O[0:HQ, 256:256 + NC], c.bias_s[:, 388:451], ALU.add).then_inc(once["c_read"], 1)
                    now("c_read")
                    dve.tensor_reduce(sm[:, 3:4], sc[:, :], AX, ALU.max, negate=True).then_inc(once["c_max"], 1)
                    now("c_exp")
                    chain(dve.reciprocal(sm[:, 5:6], sm[:, 4:5]))
                    dve.tensor_scalar(pc[:, :], pc[:, :], sm[:, 5:6], None, ALU.mult).then_inc(once["c_probs"], 1)
                    now("c_probs_turned")
                    prev("c_values")
                    dve.tensor_copy(pcT[:, :], PT[0:NC, 0:HQ]).then_inc(once["c_pT"], 1)
                    now("slc_heads")
                    dve.tensor_copy(blk[:, :], PT[0:HQ, 0:NSEL]).then_inc(once["slc_copied"], 1)
                    now("slc_sums")
                    chain(dve.tensor_copy(sel[:, 0, :], PT[0:HQ, 1:15]))
                    chain(dve.tensor_reduce(sm[:, 12:13], sel[:, 0, :], AX, ALU.min))
                    chain(dve.tensor_scalar(sel[:, 1, :], sel[:, 0, :], sm[:, 12:13], None, ALU.is_equal))
                    chain(dve.tensor_tensor(sel[:, 2, :], sel[:, 1, :], misc(c, "block_no", HQ), ALU.mult))
                    chain(dve.tensor_reduce(sm[:, 13:14], sel[:, 2, :], AX, ALU.max))
                    chain(dve.tensor_scalar(pen[:, 1:15], sel[:, 2, :], sm[:, 13:14], NEG, ALU.is_equal, ALU.mult))
                    now("s_scores")
                    chain(dve.tensor_tensor(S[0:HQ, 768:T], S[0:HQ, 768:T], c.bias_s[:, 0:256], ALU.add))
                    dve.tensor_tensor(S[0:HQ, T:T + NQ], S[0:HQ, T:T + NQ], c.bias_s[:, 256:260], ALU.add)
                    for r in range(2):
                        part = S[0:HQ, 0:T].rearrange("p (a r b m) -> p a r b m", a=4, r=2, b=4)[:, :, r, :, :]
                        drop = pen[:, :].rearrange("p (a b c) -> p a b c", a=4, c=1).to_broadcast([HQ, 4, 4, 32])
                        chain(dve.tensor_tensor(part, part, drop, ALU.add))
                    dve.tensor_reduce(sm[:, 6:7], S[0:HQ, 0:T + NQ], AX, ALU.max, negate=True).then_inc(once["s_max"], 1)
                    now("f_values")
                    chain(dve.tensor_tensor(O[0:HQ, :], O[0:HQ, :], misc(c, "own_head", HQ), ALU.mult))
                    dve.wait_ge(s_ff, b + 1)
                    dve.tensor_reduce(ofo[:, :], O[0:HQ, :].rearrange("p (h e) -> p e h", h=H), AX, ALU.add).then_inc(once["f_read"], 1)
                    now("f_read")
                    chain(dve.reciprocal(sm[:, 2:3], sm[:, 1:2]))
                    dve.tensor_scalar(ofo[:, :], ofo[:, :], sm[:, 2:3], None, ALU.mult).then_inc(once["f_out"], 1)
                    now("w_scores")
                    chain(dve.tensor_tensor(S[0:HQ, 0:P], S[0:HQ, 0:P], misc(c, "wmask_s", HQ), ALU.add))
                    chain(dve.tensor_tensor(S[0:HQ, WIN - P:WIN], S[0:HQ, WIN - P:WIN], c.bias_s[:, 260:388], ALU.add))
                    chain(dve.tensor_tensor(S[0:HQ, WIN:WIN + NQ], S[0:HQ, WIN:WIN + NQ], c.bias_s[:, 256:260], ALU.add))
                    dve.tensor_reduce(sm[:, 9:10], S[0:HQ, 0:WIN + NQ], AX, ALU.max, negate=True).then_inc(once["w_max"], 1)
                    now("w_probs")
                    chain(dve.reciprocal(sm[:, 14:15], sm[:, 7:8]))
                    chain(dve.reciprocal(sm[:, 15:16], sm[:, 10:11]))
                    gate = gt[:, ds(b, 1), :].rearrange("p a n -> p (a n)")
                    chain(dve.tensor_tensor(sm[:, 14:16], sm[:, 14:16], gate[:, 1:3], ALU.mult))
                    chain(dve.tensor_copy(sm[:, 16:17], gate[:, 0:1]))
                    now("w_values")
                    chain(dve.tensor_scalar(on[:, :], M[0:HQ, 0:P], sm[:, 16:17], None, ALU.mult))
                    chain(dve.scalar_tensor_tensor(out=on[:, :], in0=M[0:HQ, P:2 * P], scalar=sm[:, 14:15], in1=on[:, :],
                                                   op0=ALU.mult, op1=ALU.add))
                    dve.scalar_tensor_tensor(out=on[:, :], in0=M[0:HQ, 2 * P:3 * P], scalar=sm[:, 15:16], in1=on[:, :],
                                             op0=ALU.mult, op1=ALU.add).then_inc(once["n_read"], 1)
                    now("n_read")
                    dve.wait_ge(s_nf, b + 1)
                    chain(dve.tensor_scalar(ono[:, :], on[:, 0:HD], misc(c, "own_group", HQ, 0, 1), None, ALU.mult))
                    dve.scalar_tensor_tensor(out=ono[:, :], in0=on[:, HD:2 * HD], scalar=misc(c, "own_group", HQ, 1, 2),
                                             in1=ono[:, :], op0=ALU.mult, op1=ALU.add).then_inc(once["n_out"], 1)
                    assert chain.k - k0 == PER_SEQ, chain.k - k0
            chain.leave(NB // 2)

        @block.gpsimd
        def _(pool):
            pool.sem_inc(s_ff, 1)
            pool.sem_inc(s_nf, 1)
            with pool.Fori(0, NB) as b:
                for name, tile, w, sem, free in (("f_out", ofo, 0, s_fs, s_ff), ("n_out", ono, 1, s_nst, s_nf)):
                    pool.wait_ge(once[name], b + 3)
                    settled(pool, c)
                    pool.dma_start(os_v[ds(b, 1), w].rearrange("a h q e -> (a h) q e"), tile[:, :]).then_inc(sem, 16)
                    pool.wait_ge(sem, 16 * b + 16)
                    pool.sem_inc(free, 1)


PER_SEQ = 24


def prompt_compress(c):
    nc, d = c.nc, c.d
    with Phase(nc) as ph:
        rows = ph.sb("pc_rows", [P, 4, 4, 2, HD])
        xt = ph.sb("pc_rows_T", [P, 4, 512])
        hs = ph.sb("pc_hidden", [P, 4, 2 * NC])
        tr = [ph.ps(f"pc_tr{i}", [P, 512]) for i in range(4)]
        M = ph.ps("pc_hid_ps", [P, 512])
        O = ph.ps("pc_out_ps", [P, 512])
        s_ld = ph.sem("pc_rows_loaded")
        s_tr = ph.sem("pc_transposed")
        s_cp = ph.sem("pc_copied")
        s_h = ph.sem("pc_hidden_done")
        s_g = ph.sem("pc_gelu")
        s_o = ph.sem("pc_products")
        s_k = ph.sem("pc_kept")
        block = ph.block()

        @block.sync
        def _(sp):
            src = d["nsa_kv_p"][0, 0].rearrange("(a n r) w g e -> n a r (w g e)", a=4, r=2)
            for a in range(4):
                for r in range(2):
                    sp.dma_start(rows[:, a, :, r, :], src[:, a, r, 0:256].rearrange("n (w e) -> n w e", e=HD)).then_inc(s_ld, 16)

        @block.tensor
        def _(pe):
            pe.wait_ge(s_ld, 16 * 8)
            for a in range(4):
                for j in range(4):
                    ins = pe.transpose(tr[a][:, j * P:(j + 1) * P], rows[:, a, j, :, :].rearrange("p r e -> p (r e)"), c.ident[:, :])
                ins.then_inc(s_tr, 1)
            pe.wait_ge(s_cp, 4)
            compress_products(pe, c, xt, M).then_inc(s_h, 1)
            pe.wait_ge(s_g, 1)
            compress_outputs(pe, c, hs, O[:, 0:P], O[:, P:2 * P]).then_inc(s_o, 1)

        @block.scalar
        def _(act):
            act.wait_ge(s_h, 1)
            for k in range(4):
                ins = act.activation(hs[:, k, :], M[:, k * 2 * NC:(k + 1) * 2 * NC], ACT.Gelu_apprx_tanh,
                                     bias=c.b1[:, k // 2, k % 2:k % 2 + 1])
            ins.then_inc(s_g, 1)

        @block.vector
        def _(dve):
            for a in range(4):
                dve.wait_ge(s_tr, a + 1)
                dve.tensor_copy(xt[:, :, a * P:(a + 1) * P], tr[a][:, :].rearrange("p (j m) -> p j m", j=4)).then_inc(s_cp, 1)
            dve.wait_ge(s_o, 1)
            dve.tensor_copy(c.kc_p[:, :], O[:, 0:NC]).then_inc(s_k, 1)
            dve.tensor_copy(c.vc_p[:, :], O[0:NC, P:2 * P]).then_inc(s_k, 1)


class AttentionInputs:

    def __init__(self, c, ph):
        kinds = ("fox", "sel", "win")
        self.q = {kind: [ph.sb(f"pa_q_{kind}{u}", [P, T], FR) for u in range(2)] for kind in ("fox", "nsa")}
        self.k = {kind: [[ph.sb(f"pa_k_{kind}{u}{w_}", [P, T], FR) for w_ in range(2)] for u in range(2)] for kind in kinds}
        self.v = {kind: [ph.sb(f"pa_v_{kind}{u}", [P, NT + 1, 2, HD], FR) for u in range(2)] for kind in kinds}
        self.v_raw = [ph.sb(f"pa_v_raw{u}", [P, NT, HD]) for u in range(2)]
        self.g_raw = [ph.sb(f"pa_group_v_raw{n}", [P, NT, HD]) for n in range(2)]
        self.s_fl = [ph.sem(f"pa_fox_loaded{u}") for u in range(2)]
        self.s_nl = [ph.sem(f"pa_nsa_q_loaded{u}") for u in range(2)]
        self.s_kl = [ph.sem(f"pa_group_k_loaded{u}") for u in range(2)]
        self.s_fv = [ph.sem(f"pa_fox_v_loaded{u}") for u in range(2)]
        self.s_gv = [ph.sem(f"pa_group_v_loaded{n}") for n in range(4)]
        self.s_vh = ph.sem("pa_v_rounded")
        self.s_vs = [ph.sem(f"pa_fox_v_split{u}") for u in range(2)]
        self.s_gs = ph.sem("pa_group_v_split")
        self.s_vz = ph.sem("pa_v_tails")

    def load_fox(self, pool, d, h, u):
        for w_ in range(2):
            pool.dma_start(self.q["fox"][u][w_ * HD:(w_ + 1) * HD, :], d["qfs_d"][w_, ds(h, 1)].rearrange("a e n -> (a e) n")).then_inc(self.s_fl[u], 16)
            for r in range(2):
                pool.dma_start(self.k["fox"][u][w_][r * HD:(r + 1) * HD, :], d["kf_d"][w_, ds(h, 1)].rearrange("a e n -> (a e) n")).then_inc(self.s_fl[u], 16)

    def load_nsa(self, pool, d, h, u):
        for w_ in range(2):
            pool.dma_start(self.q["nsa"][u][w_ * HD:(w_ + 1) * HD, :], d["qns_d"][w_, ds(h, 1)].rearrange("a e n -> (a e) n")).then_inc(self.s_nl[u], 16)

    def load_fox_values(self, sp, d, h, u):
        sp.dma_start(self.v_raw[u][:, :, :], d["fox_kv_p"][0, 0, :, 1, ds(h, 1), :].rearrange("(t p) a e -> p t (a e)", p=P)).then_inc(self.s_fv[u], 16)

    def split_values(self, pool, dst, raw, sem, at):
        pool.tensor_copy(dst[:, 0:NT, 0, :], raw[:, :, :]).then_inc(self.s_vh, 1)
        pool.wait_ge(self.s_vh, at)
        pool.tensor_tensor(dst[:, 0:NT, 1, :], raw[:, :, :], dst[:, 0:NT, 0, :], ALU.subtract).then_inc(sem, 1)


def compressed_attention(c, pa):
    nc, d = c.nc, c.d
    with Phase(nc) as ph:
        q = [ph.sb(f"ca_q{i}", [P, GH, P]) for i in range(2)]
        sc = [ph.sb(f"ca_scores{i}", [P, H, NC]) for i in range(2)]
        pT = [ph.sb(f"ca_probs_T{i}", [NC, H, P]) for i in range(2)]
        mx = ph.sb("ca_max", [P, 2, H])
        co = ph.sb("ca_coef", [P, 2, H])
        S = [ph.ps(f"ca_s{i}", [P, G, 512]) for i in range(2)]
        T_ = ph.ps("ca_t", [P, H, P])
        O = [ph.ps(f"ca_o{i}", [P, H, HD]) for i in range(2)]
        s_q = [ph.sem(f"ca_q_loaded{i}") for i in range(2)]
        s_s = ph.sem("ca_scored")
        s_sh = ph.sem("ca_shifted")
        s_e = ph.sem("ca_exps")
        s_t = ph.sem("ca_turned")
        s_c = ph.sem("ca_turned_copied")
        s_o = ph.sem("ca_values")
        s_co = ph.sem("ca_coef_done")
        s_n = ph.sem("ca_out")
        s_ch = ph.sem("ca_chain")
        block = ph.block()
        group = [(kind, u) for u in range(2) for kind in ("sel", "win")]

        @block.gpsimd
        def _(pool):
            for kind in ("fox", "sel", "win"):
                for u in range(2):
                    pool.tensor_copy(pa.v[kind][u][:, NT, :, :].rearrange("p w e -> p (w e)"),
                                     c.zero[:, :].to_broadcast([P, P])).then_inc(pa.s_vz, 1)
            for u in range(2):
                pa.load_fox(pool, d, GH * u, u)
                pa.load_nsa(pool, d, GH * u, u)
                for kind, src in (("sel", "ks_d"), ("win", "kw_d")):
                    for w_ in range(2):
                        for r in range(2):
                            pool.dma_start(pa.k[kind][u][w_][r * HD:(r + 1) * HD, :], d[src][w_, u]).then_inc(pa.s_kl[u], 16)
            for u in range(2):
                pool.wait_ge(pa.s_fv[u], 16)
                pa.split_values(pool, pa.v["fox"][u], pa.v_raw[u], pa.s_vs[u], u + 1)
            for n, (kind, u) in enumerate(group):
                pool.wait_ge(pa.s_gv[n], 16)
                pa.split_values(pool, pa.v[kind][u], pa.g_raw[n % 2], pa.s_gs, n + 3)

        @block.sync
        def _(sp):
            sp.sem_inc(s_s, 2)
            with sp.Fori(0, NT // 2) as i:
                for u in range(2):
                    t = 2 * i + u
                    sp.wait_ge(s_s, t + 1)
                    for g in range(G):
                        sp.dma_start(q[u][g * HD:(g + 1) * HD, :, :],
                                     d["qn_d"][g * GH:(g + 1) * GH, :, ds(t * P, P)].rearrange("h e n -> e h n")).then_inc(s_q[u], 16)
            for u in range(2):
                pa.load_fox_values(sp, d, GH * u, u)
            for n, (kind, u) in enumerate(group):
                if n >= 2:
                    sp.wait_ge(pa.s_gs, n - 1)
                src = d["nsa_kv_p"][0, 0, :, 3, u, :] if kind == "sel" else d["vw_d"][:, u * HD:(u + 1) * HD]
                sp.dma_start(pa.g_raw[n % 2][:, :, :], src.rearrange("(t p) e -> p t e", p=P)).then_inc(pa.s_gv[n], 16)

        @block.tensor
        def _(pe):
            pe.sem_inc(s_t, 1)
            with pe.Fori(0, NT // 2) as i:
                for u in range(2):
                    t = 2 * i + u
                    pe.wait_ge(s_q[u], 32 * i + 32)
                    pe.wait_ge(s_n, t + 1)
                    for h in range(H):
                        rows = slice(h // GH * HD, (h // GH + 1) * HD)
                        ins = pe.matmul(S[u][:, h // GH, h % GH * NC:(h % GH + 1) * NC], q[u][rows, h % GH, :], c.kc_p[rows, :], start=True, stop=True)
                    ins.then_inc(s_s, 1)
                    pe.wait_ge(s_e, t + 1)
                    settled(pe, c)
                    for h in range(H):
                        ins = pe.transpose(T_[0:NC, h, :], sc[u][:, h, :], c.ident[:, :])
                    ins.then_inc(s_t, 1)
                    pe.wait_ge(s_c, t + 1)
                    for h in range(H):
                        g = h // GH
                        ins = pe.matmul(O[u][:, h, :], pT[u][:, h, :], c.vc_p[:, g * HD:(g + 1) * HD], start=True, stop=True)
                    ins.then_inc(s_o, 1)

        @block.scalar
        def _(act):
            with act.Fori(0, NT // 2) as i:
                for u in range(2):
                    t = 2 * i + u
                    act.wait_ge(s_sh, t + 1)
                    act.activation(sc[u][:, :, :], sc[u][:, :, :], ACT.Exp).then_inc(s_e, 1)
                    act.wait_ge(s_t, t + 2)
                    act.activation(pT[u][:, :, :], T_[0:NC, :, :], ACT.Copy).then_inc(s_c, 1)

        @block.vector
        def _(dve):
            chain = Chain(dve, s_ch)
            dve.sem_inc(s_n, 1)
            with dve.Fori(0, NT // 2) as i:
                chain.enter(i, 2 * 5)
                for u in range(2):
                    t = 2 * i + u
                    dve.wait_ge(s_s, t + 3)
                    dve.wait_ge(s_t, t + 1)
                    grouped = lambda x: x.rearrange("p (g h) n -> p g h n", g=G)
                    chain(dve.tensor_tensor(grouped(sc[u][:, :, :]), S[u][:, :, 0:GH * NC].rearrange("p g (h n) -> p g h n", h=GH),
                                            grouped(c.cb[:, :, ds(56 - 8 * t, NC)]), ALU.add))
                    chain(dve.tensor_reduce(mx[:, u, :], sc[u][:, :, :], AX, ALU.max))
                    dve.tensor_tensor(sc[u][:, :, :], sc[u][:, :, :],
                                      mx[:, u, :].rearrange("p (h a) -> p h a", a=1).to_broadcast([P, H, NC]),
                                      ALU.subtract).then_inc(s_sh, 1)
                    dve.wait_ge(s_e, t + 1)
                    chain(dve.tensor_reduce(co[:, u, :], sc[u][:, :, :], AX, ALU.add))
                    chain(dve.reciprocal(co[:, u, :], co[:, u, :]))
                    chain(dve.tensor_tensor(co[:, u, :], co[:, u, :], c.gates[:, ds(t, 1), 0:H].rearrange("p a h -> p (a h)"), ALU.mult))
                    lo = MISC["seen"][0]
                    dve.tensor_tensor(co[:, u, :], co[:, u, :],
                                      c.misc[:, ds(lo + 8 * t, 8)], ALU.mult).then_inc(s_co, 1)
                    dve.wait_ge(s_co, t + 1)
                    dve.wait_ge(s_o, t + 1)
                    dve.tensor_tensor(c.o[:, ds(t, 1), D // 2:D].rearrange("p a (h e) -> p (a h) e", h=H), O[u][:, :, :],
                                      co[:, u, :].rearrange("p (h a) -> p h a", a=1).to_broadcast([P, H, HD]),
                                      ALU.mult).then_inc(s_n, 1)
            chain.leave(NT // 2)


def prompt_attention(c, pa):
    nc, d = c.nc, c.d
    kinds = ("fox", "sel", "win")
    jobs = [(u, kind) for u in range(2) for kind in kinds]
    units = [(j, t) for j in range(len(jobs)) for t in range(NT)]
    NU = len(units)

    def first_tile(s):
        j, t = units[s]
        return max(0, t - WIN // P) if jobs[j][1] == "win" else 0

    def tiles(s):
        return units[s][1] + 1 - first_tile(s)

    chunks = [(s, a, min(4, tiles(s) - a)) for s in range(NU) for a in range(0, tiles(s), 4)]
    of_unit = [[n for n, ch in enumerate(chunks) if ch[0] == s] for s in range(NU)]
    NCK = len(chunks)

    with Phase(nc) as ph:
        q, k, v = pa.q, pa.k, pa.v
        oj = [ph.sb(f"pa_job_out{i}", [P, NT, HD]) for i in range(2)]
        scaled = ph.sb("pa_job_scaled", [P, NT, HD])
        bias = {kind: [ph.sb(f"pa_bias_{kind}{i}", [P, T]) for i in range(2)] for kind in kinds}
        sc = [ph.sb(f"pa_scores{i}", [P, T]) for i in range(3)]
        pT = [split(ph, f"pa_probs_T{i}", [P, T]) for i in range(2)]
        nm = ph.sb("pa_neg_max", [P, NU])
        sm = ph.sb("pa_sums", [P, NU])
        co = ph.sb("pa_coef", [P, NU])
        S = [ph.ps(f"pa_s{i}", [P, T]) for i in range(2)]
        PT = [ph.ps(f"pa_t{i}", [P, 4 * P]) for i in range(2)]
        O = [ph.ps(f"pa_o{i}", [P, 512]) for i in range(2)]
        s_z = ph.sem("pa_zeroed")
        s_fb = [ph.sem(f"pa_fox_bias_loaded{u}") for u in range(2)]
        s_nb = [ph.sem(f"pa_nsa_bias_loaded{u}") for u in range(2)]
        s_s = ph.sem("pa_scored")
        s_m = ph.sem("pa_biased")
        s_e = ph.sem("pa_exps")
        s_t = ph.sem("pa_turned")
        s_ca = ph.sem("pa_copied_act")
        s_cd = ph.sem("pa_copied_dve")
        s_o = ph.sem("pa_values")
        s_n = ph.sem("pa_out")
        s_co = ph.sem("pa_coef_done")
        s_mg = ph.sem("pa_merged")
        s_mc = ph.sem("pa_merge_scaled")
        s_ch = ph.sem("pa_chain")
        block = ph.block()

        def fox_free(eng, i, u):
            eng.wait_ge(s_o, i * NU + (3 * u + 1) * NT + 1)
            settled(eng, c)

        def nsa_free(eng, i, u):
            eng.wait_ge(s_o, i * NU + (3 * u + 3) * NT + 1)
            settled(eng, c)

        @block.sync
        def _(sp):
            def fox_bias(h, u):
                sp.dma_start(bias["fox"][u][:, :], d["nc_d"][ds(h, 1), :].to_broadcast([P, T])).then_inc(s_fb[u], 16)

            def nsa_bias(h, u):
                for kind in ("sel", "win"):
                    sp.dma_start(bias[kind][u][:, T - 256:T], d["tb_d"][ds(h, 1)].rearrange("a p n -> (a p) n")).then_inc(s_nb[u], 16)

            for u in range(2):
                fox_bias(GH * u, u)
                nsa_bias(GH * u, u)
            with sp.Fori(0, 3) as i:
                for u in range(2):
                    h = i + GH * u + 1
                    fox_free(sp, i, u)
                    pa.load_fox_values(sp, d, h, u)
                    fox_bias(h, u)
                    nsa_free(sp, i, u)
                    nsa_bias(h, u)

        @block.gpsimd
        def _(pool):
            for u in range(2):
                pool.memset(bias["sel"][u][:, 0:T - 256], 0.0).then_inc(s_z, 1)
                pool.memset(bias["win"][u][:, 512:T - 256], 0.0)
                pool.tensor_copy(bias["win"][u][:, 384:512], misc(c, "wmask", P)).then_inc(s_z, 1)
            pool.sem_inc(s_mg, 2)
            pool.sem_inc(s_mc, 1)

            def turn(i, last):
                for j, (u, kind) in enumerate(jobs):
                    h = i + GH * u
                    pool.wait_ge(s_mg, 6 * i + j + 2)
                    pool.wait_ge(s_co, 6 * i + j + 1)
                    settled(pool, c)
                    coef = co[:, j * NT:(j + 1) * NT].rearrange("p (t a) -> p t a", a=1).to_broadcast([P, NT, HD])
                    if kind == "fox":
                        pool.tensor_tensor(c.o[:, :, ds(h * HD, HD)], oj[j % 2][:, :, :], coef, ALU.mult).then_inc(s_mg, 1)
                    else:
                        dst = c.o[:, :, ds(h * HD + D // 2, HD)]
                        pool.tensor_tensor(scaled[:, :, :], oj[j % 2][:, :, :], coef, ALU.mult).then_inc(s_mc, 1)
                        pool.wait_ge(s_mc, 4 * i + (2 * u + (kind == "win")) + 2)
                        settled(pool, c)
                        pool.tensor_tensor(dst, dst, scaled[:, :, :], ALU.add).then_inc(s_mg, 1)
                    if last:
                        continue
                    if kind == "fox":
                        fox_free(pool, i, u)
                        pa.load_fox(pool, d, h + 1, u)
                    if kind == "sel":
                        pool.wait_ge(pa.s_fv[u], 16 * i + 32)
                        settled(pool, c)
                        pa.split_values(pool, v["fox"][u], pa.v_raw[u], pa.s_vs[u], 2 * i + u + 7)
                    if kind == "win":
                        nsa_free(pool, i, u)
                        pa.load_nsa(pool, d, h + 1, u)

            with pool.Fori(0, 3) as i:
                turn(i, False)
            turn(3, True)

        @block.tensor
        def _(pe):
            pe.sem_inc(s_t, 1)
            pe.sem_inc(s_o, 1)
            pe.wait_ge(pa.s_vz, 6)
            with pe.Fori(0, 4) as i:
                def scores(s):
                    j, t = units[s]
                    u, kind = jobs[j]
                    n = tiles(s) * P
                    if t == 0 and kind == "fox":
                        pe.wait_ge(pa.s_fl[u], 96 * i + 96)
                    if t == 0 and kind == "sel":
                        pe.wait_ge(pa.s_nl[u], 32 * i + 32)
                        pe.wait_ge(pa.s_kl[u], 16 * 8)
                    pe.wait_ge(s_m, i * NU + max(0, s - 1) + 1)
                    k0 = first_tile(s) * P
                    fox = kind == "fox"
                    qq = q["fox" if fox else "nsa"][u]
                    for a in range(0, n, 512):
                        m = min(512, (n - a + 255) // 256 * 256, T - k0 - a)
                        last = a + 512 >= n
                        for w_ in range(2):
                            ins = pe.matmul(S[s % 2][:, a:a + m], qq[:, t * P:(t + 1) * P], k[kind][u][w_][:, k0 + a:k0 + a + m],
                                            start=(w_ == 0), stop=(w_ == 1) and not (fox and last), skip_group_check=fox)
                    if fox:
                        ins = pe.matmul(S[s % 2][:, n - P:n], c.ident16[:, :], c.causal16[:, :], start=False, stop=True,
                                        skip_group_check=True)
                    ins.then_inc(s_s, 1)

                def turn(s):
                    pe.wait_ge(s_e, i * NU + s + 1)
                    for n in of_unit[s]:
                        if n >= 2:
                            pe.wait_ge(s_cd, i * NCK + n - 1)
                        _, a, m = chunks[n]
                        for x in range(m):
                            ins = pe.transpose(PT[n % 2][:, x * P:(x + 1) * P], sc[s % 3][:, (a + x) * P:(a + x + 1) * P], c.ident[:, :])
                        ins.then_inc(s_t, 1)

                def values(s):
                    j, t = units[s]
                    u, kind = jobs[j]
                    pe.wait_ge(s_cd, i * NCK + of_unit[s][-1] + 1)
                    if t == 0 and kind == "fox":
                        pe.wait_ge(pa.s_vs[u], i + 1)
                    if t == 0 and kind == "sel":
                        pe.wait_ge(pa.s_gs, 4)
                    pe.wait_ge(s_n, i * NU + max(0, s - 1) + 1)
                    m = tiles(s)
                    for x in range(m):
                        at = first_tile(s) + x
                        for w_ in range(2):
                            ins = pe.matmul(O[s % 2][:, 0:2 * P], pT[s % 2][w_][:, x * P:(x + 1) * P],
                                            v[kind][u][:, at:at + 2, :, :].rearrange("p t w e -> p (t w e)"),
                                            start=(x == 0 and w_ == 0), stop=(x == m - 1 and w_ == 1))
                    ins.then_inc(s_o, 1)

                for s in range(NU + 3):
                    if s < NU:
                        scores(s)
                    if 0 <= s - 2 < NU:
                        turn(s - 2)
                    if 0 <= s - 3 < NU:
                        values(s - 3)

        @block.scalar
        def _(act):
            with act.Fori(0, 4) as i:
                for s in range(NU + 2):
                    if 0 <= s - 1 < NU:
                        e = s - 1
                        n = tiles(e) * P
                        act.wait_ge(s_m, i * NU + e + 2)
                        act.activation(sc[e % 3][:, 0:n], sc[e % 3][:, 0:n], ACT.Exp, bias=nm[:, e:e + 1], scale=-1.0,
                                       accum_out=sm[:, e:e + 1]).then_inc(s_e, 1)
                    if 0 <= s - 2 < NU:
                        e = s - 2
                        act.wait_ge(s_o, i * NU + max(0, e - 1) + 1)
                        for n in of_unit[e]:
                            _, a, m = chunks[n]
                            act.wait_ge(s_t, i * NCK + n + 2)
                            act.activation(pT[e % 2][0][:, a * P:(a + m) * P], PT[n % 2][:, 0:m * P], ACT.Copy).then_inc(s_ca, 1)

        @block.vector
        def _(dve):
            chain = Chain(dve, s_ch)
            dve.sem_inc(s_m, 1)
            dve.sem_inc(s_n, 1)
            dve.wait_ge(s_z, 4)
            per = sum(kind != "fox" for u, kind in jobs)
            with dve.Fori(0, 4) as i:
                chain.enter(i, per)

                def bias_and_max(s):
                    j, t = units[s]
                    u, kind = jobs[j]
                    n = tiles(s) * P
                    if t == 0 and kind == "fox":
                        dve.wait_ge(s_fb[u], 16 * i + 16)
                    if t == 0 and kind == "sel":
                        dve.wait_ge(s_nb[u], 32 * i + 32)
                    dve.wait_ge(s_t, i * NCK + (of_unit[s - 3][-1] + 2 if s >= 3 else 1))
                    dve.wait_ge(s_n, i * NU + 1)
                    dve.wait_ge(s_s, i * NU + s + 1)
                    settled(dve, c)
                    row = bias[kind][u][:, 0:n] if kind == "fox" else bias[kind][u][:, T - n:T]
                    dve.tensor_tensor_reduce(out=sc[s % 3][:, 0:n], in0=S[s % 2][:, 0:n], in1=row, scale=-1.0, scalar=3e38,
                                             op0=ALU.add, op1=ALU.min, accum_out=nm[:, s:s + 1]).then_inc(s_m, 1)

                def output(s):
                    j, t = units[s]
                    u, kind = jobs[j]
                    if t == 0:
                        dve.wait_ge(s_mg, 6 * i + j + 1)
                    dve.wait_ge(s_o, i * NU + s + 2)
                    dve.tensor_reduce(oj[j % 2][:, t, :], O[s % 2][:, 0:2 * HD].rearrange("p (w e) -> p e w", w=2), AX, ALU.add).then_inc(s_n, 1)
                    if t == NT - 1:
                        dve.wait_ge(s_e, i * NU + s + 1)
                        cj = co[:, j * NT:(j + 1) * NT]
                        ins = dve.reciprocal(cj, sm[:, j * NT:(j + 1) * NT])
                        if kind != "fox":
                            chain(ins)
                            h = i + GH * u
                            gate = c.gates[:, 0:NT, ds(h + (H if kind == "sel" else 2 * H), 1)]
                            ins = dve.tensor_tensor(cj, cj, gate.rearrange("p t a -> p (t a)"), ALU.mult)
                        ins.then_inc(s_co, 1)

                for s in range(NU + 4):
                    if s < NU:
                        bias_and_max(s)
                    if 0 <= s - 2 < NU:
                        e = s - 2
                        for n in of_unit[e]:
                            _, a, m = chunks[n]
                            dve.wait_ge(s_ca, i * NCK + n + 1)
                            dve.tensor_tensor(pT[e % 2][1][:, a * P:(a + m) * P], PT[n % 2][:, 0:m * P],
                                              pT[e % 2][0][:, a * P:(a + m) * P], ALU.subtract).then_inc(s_cd, 1)
                    if 0 <= s - 4 < NU:
                        output(s - 4)
            chain.leave(4)


def store_heads(c):
    nc, d = c.nc, c.d
    with Phase(nc) as ph:
        s_st = ph.sem("o_stored")
        block = ph.block()

        @block.sync
        def _(sp):
            sp.dma_start(d["op_d"].rearrange("(t p) n -> p t n", p=P), c.o[:, :, :]).then_inc(s_st, 16)
            sp.wait_ge(s_st, 16)


def output_projection(c, oT):
    nc, d = c.nc, c.d
    with Phase(nc) as ph:
        w = ph.sb("w_out_sb", [P, KD, D])
        ws = split(ph, "w_out_split", [P, KD, D])
        x = [ph.sb(f"op_x{i}", [P, D]) for i in range(3)]
        acc = [ph.ps(f"op_acc{i}", [P, D]) for i in range(2)]
        s_w = [ph.sem(f"w_out_loaded{k}") for k in range(KD)]
        s_hi = ph.sem("w_out_rounded")
        s_lo = ph.sem("w_out_split")
        s_x = [ph.sem(f"op_x_loaded{i}") for i in range(3)]
        s_pe = ph.sem("op_products")
        s_v = ph.sem("op_added")
        s_st = [ph.sem(f"op_stored{i}") for i in range(3)]
        block = ph.block()

        @block.sync
        def _(sp):
            for k in range(KD):
                sp.dma_start(w[:, k, :], d["w_out"][0, k * P:(k + 1) * P, :]).then_inc(s_w[k], 16)
            for t, rows in enumerate(ROWS):
                if t >= 3:
                    sp.wait_ge(s_st[t % 3], 16 * (t // 3))
                src = d["x_prompt"][0, t * P:(t + 1) * P, :] if t < NT else d["x_sample"].rearrange("b q n -> (b q) n")
                sp.dma_start(x[t % 3][0:rows, :], src).then_inc(s_x[t % 3], 16)

        @block.tensor
        def _(pe):
            for t, rows in enumerate(ROWS):
                if t >= 2:
                    pe.wait_ge(s_v, t - 1)
                for k in range(KD):
                    if t == 0:
                        pe.wait_ge(s_lo, k + 1)
                    for a in range(2):
                        ins = split_products(pe, acc[t % 2][0:rows, a * 512:(a + 1) * 512], oT, ws, np.s_[:, k, t * P:t * P + rows],
                                             np.s_[:, k, a * 512:(a + 1) * 512], k == 0, k == KD - 1)
                ins.then_inc(s_pe, 1)

        @block.scalar
        def _(act):
            for k in range(KD):
                act.wait_ge(s_w[k], 16)
                act.activation(ws[0][:, k, :], w[:, k, :], ACT.Copy).then_inc(s_hi, 1)

        @block.vector
        def _(dve):
            for k in range(KD):
                dve.wait_ge(s_hi, k + 1)
                dve.tensor_tensor(ws[1][:, k, :], w[:, k, :], ws[0][:, k, :], ALU.subtract).then_inc(s_lo, 1)
            for t, rows in enumerate(ROWS):
                dve.wait_ge(s_x[t % 3], 16 * (t // 3 + 1))
                dve.wait_ge(s_pe, t + 1)
                dve.tensor_tensor(x[t % 3][0:rows, :], acc[t % 2][0:rows, :], x[t % 3][0:rows, :], ALU.add).then_inc(s_v, 1)

        @block.gpsimd
        def _(pool):
            for t, rows in enumerate(ROWS):
                pool.wait_ge(s_v, t + 1)
                pool.dma_start(d["x1_d"][t * P:t * P + rows, :], x[t % 3][0:rows, :]).then_inc(s_st[t % 3], 16)
            for i in range(3):
                pool.wait_ge(s_st[i], 16 * 3)


def gate_up(c, hT, act_T):
    nc, d = c.nc, c.d
    w_gu = d["w_gu"][0].rearrange("(k p) n -> p k n", p=P)
    SG = NQ + 2
    with Phase(nc) as ph:
        w = [ph.sb(f"w_{n}", [P, KD, P]) for n in ("gate", "up")]
        ws = [split(ph, f"w_{n}_split", [P, KD, P]) for n in ("gate", "up")]
        GW = 2 + T + NB * SG
        work = ph.sb("gate_work", [P, 2 * GW + 2 * TT])
        g = [work[:, i * GW:(i + 1) * GW] for i in range(2)]
        gc = [work[:, 2 * GW + i * TT:2 * GW + (i + 1) * TT] for i in range(2)]
        rows_io = work[0:2 + 2 * NB, 0:FF]
        cw_rows = ph.sb("conv_w_rows", [4 * NF, P])
        cw = ph.sb("conv_w_T", [P, 4, NF])
        cwn = [ph.sb(f"conv_w_now{i}", [P, 4]) for i in range(2)]
        hist = ph.sb("hist_T", [P, NF, 2 * NB])
        edge = ph.sb("edge_T", [P, NF, 2 + 2 * NB])
        G_ = ph.ps("gate_acc", [P, 3, 512])
        U_ = ph.ps("up_acc", [P, 3, 512])
        E_ = [ph.ps(f"edge_ps{i}", [P, 4, P]) for i in range(2)]
        s_ld = ph.sem("conv_tables_loaded")
        s_et = ph.sem("hist_turned")
        s_ec = ph.sem("hist_copied")
        s_w = [ph.sem(f"w_{n}_loaded") for n in ("gate", "up")]
        s_hi = [ph.sem(f"w_{n}_rounded") for n in ("gate", "up")]
        s_lo = [ph.sem(f"w_{n}_split") for n in ("gate", "up")]
        s_g = ph.sem("gate_products")
        s_u = ph.sem("up_products")
        s_gc = ph.sem("gate_copied")
        s_z = ph.sem("halo_zeroed")
        s_cv = ph.sem("convolved")
        s_si = ph.sem("silu_done")
        s_a = ph.sem("act_done")
        s_ch = ph.sem("gu_chain")
        s_xt = ph.sem("edge_turned")
        s_xc = ph.sem("edge_copied")
        s_st = ph.sem("edge_stored")
        block = ph.block()
        NE = (NF + 3) // 4

        @block.sync
        def _(sp):
            sp.dma_start(cw_rows[0:3 * NF, :], d["conv_w"][0].rearrange("w (f p) -> (w f) p", p=P)).then_inc(s_ld, 16)
            sp.dma_start(cw_rows[3 * NF:4 * NF, :], d["conv_b"][0].rearrange("(f p) -> f p", p=P)).then_inc(s_ld, 16)
            sp.dma_start(rows_io[0:2 * NB, :], d["state_conv"][0].rearrange("b r n -> (b r) n")).then_inc(s_ld, 16)
            for side in range(2):
                sp.sem_inc(s_lo[side], 1)
            with sp.Fori(0, NF) as f:
                for side in range(2):
                    sp.wait_ge(s_lo[side], f + 1)
                    sp.dma_start(w[side][:, :, :], w_gu[:, :, ds(f * P + side * FF, P)]).then_inc(s_w[side], 16)

        @block.tensor
        def _(pe):
            pe.wait_ge(s_ld, 48)
            pe.transpose(E_[0][:, 0, 0:4 * NF], cw_rows[:, :], c.ident[0:4 * NF, 0:4 * NF]).then_inc(s_et, 1)
            for f in range(NF):
                if f % 4 == 0:
                    pe.wait_ge(s_ec, f // 4 if f else 1)
                ins = pe.transpose(E_[(f // 4 + 1) % 2][:, f % 4, 0:2 * NB], rows_io[0:2 * NB, f * P:(f + 1) * P],
                                   c.ident[0:2 * NB, 0:2 * NB])
                if f % 4 == 3 or f == NF - 1:
                    ins.then_inc(s_et, 1)
            with pe.Fori(0, NF // 2) as i:
                for b in range(2):
                    f = 2 * i + b
                    for side, (acc, sem, free) in enumerate(((G_, s_g, s_gc), (U_, s_u, s_a))):
                        pe.wait_ge(s_lo[side], f + 2)
                        pe.wait_ge(free, f + 1)
                        for n in range(3):
                            for k in range(KD):
                                ins = split_products(pe, acc[:, n, 0:CH], ws[side], hT, np.s_[:, k, :],
                                                     np.s_[:, k, n * CH:(n + 1) * CH], k == 0, k == KD - 1)
                        ins.then_inc(sem, 1)
            for f in range(NF):
                if f % 4 == 0:
                    pe.wait_ge(s_cv, NF + 1)
                    if f // 4 >= 2:
                        pe.wait_ge(s_xc, f // 4 - 1)
                ins = pe.transpose(E_[f // 4 % 2][0:2 + 2 * NB, f % 4, :], edge[:, f, :], c.ident[:, :])
                if f % 4 == 3 or f == NF - 1:
                    ins.then_inc(s_xt, 1)

        @block.scalar
        def _(act):
            act.wait_ge(s_z, 2)
            act.wait_ge(s_ec, NE + 1)
            act.sem_inc(s_gc, 1)
            act.sem_inc(s_g, 1)
            act.sem_inc(s_u, 1)
            with act.Fori(0, NF // 2) as i:
                for b in range(2):
                    f = 2 * i + b
                    for side, used in enumerate((s_g, s_u)):
                        act.wait_ge(s_w[side], 16 * f + 16)
                        act.wait_ge(used, f + 1)
                        act.activation(ws[side][0][:, :, :], w[side][:, :, :], ACT.Copy).then_inc(s_hi[side], 1)
                    act.wait_ge(s_g, f + 2)
                    act.wait_ge(s_cv, f + 1)
                    new = g[b][:, 2 + T:].rearrange("p (b r) -> p b r", b=NB)
                    act.activation(g[b][:, 2:2 + 2 * CH].rearrange("p (a n) -> p a n", a=2), G_[:, 0:2, 0:CH], ACT.Copy)
                    act.activation(g[b][:, 2 + 2 * CH:2 + T], G_[:, 2, 0:CH - NS], ACT.Copy)
                    act.activation(new[:, :, 2:SG], G_[:, 2, CH - NS:CH].rearrange("p (b q) -> p b q", q=NQ), ACT.Copy).then_inc(s_gc, 1)
                    act.wait_ge(s_cv, f + 2)
                    act.activation(gc[b], gc[b], ACT.Silu).then_inc(s_si, 1)

        @block.vector
        def _(dve):
            dve.wait_ge(s_et, 1)
            dve.tensor_copy(cw[:, :, :].rearrange("p w f -> p (w f)"), E_[0][:, 0, 0:4 * NF]).then_inc(s_ec, 1)
            for n in range(NE):
                m = min(4, NF - 4 * n)
                dve.wait_ge(s_et, n + 2)
                dve.tensor_copy(hist[:, 4 * n:4 * n + m, :], E_[(n + 1) % 2][:, 0:m, 0:2 * NB]).then_inc(s_ec, 1)
            dve.wait_ge(s_ec, NE + 1)
            for b in range(2):
                dve.memset(g[b][:, 0:2], 0.0).then_inc(s_z, 1)
            dve.wait_ge(s_z, 2)
            dve.sem_inc(s_cv, 1)
            dve.sem_inc(s_a, 1)
            chain = Chain(dve, s_ch)
            with dve.Fori(0, NF // 2) as i:
                chain.enter(i, 2 * 3)
                for b in range(2):
                    f = 2 * i + b
                    k = cwn[b]
                    new = g[b][:, 2 + T:].rearrange("p (b r) -> p b r", b=NB)
                    out = gc[b][:, T:].rearrange("p (b q) -> p b q", q=NQ)
                    dve.wait_ge(s_a, f + 1)
                    dve.tensor_copy(k[:, :], cw[:, :, ds(f, 1)].rearrange("p w a -> p (w a)"))
                    chain(dve.tensor_copy(new[:, :, 0:2], hist[:, ds(f, 1), :].rearrange("p a (b r) -> p (a b) r", r=2)))
                    dve.wait_ge(s_gc, f + 2)
                    dve.tensor_copy(edge[:, ds(f, 1), 0:2].rearrange("p a r -> p (a r)"), g[b][:, T:T + 2])
                    dve.tensor_copy(edge[:, ds(f, 1), 2:].rearrange("p a (b r) -> p (a b) r", r=2), new[:, :, NQ:SG])
                    for w_ in range(3):
                        for dst, src in ((gc[b][:, 0:T], g[b][:, w_:w_ + T]), (out, new[:, :, w_:w_ + NQ])):
                            if w_ == 0:
                                ins = dve.tensor_scalar(dst, src, k[:, 0:1], k[:, 3:4], ALU.mult, ALU.add)
                            else:
                                ins = dve.scalar_tensor_tensor(out=dst, in0=src, scalar=k[:, w_:w_ + 1], in1=dst,
                                                               op0=ALU.mult, op1=ALU.add)
                        if w_ < 2:
                            chain(ins)
                        else:
                            ins.then_inc(s_cv, 1)
                    dve.wait_ge(s_si, f + 1)
                    dve.wait_ge(s_u, f + 2)
                    dve.tensor_tensor(act_T[:, ds(f, 1), :].rearrange("p a (m n) -> p (a m) n", m=3),
                                      gc[b].rearrange("p (m n) -> p m n", m=3), U_[:, :, 0:CH], ALU.mult).then_inc(s_a, 1)
            chain.leave(NF // 2)
            dve.wait_ge(s_a, NF + 1)
            for n in range(NE):
                m = min(4, NF - 4 * n)
                dve.wait_ge(s_xt, n + 1)
                dve.tensor_copy(rows_io[:, n * 512:n * 512 + m * P], E_[n % 2][0:2 + 2 * NB, 0:m, :].rearrange("p a n -> p (a n)"))\
                   .then_inc(s_xc, 1)

        @block.gpsimd
        def _(pool):
            with pool.Fori(0, NF) as f:
                for side in range(2):
                    pool.wait_ge(s_hi[side], f + 1)
                    pool.tensor_tensor(ws[side][1][:, :, :], w[side][:, :, :], ws[side][0][:, :, :], ALU.subtract).then_inc(s_lo[side], 1)
            pool.wait_ge(s_xc, NE)
            pool.dma_start(d["conv_p"][0, 0], rows_io[0:2, :]).then_inc(s_st, 16)
            pool.dma_start(d["conv_s"][0].rearrange("b r n -> (b r) n"), rows_io[2:2 + 2 * NB, :]).then_inc(s_st, 16)
            pool.wait_ge(s_st, 32)


def down(c, act_T):
    nc, d = c.nc, c.d
    NQT, QW = 4, D // 4
    with Phase(nc) as ph:
        w = [ph.sb(f"w_down{i}", [P, NF, QW]) for i in range(2)]
        y = ph.sb("y_rows", [P, 9, D])
        g = ph.sb("final_gain", [P, D])
        sq = ph.sb("y_squares", [P, D])
        ss = ph.sb("y_ss", [P, 4, 9])
        acc = [ph.ps(f"y_acc{i}", [P, 512]) for i in range(2)]
        s_w = [ph.sem(f"w_down_loaded{i}") for i in range(2)]
        s_x = ph.sem("x1_loaded")
        s_g = ph.sem("final_gain_loaded")
        s_pe = ph.sem("down_products")
        s_v = ph.sem("down_added")
        s_sq = ph.sem("y_squared")
        s_ms = ph.sem("y_mean")
        s_rt = ph.sem("y_root")
        s_rr = ph.sem("y_inverse")
        s_y = ph.sem("y_normed")
        s_st = ph.sem("y_stored")
        block = ph.block()
        w_d = d["w_down"][0].rearrange("(f p) n -> p f n", p=P)

        @block.sync
        def _(sp):
            sp.dma_start(w[0][:, :, :], w_d[:, :, 0:QW]).then_inc(s_w[0], 16)
            sp.dma_start(y[:, 0:NT, :], d["x1_d"][0:T, :].rearrange("(t p) n -> p t n", p=P)).then_inc(s_x, 16)
            sp.dma_start(y[0:NS, NT, :], d["x1_d"][T:TT, :]).then_inc(s_x, 16)
            sp.dma_start(w[1][:, :, :], w_d[:, :, QW:2 * QW]).then_inc(s_w[1], 16)
            sp.dma_start(g[:, :], d["final_norm_g"].rearrange("(a n) -> a n", a=1).to_broadcast([P, D])).then_inc(s_g, 16)
            for n in range(2, NQT):
                sp.wait_ge(s_pe, 9 * (n - 1))
                sp.dma_start(w[n % 2][:, :, :], w_d[:, :, n * QW:(n + 1) * QW]).then_inc(s_w[n % 2], 16)

        @block.tensor
        def _(pe):
            with pe.Fori(0, NQT // 2) as i:
                for b in range(2):
                    pe.wait_ge(s_w[b], 16 * i + 16)
                    for t, rows in enumerate(ROWS):
                        s = 9 * b + t
                        pe.wait_ge(s_v, i * 18 + max(0, s - 1) + 1)
                        for f in range(NF):
                            ins = pe.matmul(acc[s % 2][0:rows, 0:QW], act_T[:, f, t * P:t * P + rows], w[b][:, f, :],
                                            start=(f == 0), stop=(f == NF - 1))
                        ins.then_inc(s_pe, 1)

        @block.vector
        def _(dve):
            dve.sem_inc(s_v, 1)
            dve.wait_ge(s_x, 32)
            for n in range(NQT):
                for t, rows in enumerate(ROWS):
                    s = 9 * n + t
                    dve.wait_ge(s_pe, s + 1)
                    dst = y[0:rows, t, n * QW:(n + 1) * QW]
                    dve.tensor_tensor(dst, acc[s % 2][0:rows, 0:QW], dst, ALU.add).then_inc(s_v, 1)
            dve.wait_ge(s_g, 16)
            for t, rows in enumerate(ROWS):
                dve.wait_ge(s_sq, t + 1)
                dve.tensor_scalar(ss[0:rows, 1, t:t + 1], ss[0:rows, 0, t:t + 1], 1.0 / D, EPS, ALU.mult, ALU.add).then_inc(s_ms, 1)
                dve.wait_ge(s_rt, t + 1)
                dve.reciprocal(ss[0:rows, 3, t:t + 1], ss[0:rows, 2, t:t + 1]).then_inc(s_rr, 1)
                dve.wait_ge(s_rr, t + 1)
                dve.scalar_tensor_tensor(out=y[0:rows, t, :], in0=y[0:rows, t, :], scalar=ss[0:rows, 3, t:t + 1],
                                         in1=g[0:rows, :], op0=ALU.mult, op1=ALU.mult).then_inc(s_y, 1)

        @block.scalar
        def _(act):
            for t, rows in enumerate(ROWS):
                act.wait_ge(s_v, 9 * (NQT - 1) + t + 2)
                if t:
                    act.wait_ge(s_sq, t)
                act.activation(sq[0:rows, :], y[0:rows, t, :], ACT.Square, accum_out=ss[0:rows, 0, t:t + 1]).then_inc(s_sq, 1)
                act.wait_ge(s_ms, t + 1)
                act.activation(ss[0:rows, 2, t:t + 1], ss[0:rows, 1, t:t + 1], ACT.Sqrt).then_inc(s_rt, 1)

        @block.gpsimd
        def _(pool):
            for t, rows in enumerate(ROWS):
                pool.wait_ge(s_y, t + 1)
                dst = d["y_p"][0, t * P:(t + 1) * P, :] if t < NT else d["y_s"].rearrange("b q n -> (b q) n")
                pool.dma_start(dst, y[0:rows, t, :]).then_inc(s_st, 16)
            pool.wait_ge(s_st, 16 * 9)


def buckets(n):
    n = np.asarray(n)
    exact = NBK // 2
    far = exact + (np.log(np.maximum(n, 1) / exact) / math.log(128 / exact) * (NBK - exact) + 1e-9).astype(np.int64)
    return np.where(n < exact, np.maximum(n, 0), np.minimum(far, NBK - 1))


def one_hot(dist):
    dist = np.asarray(dist)
    b = buckets(dist)
    m = (np.arange(NBK).reshape((-1,) + (1,) * dist.ndim) == b[None]) & (dist >= 0)[None]
    return np.concatenate([m.astype(np.float32), np.where(dist < 0, np.float32(NEG), np.float32(0))[None]])


MISC = {}


def constants():
    c = {}
    c["c_oh"] = one_hot(255 - np.arange(383))
    m = np.arange(16) - 9
    c["c_cmp"] = one_hot(np.arange(P)[None, :] - (CLEN - 1) - NSTR * m[:, None])
    q = np.arange(NQ)[:, None]
    near = 768 + 2 * np.arange(P)[None, :] + np.arange(2)[:, None]
    smp = np.concatenate([
        T + q - near.reshape(1, -1),
        q - np.arange(NQ)[None, :],
        T + q - (T - P + np.arange(P))[None, :],
        T + q - (NSTR * np.arange(NC) + CLEN - 1)[None, :]], axis=1)
    c["c_smp"] = one_hot(smp)
    rel = np.zeros((NBK, NBK + 1), np.float32)
    rel[np.arange(NBK), np.arange(NBK)] = 1
    rel[NBK - 1, 0:NBK] -= 1
    c["c_rel"] = rel
    c["c_one"] = np.eye(NBK + 1, dtype=np.float32)[:, NBK:]
    parts = {}
    w = np.arange(P)
    parts["wmask"] = np.where(w[None, :] <= w[:, None], np.float32(NEG), np.float32(0))
    hq = np.arange(HQ)
    wm = np.zeros((P, P), np.float32)
    wm[:HQ] = np.where(w[None, :] <= (hq % NQ)[:, None], np.float32(NEG), np.float32(0))
    parts["wmask_s"] = wm
    ms = np.zeros((P, NSEL), np.float32)
    st, js = np.arange(NC) * NSTR, np.arange(NSEL) * HD
    ms[:NC] = (st[:, None] < js[None, :] + HD) & (st[:, None] + CLEN > js[None, :])
    parts["to_sel"] = ms
    gs = np.zeros((P, HQ), np.float32)
    gs[:HQ] = (hq[:, None] // (NQ * GH) == hq[None, :] // (NQ * GH)) & (hq[:, None] % NQ == hq[None, :] % NQ)
    parts["group_sum"] = gs
    bm = np.zeros((P, H * HD), np.float32)
    bm[:HQ] = np.repeat(hq[:, None] // NQ == np.arange(H)[None, :], HD, axis=1)
    parts["own_head"] = bm
    gm = np.zeros((P, G), np.float32)
    gm[:HQ] = hq[:, None] // (NQ * GH) == np.arange(G)[None, :]
    parts["own_group"] = gm
    parts["block_no"] = np.tile(np.arange(1, 15, dtype=np.float32), (P, 1))
    ne = np.zeros((P, HQ), np.float32)
    ne[:H] = -(np.arange(H)[:, None] == hq[None, :] // NQ).astype(np.float32)
    parts["neg_head"] = ne
    seen = np.ones((P, NT, H), np.float32)
    seen[0:CLEN - 1, 0] = 0
    parts["seen"] = seen.reshape(P, NT * H)
    cm = np.zeros((P, NQ), np.float32)
    cm[:HQ] = np.where(np.arange(NQ)[None, :] > (hq % NQ)[:, None], np.float32(NEG), np.float32(0))
    parts["causal_new"] = cm
    at = 0
    for k, v in parts.items():
        MISC[k] = (at, at + v.shape[1])
        at += v.shape[1]
    c["c_misc"] = np.concatenate(list(parts.values()), axis=1).astype(np.float32)
    return c


def build(nc, d):
    c = Ctx(nc, d)
    with Phase(nc) as top, nc.allow_non_contiguous_dma(reason="small tables of single elements"):
        c.passed = top.sem("passed")
        c.ident = top.sb("ident", [P, P])
        c.ident16 = top.sb("ident16", [P, P], BF16)
        c.causal16 = top.sb("causal16", [P, P], BF16)
        c.one = top.sb("one", [H, 1])
        c.zero = top.sb("zero", [P, 1])
        with Phase(nc) as mix:
            c.cb = mix.sb("cb", [P, H, 119])
            c.bias_s = mix.sb("bias_s", [HQ, 451])
            c.misc = mix.sb("misc", [P, d["c_misc"].shape[1]])
            c.pt = mix.sb("page_ids", [1, NB * PAGES], I32)
            c.gates = mix.sb("gates", [P, 9, 24])
            setup(c)
            c.q_smp = mix.sb("q_smp", [P, 2, 4, NS])
            c.kf_new = mix.sb("kf_new", [P, 4, NS])
            c.ks_new = mix.sb("ks_new", [P, 1, NS])
            c.kw_new = mix.sb("kw_new", [P, 1, NS])
            c.lf_new = mix.sb("lf_new", [H, NS])
            c.kc_p = mix.sb("kc_prompt", [P, NC])
            c.vc_p = mix.sb("vc_prompt", [NC, G * HD])
            with Phase(nc) as ph:
                hT = c.hT = split(ph, "h_T", [P, KD, TT])
                norm_transpose(c, "n1", lambda t: d["x_prompt"][0, t * P:(t + 1) * P, :] if t < NT
                               else d["x_sample"].rearrange("b q n -> (b q) n"),
                               d["norm1_g"][0:1, :].to_broadcast([P, D]), 1, hT)
                project_transposed(c)
                project_rows(c)
            with Phase(nc) as ph:
                compress_weights(c, ph)
                sample_attention(c)
                prompt_compress(c)
            with Phase(nc) as ph:
                c.o = ph.sb("o_prompt", [P, NT, D])
                with Phase(nc) as inputs:
                    pa = AttentionInputs(c, inputs)
                    compressed_attention(c, pa)
                    prompt_attention(c, pa)
                store_heads(c)
        with Phase(nc) as ph:
            oT = split(ph, "o_T", [P, KD, TT])
            norm_transpose(c, "no", lambda t: d["op_d"][t * P:(t + 1) * P, :] if t < NT else d["os_d"],
                           d["out_norm_g"][0:1, :].to_broadcast([P, D]), 2, oT)
            output_projection(c, oT)
        with Phase(nc) as ph:
            act_T = ph.sb("act_T", [P, NF, TT])
            with Phase(nc) as inner:
                h2T = split(inner, "h2_T", [P, KD, TT])
                norm_transpose(c, "n2", lambda t: d["x1_d"][t * P:t * P + ROWS[t], :],
                               d["norm2_g"][0:1, :].to_broadcast([P, D]), 1, h2T)
                gate_up(c, h2T, act_T)
            down(c, act_T)
    return c


_OUTS = [("y_p", (1, T, D)), ("y_s", (NB, NQ, D)),
         ("fox_kv_p", (1, 1, T, 2, H, HD)), ("fox_kv_s", (1, NB, NQ, 2, H, HD)),
         ("logf_p", (1, 1, T, H)), ("logf_s", (1, NB, NQ, H)),
         ("nsa_kv_p", (1, 1, T, 4, G, HD)), ("nsa_kv_s", (1, NB, NQ, 4, G, HD)),
         ("win_kv_p", (1, 1, WIN, 2, G, HD)), ("win_kv_s", (1, NB, WIN, 2, G, HD)),
         ("conv_p", (1, 1, 2, FF)), ("conv_s", (1, NB, 2, FF))]
_SCRATCH = [("qfs_d", (2, H, HD, T)), ("qns_d", (2, H, HD, T)), ("kf_d", (2, H, HD, T)), ("qn_d", (H, HD, T)),
            ("ks_d", (2, G, HD, T)), ("kw_d", (2, G, HD, T)), ("vw_d", (T, G * HD)),
            ("nc_d", (H, T)), ("rep_d", (H, P, 383)), ("tb_d", (H, P, 256)), ("os_d", (NS, D)), ("op_d", (T, D)), ("gs_d", (NS, 24)),
            ("x1_d", (TT, D))]


def declare(nc, inputs):
    arrays, d = {}, {}
    for name, a in {**inputs, **constants()}.items():
        a = np.ascontiguousarray(a)
        arrays[f"in_{name}"] = a
        d[name] = nc.dram_tensor(f"in_{name}", a.shape, mybir.dt.from_np(a.dtype), kind="ExternalInput").ap()
    for name, shape in _OUTS:
        d[name] = nc.dram_tensor(f"out_{name}", shape, F32, kind="ExternalOutput").ap()
    for name, shape in _SCRATCH:
        d[name] = nc.dram_tensor(f"scratch_{name}", shape, F32, kind="Internal").ap()
    return arrays, d


def kernel(**inputs):
    import concourse.bacc as bacc
    from concourse.bass_utils import run_bass_kernel_spmd

    nc = bacc.Bacc("TRN2", target_bir_lowering=False, num_devices=1)
    arrays, d = declare(nc, inputs)
    build(nc, d)
    r = run_bass_kernel_spmd(nc, [arrays], core_ids=[0])
    return tuple(r.results[0][f"out_{name}"] for name, _ in _OUTS)
```

```python
import math
from contextlib import ExitStack

import numpy as np

import concourse.bass as bass
from concourse import mybir

F32 = mybir.dt.float32
BF16 = mybir.dt.bfloat16
FR = mybir.dt.float32r
I32 = mybir.dt.int32
ALU = mybir.AluOpType
ACT = mybir.ActivationFunctionType
AX = mybir.AxisListType.X
ds = bass.ds

P = 128
D = 1024
T = 1024
NB, NQ = 8, 4
NS = NB * NQ
TT = T + NS
NT = T // P
KD = D // P
HD = 64
H = 8
G = 2
GH = H // G
HQ = H * NQ
PAGES = 8
NSTR, CLEN = 16, 32
NC = T // NSTR - 1
NSEL = T // HD + 1
WIN = 512
NBK = 32
FF = 2816
NF = FF // P
EPS = 1e-6
NEG = -1e30
C_QF, C_KF, C_VF, C_F, C_QN, C_NSA, C_WIN, C_GATE, C_END = 0, 512, 1024, 1536, 1544, 2056, 2568, 2824, 2848
ROWS = [P] * NT + [NS]
CH = TT // 3


class Chain:

    def __init__(self, eng, sem):
        self.eng, self.sem, self.done, self.at = eng, sem, 0, 0

    def enter(self, i, per):
        self.at, self.k, self.per = self.done + i * per, 0, per

    def leave(self, n):
        assert self.k == self.per, (self.k, self.per)
        self.done += n * self.per
        self.at, self.k = self.done, 0

    k = 0

    def __call__(self, ins):
        ins.then_inc(self.sem, 1)
        self.k += 1
        self.eng.wait_ge(self.sem, self.at + self.k)


class Ctx:

    def __init__(self, nc, dram):
        self.nc, self.d = nc, dram


class Phase:

    def __init__(self, nc):
        self.nc, self.stack, self.sems = nc, ExitStack(), []

    def __enter__(self):
        self.stack.__enter__()
        return self

    def __exit__(self, *a):
        done = self.stack.__exit__(*a)
        if self.sems:
            self.nc.clear_and_free_semaphores(self.sems)
            self.nc.all_engine_barrier()
        return done

    def sb(self, name, shape, dt=F32):
        return self.stack.enter_context(self.nc.sbuf_tensor(name, shape, dt))

    def ps(self, name, shape, dt=F32):
        return self.stack.enter_context(self.nc.psum_tensor(name, shape, dt))

    def sem(self, name):
        self.sems.append(self.nc.alloc_semaphore(name))
        return self.sems[-1]

    def block(self):
        return self.stack.enter_context(self.nc.Block())


def split(ph, name, shape):
    return ph.sb(f"{name}_hi", shape, FR), ph.sb(f"{name}_lo", shape, FR)


def split_products(pe, out, a, b, at, bt, start, stop):
    pe.matmul(out, a[0][at], b[0][bt], start=start, stop=False)
    pe.matmul(out, a[0][at], b[1][bt], start=False, stop=False)
    return pe.matmul(out, a[1][at], b[0][bt], start=False, stop=stop)


def settled(eng, c):
    eng.sem_inc(c.passed, 1)


def norm_transpose(c, name, source, gain, groups, out, resident=None):
    nc = c.nc
    W = D // groups
    with Phase(nc) as ph:
        x = ph.sb(f"{name}_x", [P, 4, D]) if resident is None else ph.sb(f"{name}_x", [P, 1, D])
        xn = ph.sb(f"{name}_xn", [P, 2, D])
        sq = ph.sb(f"{name}_sq", [P, 2, D])
        g = ph.sb(f"{name}_gain", [P, D])
        ss = ph.sb(f"{name}_ss", [P, 9, groups])
        ms = ph.sb(f"{name}_ms", [P, 9, groups])
        rt = ph.sb(f"{name}_rt", [P, 9, groups])
        rr = ph.sb(f"{name}_rr", [P, 9, groups])
        tp = [ph.ps(f"{name}_tp{i}", [P, D]) for i in range(2)]
        s_x = [ph.sem(f"{name}_x_loaded{i}") for i in range(4)]
        s_g = ph.sem(f"{name}_gain_loaded")
        s_ss = ph.sem(f"{name}_squares")
        s_ms = ph.sem(f"{name}_mean")
        s_rt = ph.sem(f"{name}_root")
        s_rr = ph.sem(f"{name}_inverse")
        s_xn = ph.sem(f"{name}_normed")
        s_tr = ph.sem(f"{name}_transposed")
        s_ev = ph.sem(f"{name}_copied")
        s_lo = ph.sem(f"{name}_rest_kept")
        block = ph.block()

        def rows_of(t, cols):
            if resident is not None:
                return resident[:, t, cols] if t < NT else x[0:NS, 0, cols]
            return x[0:ROWS[t], t % 4, cols]

        @block.sync
        def _(sp):
            for t, rows in enumerate(ROWS):
                if resident is not None and t < NT:
                    continue
                if resident is None and t >= 4:
                    sp.wait_ge(s_xn, t - 3)
                sp.dma_start(rows_of(t, slice(0, D)), source(t)).then_inc(s_x[t % 4], 16)
                if t == 0:
                    sp.dma_start(g[:, :], gain).then_inc(s_g, 16)
            if resident is not None:
                sp.dma_start(g[:, :], gain).then_inc(s_g, 16)

        @block.scalar
        def _(act):
            def squares(t):
                rows = ROWS[t]
                if resident is None:
                    act.wait_ge(s_x[t % 4], 16 * (t // 4 + 1))
                elif t == NT:
                    act.wait_ge(s_x[t % 4], 16)
                if t >= 2:
                    act.wait_ge(s_ss, groups * (t - 1))
                for k in range(groups):
                    act.activation(sq[0:rows, t % 2, k * W:(k + 1) * W], rows_of(t, slice(k * W, (k + 1) * W)), ACT.Square,
                                   accum_out=ss[0:rows, t, k:k + 1]).then_inc(s_ss, 1)

            def root(t):
                rows = ROWS[t]
                act.wait_ge(s_ms, t + 1)
                act.activation(rt[0:rows, t, :], ms[0:rows, t, :], ACT.Sqrt).then_inc(s_rt, 1)

            def copy(t):
                rows = ROWS[t]
                act.wait_ge(s_tr, t + 1)
                act.activation(out[0][:, :, t * P:t * P + rows],
                               tp[t % 2][:, :].rearrange("p (k n) -> p k n", k=KD)[:, :, 0:rows],
                               ACT.Copy).then_inc(s_ev, 1)

            n = len(ROWS)
            squares(0)
            for t in range(n):
                if t + 1 < n:
                    squares(t + 1)
                root(t)
                if t >= 1:
                    copy(t - 1)
            copy(n - 1)

        @block.vector
        def _(dve):
            def mean(t):
                dve.wait_ge(s_ss, groups * (t + 1))
                dve.tensor_scalar(ms[0:ROWS[t], t, :], ss[0:ROWS[t], t, :], 1.0 / W, EPS, ALU.mult, ALU.add).then_inc(s_ms, 1)

            def rest(t):
                rows = ROWS[t]
                dve.wait_ge(s_ev, t + 1)
                dve.tensor_tensor(out[1][:, :, t * P:t * P + rows],
                                  tp[t % 2][:, :].rearrange("p (k n) -> p k n", k=KD)[:, :, 0:rows],
                                  out[0][:, :, t * P:t * P + rows], ALU.subtract).then_inc(s_lo, 1)

            mean(0)
            for t, rows in enumerate(ROWS):
                if t + 1 < len(ROWS):
                    mean(t + 1)
                dve.wait_ge(s_rt, t + 1)
                dve.reciprocal(rr[0:rows, t, :], rt[0:rows, t, :]).then_inc(s_rr, 1)
                dve.wait_ge(s_rr, t + 1)
                if t == 0:
                    dve.wait_ge(s_g, 16)
                if t >= 2:
                    dve.wait_ge(s_tr, t - 1)
                for k in range(groups):
                    ins = dve.scalar_tensor_tensor(
                        out=xn[0:rows, t % 2, k * W:(k + 1) * W], in0=rows_of(t, slice(k * W, (k + 1) * W)),
                        scalar=rr[0:rows, t, k:k + 1], in1=g[0:rows, k * W:(k + 1) * W], op0=ALU.mult, op1=ALU.mult)
                ins.then_inc(s_xn, 1)
                if t >= 1:
                    rest(t - 1)
            rest(len(ROWS) - 1)

        @block.tensor
        def _(pe):
            for t, rows in enumerate(ROWS):
                pe.wait_ge(s_xn, t + 1)
                if t >= 2:
                    pe.wait_ge(s_lo, t - 1)
                for k in range(KD):
                    ins = pe.transpose(tp[t % 2][:, k * P:k * P + rows], xn[0:rows, t % 2, k * P:(k + 1) * P],
                                       c.ident[0:rows, 0:rows])
                ins.then_inc(s_tr, 1)


def setup(c):
    nc, d = c.nc, c.d
    with Phase(nc) as ph:
        ro = ph.sb("ro_rows", [H, 383])
        oh = ph.sb("oh_prompt", [NBK + 1, 383])
        ohc = ph.sb("oh_cmp", [NBK + 1, 16, P])
        ohs = ph.sb("oh_sample", [NBK + 1, NQ, 451])
        rel = ph.sb("rel_diff", [NBK, NBK + 1])
        one_last = ph.sb("one_last", [NBK + 1, 1])
        rb = ph.sb("rb", [NBK, H])
        rba = ph.sb("rba", [NBK + 1, H])
        rbx = ph.sb("rbx", [NBK + 1, NQ, H, NQ])
        ps_r = ph.ps("ps_r", [P, 512])
        ps_row = ph.ps("ps_row", [P, 512])
        ps_c = ph.ps("ps_c", [P, 16, H])
        ps_s = ph.ps("ps_s", [P, 512])
        s_ld = ph.sem("tables_loaded")
        s_id = ph.sem("fills")
        s_pe = ph.sem("table_products")
        s_v = ph.sem("table_copies")
        s_st = ph.sem("rows_stored")
        s_tb = ph.sem("toeplitz_stored")
        block = ph.block()

        @block.sync
        def _(sp):
            for dst, src in ((oh[:, :], d["c_oh"]), (ohc[:, :, :], d["c_cmp"]), (ohs[:, :, :], d["c_smp"]),
                             (rel[:, :], d["c_rel"]), (one_last[:, :], d["c_one"]), (rb[:, :], d["rel_bias"]),
                             (c.misc[:, :], d["c_misc"]), (c.pt[:, :], d["page_table"].rearrange("b p -> (b p)").rearrange("(a n) -> a n", a=1))):
                sp.dma_start(dst, src).then_inc(s_ld, 16)
            sp.wait_ge(s_v, 6)
            sp.dma_start(d["rep_d"], ro[:, :].rearrange("h (a n) -> h a n", a=1).to_broadcast([H, P, 383])).then_inc(s_st, 16)
            sp.wait_ge(s_st, 16)
            for h in range(H):
                sp.dma_start(d["tb_d"][h, :, :], bass.AP(d["rep_d"].tensor, h * P * 383 + 127, [[382, P], [1, 256]])).then_inc(s_tb, 16)
            sp.wait_ge(s_tb, 16 * H)

        @block.gpsimd
        def _(pool):
            pool.memset(c.ident[:, :], 0.0).then_inc(s_id, 1)
            pool.memset(c.ident16[:, :], 0.0).then_inc(s_id, 1)
            pool.memset(c.causal16[:, :], 0.0).then_inc(s_id, 1)
            pool.memset(c.cb[:, :, 0:47], 0.0).then_inc(s_id, 1)
            pool.memset(c.cb[:, :, 63:119], NEG).then_inc(s_id, 1)
            pool.memset(rbx[:, :, :, :], 0.0).then_inc(s_id, 1)
            pool.wait_ge(s_id, 6)
            for m in (c.ident, c.ident16):
                pool.affine_select(out=m[:, :], in_=m[:, :], compare_op=ALU.not_equal, fill=1.0, base=0,
                                   pattern=[[-1, P]], channel_multiplier=1).then_inc(s_id, 1)
            pool.affine_select(out=c.causal16[:, :], in_=c.causal16[:, :], compare_op=ALU.is_ge, fill=NEG, base=0,
                               pattern=[[-1, P]], channel_multiplier=1).then_inc(s_id, 1)
            pool.wait_ge(s_id, 9)
            pool.memset(c.one[:, :], 1.0)
            pool.memset(c.zero[:, :], 0.0)

        @block.tensor
        def _(pe):
            pe.wait_ge(s_ld, 16 * 8)
            pe.matmul(ps_r[0:NBK + 1, 0:H], rel[:, :], rb[:, :], start=True, stop=True).then_inc(s_pe, 1)
            pe.wait_ge(s_v, 1)
            pe.matmul(ps_row[0:H, 0:383], rba[:, :], oh[:, :], start=True, stop=True).then_inc(s_pe, 1)
            for m in range(16):
                ins = pe.matmul(ps_c[:, m, :], ohc[:, m, :], rba[:, :], start=True, stop=True)
            ins.then_inc(s_pe, 1)
            pe.wait_ge(s_v, 5)
            for q in range(NQ):
                ins = pe.matmul(ps_s[0:HQ, 0:451], rbx[:, q, :, :].rearrange("p h q -> p (h q)"), ohs[:, q, :],
                                start=(q == 0), stop=(q == NQ - 1))
            ins.then_inc(s_pe, 1)

        @block.vector
        def _(dve):
            dve.wait_ge(s_pe, 1)
            dve.tensor_scalar(rba[:, :], ps_r[0:NBK + 1, 0:H], one_last[:, 0:1], None, ALU.add).then_inc(s_v, 1)
            dve.wait_ge(s_v, 1)
            dve.wait_ge(s_id, 6)
            for q in range(NQ):
                dve.tensor_copy(rbx[:, q, :, q], rba[:, :]).then_inc(s_v, 1)
            dve.wait_ge(s_pe, 2)
            dve.tensor_copy(ro[:, :], ps_row[0:H, 0:383]).then_inc(s_v, 1)
            dve.wait_ge(s_pe, 3)
            dve.tensor_copy(c.cb[:, :, 47:63], ps_c[:, :, :].rearrange("p m h -> p h m")).then_inc(s_v, 1)
            dve.wait_ge(s_pe, 4)
            dve.tensor_copy(c.bias_s[:, :], ps_s[0:HQ, 0:451]).then_inc(s_v, 1)


ROW_CHUNKS = [("k_fox", C_KF, 512), ("v_fox", C_VF, 512), ("nsa", C_NSA, 512), ("win", C_WIN, 288)]


def project_transposed(c, w_rows, s_wr):
    nc, d = c.nc, c.d
    w_in = d["w_in"][0].rearrange("(k p) n -> p k n", p=P)
    with Phase(nc) as ph:
        w = [ph.sb(f"wq{i}", [P, KD, P]) for i in range(2)]
        ws = [split(ph, f"wq_split{i}", [P, KD, P]) for i in range(2)]
        z = [ph.sb(f"qt{i}", [P, TT]) for i in range(2)]
        zs = [split(ph, f"qt_split{i}", [P, T]) for i in range(2)]
        acc = [ph.ps(f"q_acc{i}", [P, 3, 512]) for i in range(2)]
        s_w = [ph.sem(f"wq_loaded{i}") for i in range(2)]
        s_hi = ph.sem("wq_rounded")
        s_lo = ph.sem("wq_split")
        s_pe = ph.sem("q_products")
        s_z = ph.sem("q_copied")
        s_zh = ph.sem("q_rounded")
        s_zs = ph.sem("q_split")
        s_st = [ph.sem(f"q_stored{i}") for i in range(2)]
        s_free = ph.sem("q_store_ended")
        block = ph.block()

        @block.sync
        def _(sp):
            sp.sem_inc(s_lo, 2)
            def load(i):
                for b, col in enumerate((C_QF, C_QN)):
                    sp.wait_ge(s_lo, 2 * i + b + 1)
                    sp.dma_start(w[b][:, :, :], w_in[:, :, ds(i * P + col, P)]).then_inc(s_w[b], 16)

            load(0)
            for ci in range(2):
                kind, col, n = ROW_CHUNKS[ci]
                sp.dma_start(w_rows[ci][:, :, :], w_in[:, :, col:col + n]).then_inc(s_wr[ci], 16)
            with sp.Fori(1, 4) as i:
                load(i)

        @block.vector
        def _(dve):
            def weights(i, b):
                dve.wait_ge(s_w[b], 16 * i + 16)
                dve.wait_ge(s_pe, 2 * i + b + 1)
                dve.tensor_copy(ws[b][0][:, :, :], w[b][:, :, :]).then_inc(s_hi, 1)
                dve.wait_ge(s_hi, 2 * i + b + 1)
                dve.tensor_tensor(ws[b][1][:, :, :], w[b][:, :, :], ws[b][0][:, :, :], ALU.subtract).then_inc(s_lo, 1)

            def queries(i, b):
                dve.wait_ge(s_z, 2 * i + b + 3)
                dve.tensor_copy(zs[b][0][:, :], z[b][:, 0:T]).then_inc(s_zh, 1)
                dve.wait_ge(s_zh, 2 * i + b + 1)
                dve.tensor_tensor(zs[b][1][:, :], z[b][:, 0:T], zs[b][0][:, :], ALU.subtract).then_inc(s_zs, 1)

            dve.sem_inc(s_pe, 2)
            weights(0, 0)
            with dve.Fori(0, 3) as i:
                weights(i, 1)
                queries(i, 0)
                weights(i + 1, 0)
                queries(i, 1)
            weights(3, 1)
            queries(3, 0)
            queries(3, 1)

        @block.tensor
        def _(pe):
            pe.sem_inc(s_z, 2)
            with pe.Fori(0, 4) as i:
                for b in range(2):
                    pe.wait_ge(s_lo, 2 * i + b + 3)
                    pe.wait_ge(s_z, 2 * i + b + 1)
                    for n in range(3):
                        for k in range(KD):
                            ins = split_products(pe, acc[b][:, n, 0:CH], ws[b], c.hT, np.s_[:, k, :], np.s_[:, k, n * CH:(n + 1) * CH],
                                                 k == 0, k == KD - 1)
                    ins.then_inc(s_pe, 1)

        @block.scalar
        def _(act):
            with act.Fori(0, 4) as i:
                for b in range(2):
                    act.wait_ge(s_pe, 2 * i + b + 3)
                    act.wait_ge(s_free, 2 * i + b + 1)
                    act.activation(z[b][:, :].rearrange("p (a n) -> p a n", a=3), acc[b][:, :, 0:CH], ACT.Copy, scale=HD ** -0.5)
                    act.activation(c.q_smp[:, b, ds(i, 1), :].rearrange("p a n -> p (a n)"), acc[b][:, 2, CH - NS:CH], ACT.Copy,
                                   scale=HD ** -0.5).then_inc(s_z, 1)

        @block.gpsimd
        def _(pool):
            pool.sem_inc(s_free, 2)
            with pool.Fori(0, 4) as i:
                for b, dst in enumerate(("qfs_d", "qns_d")):
                    pool.wait_ge(s_zs, 2 * i + b + 1)
                    settled(pool, c)
                    for w_ in range(2):
                        pool.dma_start(d[dst][w_].rearrange("h d n -> (h d) n")[ds(i * P, P), :], zs[b][w_][:, :]).then_inc(s_st[b], 16)
                    if b == 1:
                        pool.dma_start(d["qn_d"].rearrange("h d n -> (h d) n")[ds(i * P, P), :], z[b][:, 0:T]).then_inc(s_st[b], 16)
                    pool.wait_ge(s_st[b], (32 + 16 * b) * (i + 1))
                    pool.sem_inc(s_free, 1)


def project_rows(c, w, s_w):
    nc, d = c.nc, c.d
    w_in = d["w_in"][0].rearrange("(k p) n -> p k n", p=P)
    chunks = ROW_CHUNKS
    out = {
        "k_fox": lambda t, n: d["fox_kv_p"][0, 0, t * P:t * P + P, 0, :, :].rearrange("n h d -> n (h d)") if t < NT
        else d["fox_kv_s"][0, :, :, 0, :, :].rearrange("b q h d -> (b q) (h d)"),
        "v_fox": lambda t, n: d["fox_kv_p"][0, 0, t * P:t * P + P, 1, :, :].rearrange("n h d -> n (h d)") if t < NT
        else d["fox_kv_s"][0, :, :, 1, :, :].rearrange("b q h d -> (b q) (h d)"),
        "nsa": lambda t, n: d["nsa_kv_p"][0, 0, t * P:t * P + P].rearrange("n a g d -> n (a g d)") if t < NT
        else d["nsa_kv_s"][0].rearrange("b q a g d -> (b q) (a g d)"),
        "win": lambda t, n: d["win_kv_p"][0, 0, t * P - WIN:t * P - WIN + P].rearrange("n a g d -> n (a g d)") if t < NT
        else d["win_kv_s"][0, :, WIN - NQ:WIN].rearrange("b q a g d -> b q (a g d)"),
    }
    steps = [(ci, t) for ci in range(4) for t in range(9)]
    KP = 2
    PIECES = KD // KP
    blocks_of = {"k_fox": (0, 4), "v_fox": (0, 0), "nsa": (256, 1), "win": (0, 1)}
    tsteps = [s for s, (ci, t) in enumerate(steps) if blocks_of[chunks[ci][0]][1]]

    def stored(s):
        ci, t = steps[s]
        return 1 if chunks[ci][0] != "win" else (t < NT) + (t >= NT - WIN // P)

    def stores(s):
        return sum(stored(m) for m in range(min(s, len(steps))) if m % 3 == s % 3)

    def uses(s):
        return sum(1 for ci, t in steps[:s] if chunks[ci][0] == "win")

    with Phase(nc) as ph:
        ws = [split(ph, f"w_rows_split{i}", [P, KD, 512]) for i in range(2)]
        z = [ph.sb(f"z{i}", [P, 512]) for i in range(3)]
        kt = [split(ph, f"kt{i}", [P, 4, P]) for i in range(2)]
        fl = ph.sb("fl", [P, 9, 4, H])
        bf = ph.sb("bf", [P, H])
        lt = ph.sb("lt", [H, 9, P])
        cum = ph.sb("cum", [H, T])
        acc = [ph.ps(f"z_acc{i}", [P, 512]) for i in range(2)]
        tp = [ph.ps(f"z_tp{i}", [P, 4, P]) for i in range(2)]
        lp = [ph.ps(f"lf_tp{i}", [P, 4, P]) for i in range(3)]
        s_hi = ph.sem("w_rows_rounded")
        s_lo = ph.sem("w_rows_split")
        s_b = ph.sem("b_forget_loaded")
        s_acc = ph.sem("z_products")
        s_z = ph.sem("z_copied")
        s_use = ph.sem("z_kept")
        s_tr = ph.sem("z_transposed")
        s_kh = ph.sem("kt_rounded")
        s_kt = ph.sem("kt_copied")
        s_o = [ph.sem(f"z_stored{i}") for i in range(3)]
        s_ks = [ph.sem(f"kt_stored{i}") for i in range(2)]
        s_lf = ph.sem("logf_steps")
        s_la = ph.sem("logf_table_steps")
        s_lt = ph.sem("logf_transposed")
        s_wc = ph.sem("window_carried")
        s_fo = ph.sem("logf_stored")
        s_gd = ph.sem("gates_stored")
        s_zero = ph.sem("zeroed")
        block = ph.block()

        @block.sync
        def _(sp):
            sp.dma_start(bf[:, :], d["b_forget"][0:1, :].to_broadcast([P, H])).then_inc(s_b, 16)
            sp.dma_start(d["win_kv_s"][0, :, 0:WIN - NQ], d["state_win_kv"][0, :, NQ:WIN]).then_inc(s_wc, 16)
            for ci, (kind, col, n) in enumerate(chunks):
                if ci < 2:
                    continue
                sp.wait_ge(s_lo, PIECES * (ci - 1))
                if kind == "win":
                    sp.dma_start(w[ci % 2][:, :, 0:280], w_in[:, :, C_WIN:C_END]).then_inc(s_w[ci], 16)
                    sp.dma_start(w[ci % 2][:, :, 280:288], w_in[:, :, C_F:C_F + H]).then_inc(s_w[ci], 16)
                else:
                    sp.dma_start(w[ci % 2][:, :, :], w_in[:, :, col:col + n]).then_inc(s_w[ci], 16)
            sp.wait_ge(s_wc, 16)

        @block.tensor
        def _(pe):
            def transposes(n):
                s = tsteps[n]
                ci, t = steps[s]
                c0, nb = blocks_of[chunks[ci][0]]
                rows = ROWS[t]
                pe.wait_ge(s_z, s + 1)
                if n >= 2:
                    pe.wait_ge(s_kt, n - 1)
                for j in range(nb):
                    ins = pe.transpose(tp[n % 2][:, j, 0:rows], z[s % 3][0:rows, c0 + j * P:c0 + (j + 1) * P],
                                       c.ident[0:rows, 0:rows])
                ins.then_inc(s_tr, 1)

            n = 0
            for s, (ci, t) in enumerate(steps):
                rows = ROWS[t]
                width = chunks[ci][2]
                if s >= 2:
                    pe.wait_ge(s_z, s - 1)
                for k in range(KD):
                    if t == 0 and k % KP == 0:
                        pe.wait_ge(s_lo, PIECES * ci + k // KP + 1)
                    ins = split_products(pe, acc[s % 2][0:rows, 0:width], c.hT, ws[ci % 2], np.s_[:, k, t * P:t * P + rows],
                                         np.s_[:, k, 0:width], k == 0, k == KD - 1)
                ins.then_inc(s_acc, 1)
                if n < len(tsteps) and tsteps[n] < s:
                    transposes(n)
                    n += 1
            while n < len(tsteps):
                transposes(n)
                n += 1
            pe.wait_ge(s_lf, 2)
            for t, rows in enumerate(ROWS):
                ins = pe.transpose(lp[t // 4][0:H, t % 4, 0:rows], fl[0:rows, t, 3, :], c.ident[0:rows, 0:rows])
            ins.then_inc(s_lt, 1)

        def width(ci):
            return chunks[ci][2]

        @block.scalar
        def _(act):
            def rounded(ci):
                act.wait_ge(s_w[ci], 32 if ci == 3 else 16)
                if ci >= 2:
                    act.wait_ge(s_acc, 9 * (ci - 1))
                for k in range(0, KD, KP):
                    act.activation(ws[ci % 2][0][:, k:k + KP, 0:width(ci)], w[ci % 2][:, k:k + KP, 0:width(ci)], ACT.Copy).then_inc(s_hi, 1)

            rounded(0)
            for s, (ci, t) in enumerate(steps):
                rows = ROWS[t]
                if t == 1 and ci + 1 < len(chunks):
                    rounded(ci + 1)
                act.wait_ge(s_acc, s + 1)
                if s >= 3:
                    if stores(s):
                        act.wait_ge(s_o[s % 3], 16 * stores(s))
                    if uses(s - 2):
                        act.wait_ge(s_use, uses(s - 2))
                    m = sum(1 for q in tsteps if q <= s - 3)
                    if m:
                        act.wait_ge(s_tr, m)
                act.activation(z[s % 3][0:rows, 0:chunks[ci][2]], acc[s % 2][0:rows, 0:chunks[ci][2]], ACT.Copy).then_inc(s_z, 1)
            act.wait_ge(s_use, uses(len(steps)))
            act.activation(fl[:, :, 1, :], fl[:, :, 0, :], ACT.Abs).then_inc(s_la, 1)
            act.wait_ge(s_la, 1)
            act.activation(fl[:, :, 2, :], fl[:, :, 1, :], ACT.Exp, scale=-1.0).then_inc(s_la, 1)
            act.wait_ge(s_la, 2)
            act.activation(fl[:, :, 1, :], fl[:, :, 2, :], ACT.Ln, bias=1.0).then_inc(s_la, 1)
            act.activation(c.gates[:, :, :], c.gates[:, :, :], ACT.Exp, scale=-1.0).then_inc(s_la, 1)

        def stores_before(n):
            return sum(1 for m in range(n) if m % 2 == n % 2 and steps[tsteps[m]][1] < NT)

        @block.vector
        def _(dve):
            dve.memset(fl[:, NT, :, :], 0.0).then_inc(s_zero, 1)
            dve.memset(c.gates[:, NT, :], 0.0).then_inc(s_zero, 1)
            dve.wait_ge(s_zero, 2)
            n = 0

            def rests(ci):
                for k in range(0, KD, KP):
                    dve.wait_ge(s_hi, PIECES * ci + k // KP + 1)
                    dve.tensor_tensor(ws[ci % 2][1][:, k:k + KP, 0:width(ci)], w[ci % 2][:, k:k + KP, 0:width(ci)],
                                      ws[ci % 2][0][:, k:k + KP, 0:width(ci)], ALU.subtract).then_inc(s_lo, 1)

            rests(0)

            def key_copies(n):
                s = tsteps[n]
                ci, t = steps[s]
                kind = chunks[ci][0]
                rows, nb = ROWS[t], blocks_of[kind][1]
                dve.wait_ge(s_tr, n + 1)
                if t < NT:
                    if n >= 2:
                        dve.wait_ge(s_ks[n % 2], 32 * stores_before(n))
                    dve.tensor_copy(kt[n % 2][0][:, 0:nb, :], tp[n % 2][:, 0:nb, :]).then_inc(s_kh, 1)
                    dve.wait_ge(s_kh, sum(1 for m in tsteps[:n + 1] if steps[m][1] < NT))
                    dve.tensor_tensor(kt[n % 2][1][:, 0:nb, :], tp[n % 2][:, 0:nb, :], kt[n % 2][0][:, 0:nb, :],
                                      ALU.subtract).then_inc(s_kt, 1)
                else:
                    dst = {"k_fox": c.kf_new[:, :, :], "nsa": c.ks_new[:, :, :], "win": c.kw_new[:, :, :]}[kind]
                    dve.tensor_copy(dst, tp[n % 2][:, 0:nb, 0:rows]).then_inc(s_kt, 1)

            for s, (ci, t) in enumerate(steps):
                kind = chunks[ci][0]
                rows = ROWS[t]
                zz = z[s % 3]
                if t == 2 and ci + 1 < len(chunks):
                    rests(ci + 1)
                if kind == "win":
                    dve.wait_ge(s_z, s + 1)
                    if t == 0:
                        dve.wait_ge(s_b, 16)
                    dve.tensor_tensor(fl[0:rows, t, 0, :], zz[0:rows, 280:288], bf[0:rows, :], ALU.add)
                    dve.tensor_copy(c.gates[0:rows, t, :], zz[0:rows, 256:280]).then_inc(s_use, 1)
                if n < len(tsteps) and tsteps[n] < s:
                    key_copies(n)
                    n += 1
            while n < len(tsteps):
                key_copies(n)
                n += 1
            dve.wait_ge(s_use, uses(len(steps)))
            dve.wait_ge(s_la, 3)
            dve.tensor_scalar(fl[:, :, 0, :], fl[:, :, 0, :], 0.0, None, ALU.min).then_inc(s_lf, 1)
            dve.wait_ge(s_lf, 1)
            dve.tensor_tensor(fl[:, :, 3, :], fl[:, :, 0, :], fl[:, :, 1, :], ALU.subtract).then_inc(s_lf, 1)
            dve.wait_ge(s_la, 4)
            dve.tensor_scalar(c.gates[:, :, :], c.gates[:, :, :], 1.0, None, ALU.add).then_inc(s_lf, 1)
            dve.wait_ge(s_lf, 3)
            dve.reciprocal(c.gates[:, :, :], c.gates[:, :, :]).then_inc(s_lf, 1)
            dve.wait_ge(s_lt, 1)
            for a in range(2):
                dve.tensor_copy(lt[:, 4 * a:4 * a + 4, :], lp[a][0:H, :, :]).then_inc(s_lf, 1)
            dve.tensor_copy(c.lf_new[:, :], lp[2][0:H, 0, 0:NS]).then_inc(s_lf, 1)
            dve.wait_ge(s_lf, 7)
            dve.tensor_tensor_scan(cum[:, :], c.one[:, :].to_broadcast([H, T]), lt[:, 0:8, :].rearrange("h t n -> h (t n)"), 0.0,
                                   op0=ALU.mult, op1=ALU.add).then_inc(s_lf, 1)
            dve.wait_ge(s_lf, 8)
            dve.tensor_scalar(cum[:, :], cum[:, :], -1.0, None, ALU.mult).then_inc(s_lf, 1)

        @block.gpsimd
        def _(pool):
            def key_store(n):
                s = tsteps[n]
                ci, t = steps[s]
                kind = chunks[ci][0]
                if t >= NT:
                    return
                pool.wait_ge(s_kt, n + 1)
                for w_ in range(2):
                    if kind == "k_fox":
                        dst = d["kf_d"][w_].rearrange("(j s) d n -> (s d) j n", s=2)[:, :, t * P:(t + 1) * P]
                        pool.dma_start(dst, kt[n % 2][w_][:, :, :]).then_inc(s_ks[n % 2], 16)
                    else:
                        dst = d["ks_d" if kind == "nsa" else "kw_d"][w_].rearrange("g d n -> (g d) n")[:, t * P:(t + 1) * P]
                        pool.dma_start(dst, kt[n % 2][w_][:, 0, :]).then_inc(s_ks[n % 2], 16)

            n = 0
            for s, (ci, t) in enumerate(steps):
                kind = chunks[ci][0]
                rows = ROWS[t]
                pool.wait_ge(s_z, s + 1)
                if kind == "win" and t < NT:
                    pool.dma_start(d["vw_d"][t * P:(t + 1) * P, :], z[s % 3][:, P:2 * P]).then_inc(s_o[s % 3], 16)
                if kind != "win" or t >= NT - WIN // P:
                    width = 256 if kind == "win" else 512
                    pool.dma_start(out[kind](t, width), z[s % 3][0:rows, 0:width]).then_inc(s_o[s % 3], 16)
                if n < len(tsteps) and tsteps[n] < s:
                    key_store(n)
                    n += 1
            while n < len(tsteps):
                key_store(n)
                n += 1
            pool.wait_ge(s_lf, 2)
            pool.dma_start(d["logf_p"][0, 0].rearrange("(t p) h -> p t h", p=P), fl[:, 0:NT, 3, :]).then_inc(s_fo, 16)
            pool.dma_start(d["logf_s"][0].rearrange("b q h -> (b q) h"), fl[0:NS, NT, 3, :]).then_inc(s_fo, 16)
            pool.wait_ge(s_lf, 4)
            pool.dma_start(d["gs_d"], c.gates[0:NS, NT, :]).then_inc(s_gd, 16)
            pool.wait_ge(s_lf, 9)
            pool.dma_start(d["nc_d"], cum[:, :]).then_inc(s_fo, 16)
            for i in range(3):
                pool.wait_ge(s_o[i], 16 * stores(len(steps) + i))
            for i in range(2):
                pool.wait_ge(s_ks[i], 32 * sum(1 for m, s in enumerate(tsteps) if m % 2 == i and steps[s][1] < NT))
            pool.wait_ge(s_fo, 48)
            pool.wait_ge(s_gd, 16)


def misc(c, name, rows, a=None, b=None):
    lo, hi = MISC[name]
    return c.misc[0:rows, lo if a is None else lo + a:hi if b is None else lo + b]


def compress_products(pe, c, xt, hid):
    for k in range(2):
        for a in range(2):
            for j in range(16):
                rhs = xt[:, 2 * k:2 * k + 2, j:j + 8 * (NC - 1) + 1:8]
                ins = pe.matmul(hid[:, (2 * k + a) * 2 * NC:(2 * k + a + 1) * 2 * NC].rearrange("p (g n) -> p g n", g=2),
                                c.w1[:, k, j, a * P:(a + 1) * P], rhs, start=(j == 0), stop=(j == 15))
    return ins


def compress_outputs(pe, c, hs, kc_ps, vc_ps):
    for g in range(G):
        for a in range(2):
            pe.matmul(kc_ps[g * HD:(g + 1) * HD, 0:NC], c.w2[:, 0, a, :], hs[:, a, g * NC:(g + 1) * NC],
                      start=(a == 0), stop=(a == 1))
    for g in range(G):
        for a in range(2):
            ins = pe.matmul(vc_ps[0:NC, g * HD:(g + 1) * HD], hs[:, 2 + a, g * NC:(g + 1) * NC], c.w2[:, 1, a, :],
                            start=(a == 0), stop=(a == 1))
    return ins


class SamplePages:

    def __init__(self, c, ph):
        self.c = c
        self.kv = [ph.sb(f"fox_pages{i}", [P, PAGES, 2 * H * HD]) for i in range(2)]
        self.lf = [ph.sb(f"logf_pages{i}", [P, PAGES, H]) for i in range(2)]
        self.nc_ = [ph.sb(f"cmp_pages{i}", [P, PAGES // 2, 4, 2, HD]) for i in range(2)]
        self.ns = [ph.sb(f"sel_pages{i}", [P, PAGES // 2, 2, 256]) for i in range(2)]
        self.wn = [ph.sb(f"window{i}", [P, 4, 256]) for i in range(2)]
        self.vfn = [ph.sb(f"vf_new{i}", [NQ, H * HD]) for i in range(2)]
        self.vsn = [ph.sb(f"vs_new{i}", [NQ, 2, G * HD]) for i in range(2)]
        self.s_kv = [ph.sem(f"fox_pages_loaded{i}") for i in range(2)]
        self.s_ns = [ph.sem(f"nsa_pages_loaded{i}") for i in range(2)]
        self.s_wn = [ph.sem(f"window_loaded{i}") for i in range(2)]

    def load(self, sp, i, u):
        d, b = self.c.d, 2 * i + u
        for p in range(PAGES):
            v = sp.value_load(self.c.pt[0:1, ds(i * (2 * PAGES) + (u * PAGES + p), 1)], min_val=0,
                              max_val=d["cache_fox_kv"].shape[1] - 1)
            sp.dma_start(self.kv[u][:, p, :], d["cache_fox_kv"][0, ds(v, 1)].rearrange("a n w h e -> n (a w h e)")).then_inc(self.s_kv[u], 16)
            sp.dma_start(self.lf[u][:, p, :], d["cache_fox_logf"][0, ds(v, 1)].rearrange("a n h -> n (a h)")).then_inc(self.s_kv[u], 16)
            half = slice((p % 2) * 64, (p % 2) * 64 + 64)
            rows = d["cache_nsa_kv"][0, ds(v, 1)].rearrange("a (n r) w g e -> (a n) r (w g e)", r=2)
            for r in range(2):
                sp.dma_start(self.nc_[u][half, p // 2, :, r, :], rows[:, r, 0:256].rearrange("n (w e) -> n w e", e=HD)).then_inc(self.s_ns[u], 16)
            sp.dma_start(self.ns[u][half, p // 2, :, :], rows[:, :, 256:512]).then_inc(self.s_ns[u], 16)
        sp.dma_start(self.wn[u][:, :, :], d["state_win_kv"][0, ds(b, 1)].rearrange("a (t n) w g e -> n (a t) (w g e)", n=P)).then_inc(self.s_wn[u], 16)
        sp.dma_start(self.vfn[u][:, :], d["fox_kv_s"][0, ds(b, 1), :, 1].rearrange("a q h e -> (a q) (h e)")).then_inc(self.s_wn[u], 16)
        sp.dma_start(self.vsn[u][:, 0, :], d["nsa_kv_s"][0, ds(b, 1), :, 3].rearrange("a q g e -> (a q) (g e)")).then_inc(self.s_wn[u], 16)
        sp.dma_start(self.vsn[u][:, 1, :], d["win_kv_s"][0, ds(b, 1), WIN - NQ:WIN, 1].rearrange("a q g e -> (a q) (g e)")).then_inc(self.s_wn[u], 16)


def sample_attention(c, pages):
    nc, d = c.nc, c.d
    with Phase(nc) as ph:
        kv, lf, nc_, ns, wn, vfn, vsn = pages.kv, pages.lf, pages.nc_, pages.ns, pages.wn, pages.vfn, pages.vsn
        qbd = ph.sb("q_fox_blocks", [P, NB, 4, HQ])
        qnd = ph.sb("q_nsa_blocks", [P, NB, HQ])
        qb = ph.sb("q_fox_now", [P, 4, HQ])
        qn = ph.sb("q_nsa_now", [P, HQ])
        gt = ph.sb("gates_hq", [HQ, NB, 3])
        kT = ph.sb("k_fox_T", [P, 4, T])
        ksT = ph.sb("k_sel_T", [P, T])
        kwT = ph.sb("k_win_T", [P, WIN])
        xt = ph.sb("cmp_rows_T", [P, 4, 512])
        hs = ph.sb("cmp_hidden", [P, 4, 2 * NC])
        kcT = ph.sb("kc_T", [P, NC])
        vc = ph.sb("vc", [NC, G * HD])
        cum = ph.sb("cum_s", [H, T + NQ])
        pr = ph.sb("probs", [HQ, T + NQ])
        pc = ph.sb("probs_cmp", [HQ, NC])
        sc = ph.sb("scores_cmp", [HQ, NC])
        pT = ph.sb("probs_T", [P, PAGES * HQ])
        pTn = ph.sb("probs_T_new", [NQ, HQ])
        pcT = ph.sb("probs_cmp_T", [NC, HQ])
        blk = ph.sb("blk", [HQ, NSEL])
        sel = ph.sb("sel", [HQ, 4, 14])
        pen = ph.sb("penalty", [HQ, 16])
        ofo = ph.sb("o_fox_s", [HQ, HD])
        on = ph.sb("o_nsa_wide", [HQ, G * HD])
        ono = ph.sb("o_nsa_s", [HQ, HD])
        sm = ph.sb("small", [HQ, 20])
        tr = [ph.ps(f"tr{i}", [P, 512]) for i in range(2)]
        S = ph.ps("s_ps", [P, 3 * 512])
        PT = ph.ps("pt_ps", [P, 512])
        O = ph.ps("o_ps", [P, 512])
        M = ph.ps("m_ps", [P, 512])
        s_init = ph.sem("queries_spread")
        s_initd = ph.sem("small_rows_loaded")
        s_kv, s_ns, s_wn = pages.s_kv, pages.s_ns, pages.s_wn
        s_tr = ph.sem("group_transposed")
        s_tc = [ph.sem(f"group_copied{bank}") for bank in range(2)]
        s_dve = ph.sem("dve_chain")
        s_fs = ph.sem("o_fox_stored")
        s_nst = ph.sem("o_nsa_stored")
        s_ff = ph.sem("o_fox_free")
        s_nf = ph.sem("o_nsa_free")
        once = {n: ph.sem(n) for n in (
            "q_staged", "lf_transposed", "cum_ready", "f_scores", "f_max", "f_probs", "f_probs_turned", "f_pT", "f_values",
            "f_read", "f_out", "hidden", "gelu", "kc_products", "kc_copied", "c_scores", "c_read", "c_max", "c_exp", "c_probs",
            "c_probs_turned", "c_pT", "c_values", "slc_heads", "slc_copied", "slc_sums", "s_scores", "s_max", "s_probs",
            "s_probs_turned", "s_pT", "s_values", "w_scores", "w_max", "w_probs", "w_probs_turned", "w_pT", "w_values",
            "n_read", "n_out")}
        block = ph.block()
        os_v = d["os_d"].rearrange("(b q) (w h e) -> b w h q e", q=NQ, w=2, h=H)

        def waits(eng, b):
            return (lambda n: eng.wait_ge(once[n], b + 3)), (lambda n: eng.wait_ge(once[n], b + 2))

        def start(eng, names):
            for n in names.split():
                eng.sem_inc(once[n], 2)

        @block.sync
        def _(sp):
            for br in range(3):
                for h in range(H):
                    sp.dma_start(gt[h * NQ:(h + 1) * NQ, :, br:br + 1],
                                 d["gs_d"].rearrange("(b q) n -> q b n", q=NQ)[:, :, br * H + h:br * H + h + 1]).then_inc(s_initd, 16)
            pages.load(sp, 0, 1)
            with sp.Fori(0, NB // 2 - 1) as i:
                for u in range(2):
                    sp.wait_ge(once["w_values"], 2 * i + u + 3)
                    settled(sp, c)
                    pages.load(sp, i + 1, u)

        NG = 15

        def group_blocks(u, m):
            if m < 8:
                return [kv[u][:, m, j * P:(j + 1) * P] for j in range(4)]
            if m < 12:
                return [nc_[u][:, m - 8, j, :, :].rearrange("p r e -> p (r e)") for j in range(4)]
            if m < 14:
                return [ns[u][:, 2 * (m - 12) + j // 2, j % 2, 0:128] for j in range(4)]
            return [wn[u][:, j, 0:P] for j in range(4)]

        def before(u, m, bank):
            return sum(1 for v in range(2) for n in range(NG) if (v, n) < (u, m) and (v + n) % 2 == bank)

        def group_target(m):
            if m < 8:
                return kT[:, :, m * P:(m + 1) * P]
            if m < 12:
                return xt[:, :, (m - 8) * P:(m - 7) * P]
            if m < 14:
                return ksT[:, (m - 12) * 512:(m - 11) * 512].rearrange("p (j m) -> p j m", j=4)
            return kwT[:, :].rearrange("p (j m) -> p j m", j=4)

        @block.tensor
        def _(pe):
            start(pe, "lf_transposed f_scores f_probs_turned f_values hidden kc_products c_scores c_probs_turned c_values "
                      "slc_heads slc_sums s_scores s_probs_turned s_values w_scores w_probs_turned w_values")
            for bank in range(2):
                pe.sem_inc(s_tc[bank], 1)
            pe.wait_ge(s_init, 18)
            with pe.Fori(0, NB // 2) as i:
                for u in range(2):
                    b = 2 * i + u
                    now, prev = waits(pe, b)

                    def group(m):
                        bank = (u + m) % 2
                        pe.wait_ge(s_tc[bank], i * NG + before(u, m, bank) + 1)
                        for j, src in enumerate(group_blocks(u, m)):
                            ins = pe.transpose(tr[(u + m) % 2][:, j * P:(j + 1) * P], src, c.ident[:, :])
                        ins.then_inc(s_tr, 1)

                    def copied(m):
                        for bank in range(2):
                            pe.wait_ge(s_tc[bank], i * NG + before(u, m + 1, bank) + 1)

                    def turn(src, tiles, name):
                        settled(pe, c)
                        for p in range(tiles):
                            pe.transpose(PT[:, p * HQ:(p + 1) * HQ], pr[:, p * P:(p + 1) * P], c.ident[0:HQ, 0:HQ])
                        pe.transpose(PT[0:NQ, 256:256 + HQ], pr[:, tiles * P:tiles * P + NQ],
                                     c.ident[0:HQ, 0:HQ]).then_inc(once[name], 1)

                    pe.wait_ge(s_kv[u], i * (2 * PAGES * 16) + 2 * PAGES * 16)
                    prev("w_probs")
                    for p in range(PAGES):
                        ins = pe.transpose(S[0:H, p * P:(p + 1) * P], lf[u][:, p, :], c.ident[:, :])
                    ins.then_inc(once["lf_transposed"], 1)
                    for m in range(8):
                        group(m)
                    pe.wait_ge(s_ns[u], i * (3 * PAGES * 16) + 3 * PAGES * 16)
                    pe.wait_ge(s_wn[u], i * 64 + 64)
                    for m in range(8, 12):
                        group(m)
                    now("q_staged")
                    now("cum_ready")
                    copied(7)
                    for n in range(2):
                        cols = slice(n * 512, (n + 1) * 512)
                        for j in range(4):
                            pe.matmul(S[0:HQ, cols], qb[:, j, :], kT[:, j, cols], start=(j == 0), stop=False)
                        pe.matmul(S[0:HQ, cols], misc(c, "neg_head", H), cum[:, cols], start=False, stop=True)
                    for j in range(4):
                        pe.matmul(S[0:HQ, T:T + NQ], qb[:, j, :], c.kf_new[:, j, ds(b * NQ, NQ)], start=(j == 0), stop=False)
                    pe.matmul(S[0:HQ, T:T + NQ], misc(c, "neg_head", H), cum[:, T:T + NQ],
                              start=False, stop=True).then_inc(once["f_scores"], 1)
                    copied(11)
                    prev("n_read")
                    compress_products(pe, c, xt, M).then_inc(once["hidden"], 1)
                    for m in range(12, 15):
                        group(m)
                    now("f_probs")
                    prev("w_pT")
                    turn(pr, PAGES, "f_probs_turned")
                    now("gelu")
                    prev("f_read")
                    compress_outputs(pe, c, hs, O[:, 0:P], O[:, P:2 * P]).then_inc(once["kc_products"], 1)
                    now("kc_copied")
                    pe.matmul(O[0:HQ, 256:256 + NC], qn[:, :], kcT[:, :], start=True, stop=True).then_inc(once["c_scores"], 1)
                    now("f_pT")
                    now("c_read")

                    def fox_values(p0, p1):
                        for p in range(p0, p1):
                            pe.matmul(O[0:HQ, :], pT[:, p * HQ:(p + 1) * HQ], kv[u][:, p, 512:1024], start=(p == 0), stop=False)

                    fox_values(0, 2)
                    now("c_probs")
                    settled(pe, c)
                    pe.transpose(PT[0:NC, 0:HQ], pc[:, :], c.ident[0:HQ, 0:HQ]).then_inc(once["c_probs_turned"], 1)
                    copied(13)
                    for n in range(2):
                        cols = slice(n * 512, (n + 1) * 512)
                        pe.matmul(S[0:HQ, cols], qn[:, :], ksT[:, cols], start=True, stop=True)
                    pe.matmul(S[0:HQ, T:T + NQ], qn[:, :], c.ks_new[:, 0, ds(b * NQ, NQ)],
                              start=True, stop=True).then_inc(once["s_scores"], 1)
                    now("c_pT")
                    settled(pe, c)
                    pe.matmul(PT[0:HQ, 0:NSEL], pcT[:, :], misc(c, "to_sel", NC), start=True, stop=True).then_inc(once["slc_heads"], 1)
                    pe.matmul(M[0:HQ, 0:G * HD], pcT[:, :], vc[:, :], start=True, stop=True).then_inc(once["c_values"], 1)
                    fox_values(2, 3)
                    now("slc_copied")
                    settled(pe, c)
                    pe.matmul(PT[0:HQ, 0:NSEL], misc(c, "group_sum", HQ), blk[:, :], start=True, stop=True).then_inc(once["slc_sums"], 1)
                    fox_values(3, PAGES)
                    pe.matmul(O[0:HQ, :], pTn[:, :], vfn[u][:, :], start=False, stop=True).then_inc(once["f_values"], 1)
                    now("s_probs")
                    turn(pr, PAGES, "s_probs_turned")
                    copied(14)
                    pe.matmul(S[0:HQ, 0:WIN], qn[:, :], kwT[:, :], start=True, stop=True)
                    pe.matmul(S[0:HQ, WIN:WIN + NQ], qn[:, :], c.kw_new[:, 0, ds(b * NQ, NQ)],
                              start=True, stop=True).then_inc(once["w_scores"], 1)
                    now("s_pT")
                    for p in range(PAGES):
                        pe.matmul(M[0:HQ, 128:256], pT[:, p * HQ:(p + 1) * HQ], ns[u][:, p // 2, p % 2, 128:256],
                                  start=(p == 0), stop=False)
                    pe.matmul(M[0:HQ, 128:256], pTn[:, :], vsn[u][:, 0, :], start=False, stop=True).then_inc(once["s_values"], 1)
                    now("w_probs")
                    turn(pr, WIN // P, "w_probs_turned")
                    now("w_pT")
                    for p in range(WIN // P):
                        pe.matmul(M[0:HQ, 256:384], pT[:, p * HQ:(p + 1) * HQ], wn[u][:, p, P:2 * P], start=(p == 0), stop=False)
                    pe.matmul(M[0:HQ, 256:384], pTn[:, :], vsn[u][:, 1, :], start=False, stop=True).then_inc(once["w_values"], 1)

        @block.scalar
        def _(act):
            start(act, "f_probs gelu f_pT c_exp s_probs s_pT w_probs w_pT")
            with act.Fori(0, NB // 2) as i:
                for u in range(2):
                    b = 2 * i + u
                    now, prev = waits(act, b)

                    def probs(name, out, src, col):
                        now(f"{name}_max")
                        act.activation(out, src, ACT.Exp, bias=sm[:, col:col + 1], accum_out=sm[:, col + 1:col + 2])\
                           .then_inc(once[{"c": "c_exp"}.get(name, f"{name}_probs")], 1)

                    def turned(name, before):
                        now(f"{name}_probs_turned")
                        before()
                        n = (WIN // P if name == "w" else PAGES) * HQ
                        act.activation(pT[:, 0:n], PT[:, 0:n], ACT.Copy)
                        act.activation(pTn[:, :], PT[0:NQ, 256:256 + HQ], ACT.Copy).then_inc(once[f"{name}_pT"], 1)

                    def copy_groups(ms):
                        for m in ms:
                            if (u + m) % 2 == 1:
                                act.wait_ge(s_tr, b * NG + m + 1)
                                act.activation(group_target(m), tr[1][:, :].rearrange("p (j m) -> p j m", j=4), ACT.Copy).then_inc(s_tc[1], 1)

                    prev("f_scores")
                    copy_groups(range(8))
                    prev("hidden")
                    copy_groups(range(8, 12))
                    prev("w_probs_turned")
                    probs("f", pr[:, :], S[0:HQ, 0:T + NQ], 0)
                    now("hidden")
                    prev("kc_products")
                    for k in range(4):
                        ins = act.activation(hs[:, k, :], M[:, k * 2 * NC:(k + 1) * 2 * NC], ACT.Gelu_apprx_tanh,
                                             bias=c.b1[:, k // 2, k % 2:k % 2 + 1])
                    ins.then_inc(once["gelu"], 1)
                    prev("w_scores")
                    copy_groups(range(12, 15))
                    turned("f", lambda: prev("w_values"))
                    probs("c", pc[:, :], sc[:, :], 3)
                    probs("s", pr[:, :], S[0:HQ, 0:T + NQ], 6)
                    turned("s", lambda: now("f_values"))
                    probs("w", pr[:, 0:WIN + NQ], S[0:HQ, 0:WIN + NQ], 9)
                    turned("w", lambda: now("s_values"))

        @block.vector
        def _(dve):
            start(dve, "q_staged cum_ready f_max f_read f_out kc_copied c_read c_max c_probs c_pT slc_copied s_max w_max "
                       "n_read n_out")
            dve.memset(qbd[:, :, :, :], 0.0).then_inc(s_init, 1)
            dve.memset(qnd[:, :, :], 0.0).then_inc(s_init, 1)
            dve.wait_ge(s_init, 2)
            for h in range(H):
                j, s, g = h // 2, h % 2, h // GH
                q_of = lambda k: c.q_smp[s * HD:(s + 1) * HD, k, j, :].rearrange("p (b q) -> p b q", q=NQ)
                dve.tensor_copy(qbd[s * HD:(s + 1) * HD, :, j, h * NQ:(h + 1) * NQ], q_of(0)).then_inc(s_init, 1)
                dve.tensor_copy(qnd[g * HD:(g + 1) * HD, :, h * NQ:(h + 1) * NQ], q_of(1)).then_inc(s_init, 1)
            dve.wait_ge(s_init, 18)
            chain = Chain(dve, s_dve)
            chain(dve.memset(pen[:, :], 0.0))
            chain.done, chain.k = 1, 0
            dve.wait_ge(s_initd, 16 * 24)
            with dve.Fori(0, NB // 2) as i:
                chain.enter(i, 2 * PER_SEQ)
                for u in range(2):
                    b = 2 * i + u
                    now, prev = waits(dve, b)
                    k0 = chain.k

                    def copy_group(m):
                        if (u + m) % 2 == 0:
                            dve.wait_ge(s_tr, b * NG + m + 1)
                            dve.tensor_copy(group_target(m), tr[0][:, :].rearrange("p (j m) -> p j m", j=4)).then_inc(s_tc[0], 1)

                    prev("f_scores")
                    dve.tensor_copy(qb[:, :, :], qbd[:, ds(b, 1), :, :].rearrange("p a j n -> p (a j) n"))
                    prev("w_scores")
                    dve.tensor_copy(qn[:, :], qnd[:, ds(b, 1), :].rearrange("p a n -> p (a n)")).then_inc(once["q_staged"], 1)
                    now("lf_transposed")
                    chain(dve.tensor_tensor_scan(cum[:, 0:T], c.one[:, :].to_broadcast([H, T]), S[0:H, 0:T], 0.0, op0=ALU.mult, op1=ALU.add))
                    dve.tensor_tensor_scan(cum[:, T:T + NQ], c.one[:, :].to_broadcast([H, NQ]), c.lf_new[:, ds(b * NQ, NQ)],
                                           cum[:, T - 1:T], op0=ALU.mult, op1=ALU.add).then_inc(once["cum_ready"], 1)
                    for m in range(8):
                        copy_group(m)
                    prev("hidden")
                    for m in range(8, 12):
                        copy_group(m)
                    now("f_scores")
                    chain(dve.tensor_tensor(S[0:HQ, T:T + NQ], S[0:HQ, T:T + NQ], misc(c, "causal_new", HQ), ALU.add))
                    dve.tensor_reduce(sm[:, 0:1], S[0:HQ, 0:T + NQ], AX, ALU.max, negate=True).then_inc(once["f_max"], 1)
                    prev("s_scores")
                    for m in range(12, 15):
                        copy_group(m)
                    now("kc_products")
                    dve.tensor_copy(kcT[:, :], O[:, 0:NC])
                    prev("c_values")
                    dve.tensor_copy(vc[:, :], O[0:NC, P:2 * P]).then_inc(once["kc_copied"], 1)
                    now("c_scores")
                    dve.tensor_tensor(sc[:, :], O[0:HQ, 256:256 + NC], c.bias_s[:, 388:451], ALU.add).then_inc(once["c_read"], 1)
                    now("c_read")
                    dve.tensor_reduce(sm[:, 3:4], sc[:, :], AX, ALU.max, negate=True).then_inc(once["c_max"], 1)
                    now("c_exp")
                    chain(dve.reciprocal(sm[:, 5:6], sm[:, 4:5]))
                    dve.tensor_scalar(pc[:, :], pc[:, :], sm[:, 5:6], None, ALU.mult).then_inc(once["c_probs"], 1)
                    now("c_probs_turned")
                    prev("c_values")
                    dve.tensor_copy(pcT[:, :], PT[0:NC, 0:HQ]).then_inc(once["c_pT"], 1)
                    now("slc_heads")
                    dve.tensor_copy(blk[:, :], PT[0:HQ, 0:NSEL]).then_inc(once["slc_copied"], 1)
                    now("slc_sums")
                    chain(dve.tensor_copy(sel[:, 0, :], PT[0:HQ, 1:15]))
                    chain(dve.tensor_reduce(sm[:, 12:13], sel[:, 0, :], AX, ALU.min))
                    chain(dve.tensor_scalar(sel[:, 1, :], sel[:, 0, :], sm[:, 12:13], None, ALU.is_equal))
                    chain(dve.tensor_tensor(sel[:, 2, :], sel[:, 1, :], misc(c, "block_no", HQ), ALU.mult))
                    chain(dve.tensor_reduce(sm[:, 13:14], sel[:, 2, :], AX, ALU.max))
                    chain(dve.tensor_scalar(pen[:, 1:15], sel[:, 2, :], sm[:, 13:14], NEG, ALU.is_equal, ALU.mult))
                    now("s_scores")
                    chain(dve.tensor_tensor(S[0:HQ, 768:T], S[0:HQ, 768:T], c.bias_s[:, 0:256], ALU.add))
                    dve.tensor_tensor(S[0:HQ, T:T + NQ], S[0:HQ, T:T + NQ], c.bias_s[:, 256:260], ALU.add)
                    for r in range(2):
                        part = S[0:HQ, 0:T].rearrange("p (a r b m) -> p a r b m", a=4, r=2, b=4)[:, :, r, :, :]
                        drop = pen[:, :].rearrange("p (a b c) -> p a b c", a=4, c=1).to_broadcast([HQ, 4, 4, 32])
                        chain(dve.tensor_tensor(part, part, drop, ALU.add))
                    dve.tensor_reduce(sm[:, 6:7], S[0:HQ, 0:T + NQ], AX, ALU.max, negate=True).then_inc(once["s_max"], 1)
                    now("f_values")
                    chain(dve.tensor_tensor(O[0:HQ, :], O[0:HQ, :], misc(c, "own_head", HQ), ALU.mult))
                    dve.wait_ge(s_ff, b + 1)
                    dve.tensor_reduce(ofo[:, :], O[0:HQ, :].rearrange("p (h e) -> p e h", h=H), AX, ALU.add).then_inc(once["f_read"], 1)
                    now("f_read")
                    chain(dve.reciprocal(sm[:, 2:3], sm[:, 1:2]))
                    dve.tensor_scalar(ofo[:, :], ofo[:, :], sm[:, 2:3], None, ALU.mult).then_inc(once["f_out"], 1)
                    now("w_scores")
                    chain(dve.tensor_tensor(S[0:HQ, 0:P], S[0:HQ, 0:P], misc(c, "wmask_s", HQ), ALU.add))
                    chain(dve.tensor_tensor(S[0:HQ, WIN - P:WIN], S[0:HQ, WIN - P:WIN], c.bias_s[:, 260:388], ALU.add))
                    chain(dve.tensor_tensor(S[0:HQ, WIN:WIN + NQ], S[0:HQ, WIN:WIN + NQ], c.bias_s[:, 256:260], ALU.add))
                    dve.tensor_reduce(sm[:, 9:10], S[0:HQ, 0:WIN + NQ], AX, ALU.max, negate=True).then_inc(once["w_max"], 1)
                    now("w_probs")
                    chain(dve.reciprocal(sm[:, 14:15], sm[:, 7:8]))
                    chain(dve.reciprocal(sm[:, 15:16], sm[:, 10:11]))
                    gate = gt[:, ds(b, 1), :].rearrange("p a n -> p (a n)")
                    chain(dve.tensor_tensor(sm[:, 14:16], sm[:, 14:16], gate[:, 1:3], ALU.mult))
                    chain(dve.tensor_copy(sm[:, 16:17], gate[:, 0:1]))
                    now("w_values")
                    chain(dve.tensor_scalar(on[:, :], M[0:HQ, 0:P], sm[:, 16:17], None, ALU.mult))
                    chain(dve.scalar_tensor_tensor(out=on[:, :], in0=M[0:HQ, P:2 * P], scalar=sm[:, 14:15], in1=on[:, :],
                                                   op0=ALU.mult, op1=ALU.add))
                    dve.scalar_tensor_tensor(out=on[:, :], in0=M[0:HQ, 2 * P:3 * P], scalar=sm[:, 15:16], in1=on[:, :],
                                             op0=ALU.mult, op1=ALU.add).then_inc(once["n_read"], 1)
                    now("n_read")
                    dve.wait_ge(s_nf, b + 1)
                    chain(dve.tensor_scalar(ono[:, :], on[:, 0:HD], misc(c, "own_group", HQ, 0, 1), None, ALU.mult))
                    dve.scalar_tensor_tensor(out=ono[:, :], in0=on[:, HD:2 * HD], scalar=misc(c, "own_group", HQ, 1, 2),
                                             in1=ono[:, :], op0=ALU.mult, op1=ALU.add).then_inc(once["n_out"], 1)
                    assert chain.k - k0 == PER_SEQ, chain.k - k0
            chain.leave(NB // 2)

        @block.gpsimd
        def _(pool):
            pool.sem_inc(s_ff, 1)
            pool.sem_inc(s_nf, 1)
            with pool.Fori(0, NB) as b:
                for name, tile, w, sem, free in (("f_out", ofo, 0, s_fs, s_ff), ("n_out", ono, 1, s_nst, s_nf)):
                    pool.wait_ge(once[name], b + 3)
                    settled(pool, c)
                    pool.dma_start(os_v[ds(b, 1), w].rearrange("a h q e -> (a h) q e"), tile[:, :]).then_inc(sem, 16)
                    pool.wait_ge(sem, 16 * b + 16)
                    pool.sem_inc(free, 1)


PER_SEQ = 24


def prompt_compress(c, pages):
    nc, d = c.nc, c.d
    with Phase(nc) as ph:
        rows = ph.sb("pc_rows", [P, 4, 4, 2, HD])
        pos = ph.sb("cmp_pos_sb", [P, 2, 16])
        b1 = ph.sb("cmp_b1_raw", [P, 2, 2])
        xt = ph.sb("pc_rows_T", [P, 4, 512])
        hs = ph.sb("pc_hidden", [P, 4, 2 * NC])
        tr = [ph.ps(f"pc_tr{i}", [P, 512]) for i in range(4)]
        M = ph.ps("pc_hid_ps", [P, 512])
        O = ph.ps("pc_out_ps", [P, 512])
        acc = ph.ps("b1_acc", [P, 4])
        s_rows = ph.sem("pc_rows_loaded")
        s_w = ph.sem("cmp_weights_loaded")
        s_b = ph.sem("pos_products")
        s_b1 = ph.sem("b1_summed")
        s_tr = ph.sem("pc_transposed")
        s_cp = ph.sem("pc_copied")
        s_h = ph.sem("pc_hidden_done")
        s_g = ph.sem("pc_gelu")
        s_o = ph.sem("pc_products")
        s_k = ph.sem("pc_kept")
        block = ph.block()

        @block.sync
        def _(sp):
            src = d["nsa_kv_p"][0, 0].rearrange("(a n r) w g e -> n a r (w g e)", a=4, r=2)
            for a in range(4):
                for r in range(2):
                    sp.dma_start(rows[:, a, :, r, :], src[:, a, r, 0:256].rearrange("n (w e) -> n w e", e=HD)).then_inc(s_rows, 16)
            for k in range(2):
                sp.dma_start(c.w1[:, k, :, :], d["cmp_w1"][0, k].rearrange("(j p) n -> p j n", p=P)).then_inc(s_w, 16)
                sp.dma_start(c.w2[:, k, :, :], d["cmp_w2"][0, k].rearrange("(a p) n -> p a n", p=P)).then_inc(s_w, 16)
                sp.dma_start(pos[:, k, :], d["cmp_pos"][0, k].rearrange("(j r) e -> (r e) j", r=2)).then_inc(s_w, 16)
                sp.dma_start(b1[:, k, :], d["cmp_b1"][0, k].rearrange("(a p) -> p a", p=P)).then_inc(s_w, 16)
            pages.load(sp, 0, 0)

        @block.tensor
        def _(pe):
            pe.wait_ge(s_rows, 16 * 8)
            for a in range(4):
                for j in range(4):
                    ins = pe.transpose(tr[a][:, j * P:(j + 1) * P], rows[:, a, j, :, :].rearrange("p r e -> p (r e)"), c.ident[:, :])
                ins.then_inc(s_tr, 1)
            pe.wait_ge(s_w, 16 * 8)
            for k in range(2):
                for a in range(2):
                    for j in range(16):
                        ins = pe.matmul(acc[:, 2 * k + a:2 * k + a + 1], c.w1[:, k, j, a * P:(a + 1) * P], pos[:, k, j:j + 1],
                                        start=(j == 0), stop=(j == 15))
            ins.then_inc(s_b, 1)
            pe.wait_ge(s_cp, 4)
            compress_products(pe, c, xt, M).then_inc(s_h, 1)
            pe.wait_ge(s_g, 1)
            compress_outputs(pe, c, hs, O[:, 0:P], O[:, P:2 * P]).then_inc(s_o, 1)

        @block.scalar
        def _(act):
            act.wait_ge(s_b1, 1)
            act.wait_ge(s_h, 1)
            for k in range(4):
                ins = act.activation(hs[:, k, :], M[:, k * 2 * NC:(k + 1) * 2 * NC], ACT.Gelu_apprx_tanh,
                                     bias=c.b1[:, k // 2, k % 2:k % 2 + 1])
            ins.then_inc(s_g, 1)

        @block.vector
        def _(dve):
            for a in range(4):
                dve.wait_ge(s_tr, a + 1)
                dve.tensor_copy(xt[:, :, a * P:(a + 1) * P], tr[a][:, :].rearrange("p (j m) -> p j m", j=4)).then_inc(s_cp, 1)
            dve.wait_ge(s_w, 16 * 8)
            dve.wait_ge(s_b, 1)
            dve.tensor_tensor(c.b1[:, :, :].rearrange("p k a -> p (k a)"), acc[:, :], b1[:, :, :].rearrange("p k a -> p (k a)"),
                              ALU.add).then_inc(s_b1, 1)
            dve.wait_ge(s_o, 1)
            dve.tensor_copy(c.kc_p[:, :], O[:, 0:NC]).then_inc(s_k, 1)
            dve.tensor_copy(c.vc_p[:, :], O[0:NC, P:2 * P]).then_inc(s_k, 1)


class AttentionInputs:

    def __init__(self, c, ph):
        kinds = ("fox", "sel", "win")
        self.q = {kind: [ph.sb(f"pa_q_{kind}{u}", [P, T], FR) for u in range(2)] for kind in ("fox", "nsa")}
        self.k = {kind: [[ph.sb(f"pa_k_{kind}{u}{w_}", [P, T], FR) for w_ in range(2)] for u in range(2)] for kind in kinds}
        self.v = {kind: [ph.sb(f"pa_v_{kind}{u}", [P, NT + 1, 2, HD], FR) for u in range(2)] for kind in kinds}
        self.v_raw = [ph.sb(f"pa_v_raw{u}", [P, NT, HD]) for u in range(2)]
        self.g_raw = [ph.sb(f"pa_group_v_raw{n}", [P, NT, HD]) for n in range(2)]
        self.s_fl = [ph.sem(f"pa_fox_loaded{u}") for u in range(2)]
        self.s_nl = [ph.sem(f"pa_nsa_q_loaded{u}") for u in range(2)]
        self.s_kl = [ph.sem(f"pa_group_k_loaded{u}") for u in range(2)]
        self.s_fv = [ph.sem(f"pa_fox_v_loaded{u}") for u in range(2)]
        self.s_gv = [ph.sem(f"pa_group_v_loaded{n}") for n in range(4)]
        self.s_vh = ph.sem("pa_v_rounded")
        self.s_vs = [ph.sem(f"pa_fox_v_split{u}") for u in range(2)]
        self.s_gs = ph.sem("pa_group_v_split")
        self.s_vz = ph.sem("pa_v_tails")

    def load_fox(self, pool, d, h, u):
        for w_ in range(2):
            pool.dma_start(self.q["fox"][u][w_ * HD:(w_ + 1) * HD, :], d["qfs_d"][w_, ds(h, 1)].rearrange("a e n -> (a e) n")).then_inc(self.s_fl[u], 16)
            for r in range(2):
                pool.dma_start(self.k["fox"][u][w_][r * HD:(r + 1) * HD, :], d["kf_d"][w_, ds(h, 1)].rearrange("a e n -> (a e) n")).then_inc(self.s_fl[u], 16)

    def load_nsa(self, pool, d, h, u):
        for w_ in range(2):
            pool.dma_start(self.q["nsa"][u][w_ * HD:(w_ + 1) * HD, :], d["qns_d"][w_, ds(h, 1)].rearrange("a e n -> (a e) n")).then_inc(self.s_nl[u], 16)

    def load_fox_values(self, sp, d, h, u):
        sp.dma_start(self.v_raw[u][:, :, :], d["fox_kv_p"][0, 0, :, 1, ds(h, 1), :].rearrange("(t p) a e -> p t (a e)", p=P)).then_inc(self.s_fv[u], 16)

    def split_values(self, pool, dst, raw, sem, at):
        pool.tensor_copy(dst[:, 0:NT, 0, :], raw[:, :, :]).then_inc(self.s_vh, 1)
        pool.wait_ge(self.s_vh, at)
        pool.tensor_tensor(dst[:, 0:NT, 1, :], raw[:, :, :], dst[:, 0:NT, 0, :], ALU.subtract).then_inc(sem, 1)


def compressed_attention(c, pa):
    nc, d = c.nc, c.d
    with Phase(nc) as ph:
        q = [ph.sb(f"ca_q{i}", [P, GH, P]) for i in range(2)]
        sc = [ph.sb(f"ca_scores{i}", [P, H, NC]) for i in range(2)]
        pT = [ph.sb(f"ca_probs_T{i}", [NC, H, P]) for i in range(2)]
        mx = ph.sb("ca_max", [P, 2, H])
        co = ph.sb("ca_coef", [P, 2, H])
        S = [ph.ps(f"ca_s{i}", [P, G, 512]) for i in range(2)]
        T_ = ph.ps("ca_t", [P, H, P])
        O = [ph.ps(f"ca_o{i}", [P, H, HD]) for i in range(2)]
        s_q = [ph.sem(f"ca_q_loaded{i}") for i in range(2)]
        s_s = ph.sem("ca_scored")
        s_sh = ph.sem("ca_shifted")
        s_e = ph.sem("ca_exps")
        s_t = ph.sem("ca_turned")
        s_c = ph.sem("ca_turned_copied")
        s_o = ph.sem("ca_values")
        s_co = ph.sem("ca_coef_done")
        s_n = ph.sem("ca_out")
        s_ch = ph.sem("ca_chain")
        block = ph.block()
        group = [(kind, u) for u in range(2) for kind in ("sel", "win")]

        @block.gpsimd
        def _(pool):
            for kind in ("fox", "sel", "win"):
                for u in range(2):
                    pool.tensor_copy(pa.v[kind][u][:, NT, :, :].rearrange("p w e -> p (w e)"),
                                     c.zero[:, :].to_broadcast([P, P])).then_inc(pa.s_vz, 1)
            for u in range(2):
                pa.load_fox(pool, d, GH * u, u)
                pa.load_nsa(pool, d, GH * u, u)
                for kind, src in (("sel", "ks_d"), ("win", "kw_d")):
                    for w_ in range(2):
                        for r in range(2):
                            pool.dma_start(pa.k[kind][u][w_][r * HD:(r + 1) * HD, :], d[src][w_, u]).then_inc(pa.s_kl[u], 16)
            for u in range(2):
                pool.wait_ge(pa.s_fv[u], 16)
                pa.split_values(pool, pa.v["fox"][u], pa.v_raw[u], pa.s_vs[u], u + 1)
            for n, (kind, u) in enumerate(group):
                pool.wait_ge(pa.s_gv[n], 16)
                pa.split_values(pool, pa.v[kind][u], pa.g_raw[n % 2], pa.s_gs, n + 3)

        U = 4
        NTURN = NT // U

        @block.sync
        def _(sp):
            sp.sem_inc(s_s, 2)
            with sp.Fori(0, NTURN) as i:
                for u in range(U):
                    t = U * i + u
                    sp.wait_ge(s_s, t + 1)
                    for g in range(G):
                        sp.dma_start(q[u % 2][g * HD:(g + 1) * HD, :, :],
                                     d["qn_d"][g * GH:(g + 1) * GH, :, ds(t * P, P)].rearrange("h e n -> e h n")).then_inc(s_q[u % 2], 16)
            for u in range(2):
                pa.load_fox_values(sp, d, GH * u, u)
            for n, (kind, u) in enumerate(group):
                if n >= 2:
                    sp.wait_ge(pa.s_gs, n - 1)
                src = d["nsa_kv_p"][0, 0, :, 3, u, :] if kind == "sel" else d["vw_d"][:, u * HD:(u + 1) * HD]
                sp.dma_start(pa.g_raw[n % 2][:, :, :], src.rearrange("(t p) e -> p t e", p=P)).then_inc(pa.s_gv[n], 16)

        @block.tensor
        def _(pe):
            pe.sem_inc(s_t, 2)
            pe.sem_inc(s_o, 2)
            with pe.Fori(0, NTURN) as i:
                def scores(u):
                    t = U * i + u
                    pe.wait_ge(s_q[u % 2], 32 * (U // 2) * i + 32 * (u // 2 + 1))
                    pe.wait_ge(s_sh, t + 1)
                    for h in range(H):
                        rows = slice(h // GH * HD, (h // GH + 1) * HD)
                        ins = pe.matmul(S[u % 2][:, h // GH, h % GH * NC:(h % GH + 1) * NC], q[u % 2][rows, h % GH, :], c.kc_p[rows, :],
                                        start=True, stop=True)
                    ins.then_inc(s_s, 1)

                def turn(u):
                    t = U * i + u
                    pe.wait_ge(s_e, t + 1)
                    pe.wait_ge(s_c, t + 1)
                    settled(pe, c)
                    for h in range(H):
                        ins = pe.transpose(T_[0:NC, h, :], sc[u % 2][:, h, :], c.ident[:, :])
                    ins.then_inc(s_t, 1)

                def values(u):
                    t = U * i + u
                    pe.wait_ge(s_c, t + 2)
                    pe.wait_ge(s_n, t + 1)
                    for h in range(H):
                        g = h // GH
                        ins = pe.matmul(O[u % 2][:, h, :], pT[u % 2][:, h, :], c.vc_p[:, g * HD:(g + 1) * HD], start=True, stop=True)
                    ins.then_inc(s_o, 1)

                for x in range(U + 2):
                    if x < U:
                        scores(x)
                    if 0 <= x - 1 < U:
                        turn(x - 1)
                    if 0 <= x - 2 < U:
                        values(x - 2)

        @block.scalar
        def _(act):
            act.sem_inc(s_c, 1)
            with act.Fori(0, NTURN) as i:
                for x in range(U + 1):
                    if x < U:
                        act.wait_ge(s_sh, U * i + x + 3)
                        act.activation(sc[x % 2][:, :, :], sc[x % 2][:, :, :], ACT.Exp).then_inc(s_e, 1)
                    if x >= 1:
                        u = x - 1
                        act.wait_ge(s_t, U * i + u + 3)
                        act.wait_ge(s_o, U * i + u + 1)
                        act.activation(pT[u % 2][:, :, :], T_[0:NC, :, :], ACT.Copy).then_inc(s_c, 1)

        @block.vector
        def _(dve):
            chain = Chain(dve, s_ch)
            dve.sem_inc(s_n, 2)
            dve.sem_inc(s_sh, 2)
            with dve.Fori(0, NTURN) as i:
                chain.enter(i, U * 5)

                def shifted(u):
                    t = U * i + u
                    x = sc[u % 2]
                    dve.wait_ge(s_s, t + 3)
                    dve.wait_ge(s_t, t + 1)
                    grouped = lambda y: y.rearrange("p (g h) n -> p g h n", g=G)
                    chain(dve.tensor_tensor(grouped(x[:, :, :]), S[u % 2][:, :, 0:GH * NC].rearrange("p g (h n) -> p g h n", h=GH),
                                            grouped(c.cb[:, :, ds(56 - 8 * t, NC)]), ALU.add))
                    chain(dve.tensor_reduce(mx[:, u % 2, :], x[:, :, :], AX, ALU.max))
                    dve.tensor_tensor(x[:, :, :], x[:, :, :],
                                      mx[:, u % 2, :].rearrange("p (h a) -> p h a", a=1).to_broadcast([P, H, NC]),
                                      ALU.subtract).then_inc(s_sh, 1)

                def coefficients(u):
                    t = U * i + u
                    cf = co[:, u % 2, :]
                    dve.wait_ge(s_e, t + 1)
                    dve.wait_ge(s_n, t + 1)
                    chain(dve.tensor_reduce(cf, sc[u % 2][:, :, :], AX, ALU.add))
                    chain(dve.reciprocal(cf, cf))
                    chain(dve.tensor_tensor(cf, cf, c.gates[:, ds(t, 1), 0:H].rearrange("p a h -> p (a h)"), ALU.mult))
                    lo = MISC["seen"][0]
                    dve.tensor_tensor(cf, cf, c.misc[:, ds(lo + 8 * t, 8)], ALU.mult).then_inc(s_co, 1)

                def output(u):
                    t = U * i + u
                    dve.wait_ge(s_co, t + 1)
                    dve.wait_ge(s_o, t + 3)
                    dve.tensor_tensor(c.o[:, ds(t, 1), D // 2:D].rearrange("p a (h e) -> p (a h) e", h=H), O[u % 2][:, :, :],
                                      co[:, u % 2, :].rearrange("p (h a) -> p h a", a=1).to_broadcast([P, H, HD]),
                                      ALU.mult).then_inc(s_n, 1)

                for x in range(U + 2):
                    if x < U:
                        shifted(x)
                    if 0 <= x - 1 < U:
                        coefficients(x - 1)
                    if 0 <= x - 2 < U:
                        output(x - 2)
            chain.leave(NTURN)


def prompt_attention(c, pa):
    nc, d = c.nc, c.d
    kinds = ("fox", "sel", "win")
    jobs = [(u, kind) for u in range(2) for kind in kinds]
    units = [(j, t) for j in range(len(jobs)) for t in range(NT)]
    NU = len(units)

    def first_tile(s):
        j, t = units[s]
        return max(0, t - WIN // P) if jobs[j][1] == "win" else 0

    def tiles(s):
        return units[s][1] + 1 - first_tile(s)

    chunks = [(s, a, min(4, tiles(s) - a)) for s in range(NU) for a in range(0, tiles(s), 4)]
    of_unit = [[n for n, ch in enumerate(chunks) if ch[0] == s] for s in range(NU)]
    NCK = len(chunks)

    with Phase(nc) as ph:
        q, k, v = pa.q, pa.k, pa.v
        oj = [ph.sb(f"pa_job_out{i}", [P, NT, HD]) for i in range(2)]
        scaled = ph.sb("pa_job_scaled", [P, NT, HD])
        bias = {kind: [ph.sb(f"pa_bias_{kind}{i}", [P, T]) for i in range(2)] for kind in kinds}
        sc = [ph.sb(f"pa_scores{i}", [P, T]) for i in range(3)]
        pT = [split(ph, f"pa_probs_T{i}", [P, T]) for i in range(2)]
        nm = ph.sb("pa_neg_max", [P, NU])
        sm = ph.sb("pa_sums", [P, NU])
        co = ph.sb("pa_coef", [P, NU])
        S = [ph.ps(f"pa_s{i}", [P, T]) for i in range(2)]
        PT = [ph.ps(f"pa_t{i}", [P, 4 * P]) for i in range(2)]
        O = [ph.ps(f"pa_o{i}", [P, 512]) for i in range(2)]
        s_z = ph.sem("pa_zeroed")
        s_fb = [ph.sem(f"pa_fox_bias_loaded{u}") for u in range(2)]
        s_nb = [ph.sem(f"pa_nsa_bias_loaded{u}") for u in range(2)]
        s_s = ph.sem("pa_scored")
        s_m = ph.sem("pa_biased")
        s_e = ph.sem("pa_exps")
        s_t = ph.sem("pa_turned")
        s_ca = ph.sem("pa_copied_act")
        s_cd = ph.sem("pa_copied_dve")
        s_o = ph.sem("pa_values")
        s_n = ph.sem("pa_out")
        s_co = ph.sem("pa_coef_done")
        s_mg = ph.sem("pa_merged")
        s_mc = ph.sem("pa_merge_scaled")
        s_ch = ph.sem("pa_chain")
        block = ph.block()

        def fox_free(eng, i, u):
            eng.wait_ge(s_o, i * NU + (3 * u + 1) * NT + 1)
            settled(eng, c)

        def nsa_free(eng, i, u):
            eng.wait_ge(s_o, i * NU + (3 * u + 3) * NT + 1)
            settled(eng, c)

        @block.sync
        def _(sp):
            def fox_bias(h, u):
                sp.dma_start(bias["fox"][u][:, :], d["nc_d"][ds(h, 1), :].to_broadcast([P, T])).then_inc(s_fb[u], 16)

            def nsa_bias(h, u):
                for kind in ("sel", "win"):
                    sp.dma_start(bias[kind][u][:, T - 256:T], d["tb_d"][ds(h, 1)].rearrange("a p n -> (a p) n")).then_inc(s_nb[u], 16)

            for u in range(2):
                fox_bias(GH * u, u)
                nsa_bias(GH * u, u)
            with sp.Fori(0, 3) as i:
                for u in range(2):
                    h = i + GH * u + 1
                    fox_free(sp, i, u)
                    pa.load_fox_values(sp, d, h, u)
                    fox_bias(h, u)
                    nsa_free(sp, i, u)
                    nsa_bias(h, u)

        @block.gpsimd
        def _(pool):
            for u in range(2):
                pool.memset(bias["sel"][u][:, 0:T - 256], 0.0).then_inc(s_z, 1)
                pool.memset(bias["win"][u][:, 512:T - 256], 0.0)
                pool.tensor_copy(bias["win"][u][:, 384:512], misc(c, "wmask", P)).then_inc(s_z, 1)
            pool.sem_inc(s_mg, 2)
            pool.sem_inc(s_mc, 1)

            def turn(i, last):
                for j, (u, kind) in enumerate(jobs):
                    h = i + GH * u
                    pool.wait_ge(s_mg, 6 * i + j + 2)
                    pool.wait_ge(s_co, 6 * i + j + 1)
                    settled(pool, c)
                    coef = co[:, j * NT:(j + 1) * NT].rearrange("p (t a) -> p t a", a=1).to_broadcast([P, NT, HD])
                    if kind == "fox":
                        pool.tensor_tensor(c.o[:, :, ds(h * HD, HD)], oj[j % 2][:, :, :], coef, ALU.mult).then_inc(s_mg, 1)
                    else:
                        dst = c.o[:, :, ds(h * HD + D // 2, HD)]
                        pool.tensor_tensor(scaled[:, :, :], oj[j % 2][:, :, :], coef, ALU.mult).then_inc(s_mc, 1)
                        pool.wait_ge(s_mc, 4 * i + (2 * u + (kind == "win")) + 2)
                        settled(pool, c)
                        pool.tensor_tensor(dst, dst, scaled[:, :, :], ALU.add).then_inc(s_mg, 1)
                    if last:
                        continue
                    if kind == "fox":
                        fox_free(pool, i, u)
                        pa.load_fox(pool, d, h + 1, u)
                    if kind == "sel":
                        pool.wait_ge(pa.s_fv[u], 16 * i + 32)
                        settled(pool, c)
                        pa.split_values(pool, v["fox"][u], pa.v_raw[u], pa.s_vs[u], 2 * i + u + 7)
                    if kind == "win":
                        nsa_free(pool, i, u)
                        pa.load_nsa(pool, d, h + 1, u)

            with pool.Fori(0, 3) as i:
                turn(i, False)
            turn(3, True)

        @block.tensor
        def _(pe):
            pe.sem_inc(s_t, 1)
            pe.sem_inc(s_o, 1)
            pe.wait_ge(pa.s_vz, 6)
            with pe.Fori(0, 4) as i:
                def scores(s):
                    j, t = units[s]
                    u, kind = jobs[j]
                    n = tiles(s) * P
                    if t == 0 and kind == "fox":
                        pe.wait_ge(pa.s_fl[u], 96 * i + 96)
                    if t == 0 and kind == "sel":
                        pe.wait_ge(pa.s_nl[u], 32 * i + 32)
                        pe.wait_ge(pa.s_kl[u], 16 * 8)
                    pe.wait_ge(s_m, i * NU + max(0, s - 1) + 1)
                    k0 = first_tile(s) * P
                    fox = kind == "fox"
                    qq = q["fox" if fox else "nsa"][u]
                    for a in range(0, n, 512):
                        m = min(512, (n - a + 255) // 256 * 256, T - k0 - a)
                        last = a + 512 >= n
                        for w_ in range(2):
                            ins = pe.matmul(S[s % 2][:, a:a + m], qq[:, t * P:(t + 1) * P], k[kind][u][w_][:, k0 + a:k0 + a + m],
                                            start=(w_ == 0), stop=(w_ == 1) and not (fox and last), skip_group_check=fox)
                    if fox:
                        ins = pe.matmul(S[s % 2][:, n - P:n], c.ident16[:, :], c.causal16[:, :], start=False, stop=True,
                                        skip_group_check=True)
                    ins.then_inc(s_s, 1)

                def turn(s):
                    pe.wait_ge(s_e, i * NU + s + 1)
                    for n in of_unit[s]:
                        if n >= 2:
                            pe.wait_ge(s_cd, i * NCK + n - 1)
                        _, a, m = chunks[n]
                        for x in range(m):
                            ins = pe.transpose(PT[n % 2][:, x * P:(x + 1) * P], sc[s % 3][:, (a + x) * P:(a + x + 1) * P], c.ident[:, :])
                        ins.then_inc(s_t, 1)

                def values(s):
                    j, t = units[s]
                    u, kind = jobs[j]
                    pe.wait_ge(s_cd, i * NCK + of_unit[s][-1] + 1)
                    if t == 0 and kind == "fox":
                        pe.wait_ge(pa.s_vs[u], i + 1)
                    if t == 0 and kind == "sel":
                        pe.wait_ge(pa.s_gs, 4)
                    pe.wait_ge(s_n, i * NU + max(0, s - 1) + 1)
                    m = tiles(s)
                    for x in range(m):
                        at = first_tile(s) + x
                        for w_ in range(2):
                            ins = pe.matmul(O[s % 2][:, 0:2 * P], pT[s % 2][w_][:, x * P:(x + 1) * P],
                                            v[kind][u][:, at:at + 2, :, :].rearrange("p t w e -> p (t w e)"),
                                            start=(x == 0 and w_ == 0), stop=(x == m - 1 and w_ == 1))
                    ins.then_inc(s_o, 1)

                for s in range(NU + 3):
                    if s < NU:
                        scores(s)
                    if 0 <= s - 2 < NU:
                        turn(s - 2)
                    if 0 <= s - 3 < NU:
                        values(s - 3)

        @block.scalar
        def _(act):
            with act.Fori(0, 4) as i:
                for s in range(NU + 2):
                    if 0 <= s - 1 < NU:
                        e = s - 1
                        n = tiles(e) * P
                        act.wait_ge(s_m, i * NU + e + 2)
                        act.activation(sc[e % 3][:, 0:n], sc[e % 3][:, 0:n], ACT.Exp, bias=nm[:, e:e + 1], scale=-1.0,
                                       accum_out=sm[:, e:e + 1]).then_inc(s_e, 1)
                    if 0 <= s - 2 < NU:
                        e = s - 2
                        act.wait_ge(s_o, i * NU + max(0, e - 1) + 1)
                        for n in of_unit[e]:
                            _, a, m = chunks[n]
                            act.wait_ge(s_t, i * NCK + n + 2)
                            act.activation(pT[e % 2][0][:, a * P:(a + m) * P], PT[n % 2][:, 0:m * P], ACT.Copy).then_inc(s_ca, 1)

        @block.vector
        def _(dve):
            chain = Chain(dve, s_ch)
            dve.sem_inc(s_m, 1)
            dve.sem_inc(s_n, 1)
            dve.wait_ge(s_z, 4)
            per = sum(kind != "fox" for u, kind in jobs)
            with dve.Fori(0, 4) as i:
                chain.enter(i, per)

                def bias_and_max(s):
                    j, t = units[s]
                    u, kind = jobs[j]
                    n = tiles(s) * P
                    if t == 0 and kind == "fox":
                        dve.wait_ge(s_fb[u], 16 * i + 16)
                    if t == 0 and kind == "sel":
                        dve.wait_ge(s_nb[u], 32 * i + 32)
                    dve.wait_ge(s_t, i * NCK + (of_unit[s - 3][-1] + 2 if s >= 3 else 1))
                    dve.wait_ge(s_n, i * NU + 1)
                    dve.wait_ge(s_s, i * NU + s + 1)
                    settled(dve, c)
                    row = bias[kind][u][:, 0:n] if kind == "fox" else bias[kind][u][:, T - n:T]
                    dve.tensor_tensor_reduce(out=sc[s % 3][:, 0:n], in0=S[s % 2][:, 0:n], in1=row, scale=-1.0, scalar=3e38,
                                             op0=ALU.add, op1=ALU.min, accum_out=nm[:, s:s + 1]).then_inc(s_m, 1)

                def output(s):
                    j, t = units[s]
                    u, kind = jobs[j]
                    if t == 0:
                        dve.wait_ge(s_mg, 6 * i + j + 1)
                    dve.wait_ge(s_o, i * NU + s + 2)
                    dve.tensor_reduce(oj[j % 2][:, t, :], O[s % 2][:, 0:2 * HD].rearrange("p (w e) -> p e w", w=2), AX, ALU.add).then_inc(s_n, 1)
                    if t == NT - 1:
                        dve.wait_ge(s_e, i * NU + s + 1)
                        cj = co[:, j * NT:(j + 1) * NT]
                        ins = dve.reciprocal(cj, sm[:, j * NT:(j + 1) * NT])
                        if kind != "fox":
                            chain(ins)
                            h = i + GH * u
                            gate = c.gates[:, 0:NT, ds(h + (H if kind == "sel" else 2 * H), 1)]
                            ins = dve.tensor_tensor(cj, cj, gate.rearrange("p t a -> p (t a)"), ALU.mult)
                        ins.then_inc(s_co, 1)

                for s in range(NU + 4):
                    if s < NU:
                        bias_and_max(s)
                    if 0 <= s - 2 < NU:
                        e = s - 2
                        for n in of_unit[e]:
                            _, a, m = chunks[n]
                            dve.wait_ge(s_ca, i * NCK + n + 1)
                            dve.tensor_tensor(pT[e % 2][1][:, a * P:(a + m) * P], PT[n % 2][:, 0:m * P],
                                              pT[e % 2][0][:, a * P:(a + m) * P], ALU.subtract).then_inc(s_cd, 1)
                    if 0 <= s - 4 < NU:
                        output(s - 4)
            chain.leave(4)


def output_projection(c, oT):
    nc, d = c.nc, c.d
    with Phase(nc) as ph:
        w = ph.sb("w_out_sb", [P, 2, D])
        ws = split(ph, "w_out_split", [P, KD, D])
        x = [ph.sb(f"op_x{i}", [P, D]) for i in range(3)]
        acc = [ph.ps(f"op_acc{i}", [P, D]) for i in range(2)]
        s_w = [ph.sem(f"w_out_loaded{k}") for k in range(KD)]
        s_hi = ph.sem("w_out_rounded")
        s_lo = ph.sem("w_out_split")
        s_x = [ph.sem(f"op_x_loaded{i}") for i in range(3)]
        s_pe = ph.sem("op_products")
        s_v = ph.sem("op_added")
        s_st = [ph.sem(f"op_stored{i}") for i in range(3)]
        block = ph.block()

        @block.sync
        def _(sp):
            for k in range(KD):
                if k >= 2:
                    sp.wait_ge(s_lo, k - 1)
                sp.dma_start(w[:, k % 2, :], d["w_out"][0, k * P:(k + 1) * P, :]).then_inc(s_w[k], 16)
            for t, rows in enumerate(ROWS):
                if t >= 3:
                    sp.wait_ge(s_st[t % 3], 16 * (t // 3))
                src = d["x_prompt"][0, t * P:(t + 1) * P, :] if t < NT else d["x_sample"].rearrange("b q n -> (b q) n")
                sp.dma_start(x[t % 3][0:rows, :], src).then_inc(s_x[t % 3], 16)

        @block.tensor
        def _(pe):
            for t, rows in enumerate(ROWS):
                if t >= 2:
                    pe.wait_ge(s_v, t - 1)
                for k in range(KD):
                    if t == 0:
                        pe.wait_ge(s_lo, k + 1)
                    for a in range(2):
                        ins = split_products(pe, acc[t % 2][0:rows, a * 512:(a + 1) * 512], oT, ws, np.s_[:, k, t * P:t * P + rows],
                                             np.s_[:, k, a * 512:(a + 1) * 512], k == 0, k == KD - 1)
                ins.then_inc(s_pe, 1)

        @block.scalar
        def _(act):
            for k in range(KD):
                act.wait_ge(s_w[k], 16)
                act.activation(ws[0][:, k, :], w[:, k % 2, :], ACT.Copy).then_inc(s_hi, 1)

        @block.vector
        def _(dve):
            for k in range(KD):
                dve.wait_ge(s_hi, k + 1)
                dve.tensor_tensor(ws[1][:, k, :], w[:, k % 2, :], ws[0][:, k, :], ALU.subtract).then_inc(s_lo, 1)
            for t, rows in enumerate(ROWS):
                dve.wait_ge(s_x[t % 3], 16 * (t // 3 + 1))
                dve.wait_ge(s_pe, t + 1)
                dve.tensor_tensor(x[t % 3][0:rows, :], acc[t % 2][0:rows, :], x[t % 3][0:rows, :], ALU.add).then_inc(s_v, 1)

        @block.gpsimd
        def _(pool):
            for t, rows in enumerate(ROWS):
                pool.wait_ge(s_v, t + 1)
                pool.dma_start(d["x1_d"][t * P:t * P + rows, :], x[t % 3][0:rows, :]).then_inc(s_st[t % 3], 16)
            for i in range(3):
                pool.wait_ge(s_st[i], 16 * 3)


def gate_up(c, hT, act_T):
    nc, d = c.nc, c.d
    w_gu = d["w_gu"][0].rearrange("(k p) n -> p k n", p=P)
    SG = NQ + 2
    with Phase(nc) as ph:
        w = [ph.sb(f"w_{n}", [P, KD, P]) for n in ("gate", "up")]
        ws = [split(ph, f"w_{n}_split", [P, KD, P]) for n in ("gate", "up")]
        GW = 2 + T + NB * SG
        work = ph.sb("gate_work", [P, 2 * GW + 2 * TT])
        g = [work[:, i * GW:(i + 1) * GW] for i in range(2)]
        gc = [work[:, 2 * GW + i * TT:2 * GW + (i + 1) * TT] for i in range(2)]
        rows_io = work[0:2 + 2 * NB, 0:FF]
        cw_rows = ph.sb("conv_w_rows", [4 * NF, P])
        cw = ph.sb("conv_w_T", [P, 4, NF])
        cwn = [ph.sb(f"conv_w_now{i}", [P, 4]) for i in range(2)]
        hist = ph.sb("hist_T", [P, NF, 2 * NB])
        edge = ph.sb("edge_T", [P, NF, 2 + 2 * NB])
        G_ = ph.ps("gate_acc", [P, 3, 512])
        U_ = ph.ps("up_acc", [P, 3, 512])
        E_ = [ph.ps(f"edge_ps{i}", [P, 4, P]) for i in range(2)]
        s_ld = ph.sem("conv_tables_loaded")
        s_et = ph.sem("hist_turned")
        s_ec = ph.sem("hist_copied")
        s_w = [ph.sem(f"w_{n}_loaded") for n in ("gate", "up")]
        s_hi = [ph.sem(f"w_{n}_rounded") for n in ("gate", "up")]
        s_lo = [ph.sem(f"w_{n}_split") for n in ("gate", "up")]
        s_g = ph.sem("gate_products")
        s_u = ph.sem("up_products")
        s_gc = ph.sem("gate_copied")
        s_z = ph.sem("halo_zeroed")
        s_cv = ph.sem("convolved")
        s_si = ph.sem("silu_done")
        s_a = ph.sem("act_done")
        s_ch = ph.sem("gu_chain")
        s_xt = ph.sem("edge_turned")
        s_xc = ph.sem("edge_copied")
        s_st = ph.sem("edge_stored")
        block = ph.block()
        NE = (NF + 3) // 4

        @block.sync
        def _(sp):
            sp.dma_start(cw_rows[0:3 * NF, :], d["conv_w"][0].rearrange("w (f p) -> (w f) p", p=P)).then_inc(s_ld, 16)
            sp.dma_start(cw_rows[3 * NF:4 * NF, :], d["conv_b"][0].rearrange("(f p) -> f p", p=P)).then_inc(s_ld, 16)
            sp.dma_start(rows_io[0:2 * NB, :], d["state_conv"][0].rearrange("b r n -> (b r) n")).then_inc(s_ld, 16)
            for side in range(2):
                sp.sem_inc(s_lo[side], 1)
            with sp.Fori(0, NF) as f:
                for side in range(2):
                    sp.wait_ge(s_lo[side], f + 1)
                    sp.dma_start(w[side][:, :, :], w_gu[:, :, ds(f * P + side * FF, P)]).then_inc(s_w[side], 16)

        @block.tensor
        def _(pe):
            pe.wait_ge(s_ld, 48)
            pe.transpose(E_[0][:, 0, 0:4 * NF], cw_rows[:, :], c.ident[0:4 * NF, 0:4 * NF]).then_inc(s_et, 1)
            for f in range(NF):
                if f % 4 == 0:
                    pe.wait_ge(s_ec, f // 4 if f else 1)
                ins = pe.transpose(E_[(f // 4 + 1) % 2][:, f % 4, 0:2 * NB], rows_io[0:2 * NB, f * P:(f + 1) * P],
                                   c.ident[0:2 * NB, 0:2 * NB])
                if f % 4 == 3 or f == NF - 1:
                    ins.then_inc(s_et, 1)
            with pe.Fori(0, NF // 2) as i:
                for b in range(2):
                    f = 2 * i + b
                    for side, (acc, sem, free) in enumerate(((G_, s_g, s_gc), (U_, s_u, s_a))):
                        pe.wait_ge(s_lo[side], f + 2)
                        pe.wait_ge(free, f + 1)
                        for n in range(3):
                            for k in range(KD):
                                ins = split_products(pe, acc[:, n, 0:CH], ws[side], hT, np.s_[:, k, :],
                                                     np.s_[:, k, n * CH:(n + 1) * CH], k == 0, k == KD - 1)
                        ins.then_inc(sem, 1)
            for f in range(NF):
                if f % 4 == 0:
                    pe.wait_ge(s_cv, NF + 1)
                    if f // 4 >= 2:
                        pe.wait_ge(s_xc, f // 4 - 1)
                ins = pe.transpose(E_[f // 4 % 2][0:2 + 2 * NB, f % 4, :], edge[:, f, :], c.ident[:, :])
                if f % 4 == 3 or f == NF - 1:
                    ins.then_inc(s_xt, 1)

        @block.scalar
        def _(act):
            act.wait_ge(s_z, 2)
            act.wait_ge(s_ec, NE + 1)
            act.sem_inc(s_gc, 1)
            act.sem_inc(s_g, 1)
            act.sem_inc(s_u, 1)
            with act.Fori(0, NF // 2) as i:
                for b in range(2):
                    f = 2 * i + b
                    for side, used in enumerate((s_g, s_u)):
                        act.wait_ge(s_w[side], 16 * f + 16)
                        act.wait_ge(used, f + 1)
                        act.activation(ws[side][0][:, :, :], w[side][:, :, :], ACT.Copy).then_inc(s_hi[side], 1)
                    act.wait_ge(s_g, f + 2)
                    act.wait_ge(s_cv, f + 1)
                    new = g[b][:, 2 + T:].rearrange("p (b r) -> p b r", b=NB)
                    act.activation(g[b][:, 2:2 + 2 * CH].rearrange("p (a n) -> p a n", a=2), G_[:, 0:2, 0:CH], ACT.Copy)
                    act.activation(g[b][:, 2 + 2 * CH:2 + T], G_[:, 2, 0:CH - NS], ACT.Copy)
                    act.activation(new[:, :, 2:SG], G_[:, 2, CH - NS:CH].rearrange("p (b q) -> p b q", q=NQ), ACT.Copy).then_inc(s_gc, 1)
                    act.wait_ge(s_cv, f + 2)
                    act.activation(gc[b], gc[b], ACT.Silu).then_inc(s_si, 1)

        @block.vector
        def _(dve):
            dve.wait_ge(s_et, 1)
            dve.tensor_copy(cw[:, :, :].rearrange("p w f -> p (w f)"), E_[0][:, 0, 0:4 * NF]).then_inc(s_ec, 1)
            for n in range(NE):
                m = min(4, NF - 4 * n)
                dve.wait_ge(s_et, n + 2)
                dve.tensor_copy(hist[:, 4 * n:4 * n + m, :], E_[(n + 1) % 2][:, 0:m, 0:2 * NB]).then_inc(s_ec, 1)
            dve.wait_ge(s_ec, NE + 1)
            for b in range(2):
                dve.memset(g[b][:, 0:2], 0.0).then_inc(s_z, 1)
            dve.wait_ge(s_z, 2)
            dve.sem_inc(s_cv, 1)
            dve.sem_inc(s_a, 1)
            chain = Chain(dve, s_ch)
            with dve.Fori(0, NF // 2) as i:
                chain.enter(i, 2 * 3)
                for b in range(2):
                    f = 2 * i + b
                    k = cwn[b]
                    new = g[b][:, 2 + T:].rearrange("p (b r) -> p b r", b=NB)
                    out = gc[b][:, T:].rearrange("p (b q) -> p b q", q=NQ)
                    dve.wait_ge(s_a, f + 1)
                    dve.tensor_copy(k[:, :], cw[:, :, ds(f, 1)].rearrange("p w a -> p (w a)"))
                    chain(dve.tensor_copy(new[:, :, 0:2], hist[:, ds(f, 1), :].rearrange("p a (b r) -> p (a b) r", r=2)))
                    dve.wait_ge(s_gc, f + 2)
                    dve.tensor_copy(edge[:, ds(f, 1), 0:2].rearrange("p a r -> p (a r)"), g[b][:, T:T + 2])
                    dve.tensor_copy(edge[:, ds(f, 1), 2:].rearrange("p a (b r) -> p (a b) r", r=2), new[:, :, NQ:SG])
                    for w_ in range(3):
                        for dst, src in ((gc[b][:, 0:T], g[b][:, w_:w_ + T]), (out, new[:, :, w_:w_ + NQ])):
                            if w_ == 0:
                                ins = dve.tensor_scalar(dst, src, k[:, 0:1], k[:, 3:4], ALU.mult, ALU.add)
                            else:
                                ins = dve.scalar_tensor_tensor(out=dst, in0=src, scalar=k[:, w_:w_ + 1], in1=dst,
                                                               op0=ALU.mult, op1=ALU.add)
                        if w_ < 2:
                            chain(ins)
                        else:
                            ins.then_inc(s_cv, 1)
                    dve.wait_ge(s_si, f + 1)
                    dve.wait_ge(s_u, f + 2)
                    dve.tensor_tensor(act_T[:, ds(f, 1), :].rearrange("p a (m n) -> p (a m) n", m=3),
                                      gc[b].rearrange("p (m n) -> p m n", m=3), U_[:, :, 0:CH], ALU.mult).then_inc(s_a, 1)
            chain.leave(NF // 2)
            dve.wait_ge(s_a, NF + 1)
            for n in range(NE):
                m = min(4, NF - 4 * n)
                dve.wait_ge(s_xt, n + 1)
                dve.tensor_copy(rows_io[:, n * 512:n * 512 + m * P], E_[n % 2][0:2 + 2 * NB, 0:m, :].rearrange("p a n -> p (a n)"))\
                   .then_inc(s_xc, 1)

        @block.gpsimd
        def _(pool):
            with pool.Fori(0, NF) as f:
                for side in range(2):
                    pool.wait_ge(s_hi[side], f + 1)
                    pool.tensor_tensor(ws[side][1][:, :, :], w[side][:, :, :], ws[side][0][:, :, :], ALU.subtract).then_inc(s_lo[side], 1)
            pool.wait_ge(s_xc, NE)
            pool.dma_start(d["conv_p"][0, 0], rows_io[0:2, :]).then_inc(s_st, 16)
            pool.dma_start(d["conv_s"][0].rearrange("b r n -> (b r) n"), rows_io[2:2 + 2 * NB, :]).then_inc(s_st, 16)
            pool.wait_ge(s_st, 32)


def down(c, act_T):
    nc, d = c.nc, c.d
    HW, TG, NG = D // 2, 3, 3
    NP = NF // 2
    passes = [(half, grp) for half in range(2) for grp in range(NG)]
    with Phase(nc) as ph:
        w = ph.sb("w_down_half", [P, NF, HW])
        ws = [split(ph, f"w_down_split{b}", [P, HW]) for b in range(2)]
        a_s = [split(ph, f"act_split{b}", [P, TG * P]) for b in range(2)]
        y = ph.sb("y_rows", [P, 9, D])
        g = ph.sb("final_gain", [P, D])
        sq = ph.sb("y_squares", [P, D])
        ss = ph.sb("y_ss", [P, 4, 9])
        acc = [[ph.ps(f"y_acc{i}_{t}", [P, HW]) for t in range(TG)] for i in range(2)]
        s_r = [ph.sem(f"w_down_pair_loaded{i}") for i in range(4)]
        s_w = ph.sem("w_down_pairs")
        s_x = ph.sem("x1_loaded")
        s_g = ph.sem("final_gain_loaded")
        s_hi = ph.sem("down_rounded")
        s_lo = ph.sem("down_split")
        s_pe = ph.sem("down_products")
        s_v = ph.sem("down_added")
        s_z = ph.sem("y_ss_zeroed")
        s_sq = ph.sem("y_squared")
        s_ms = ph.sem("y_mean")
        s_rt = ph.sem("y_root")
        s_rr = ph.sem("y_inverse")
        s_y = ph.sem("y_normed")
        s_st = ph.sem("y_stored")
        block = ph.block()
        w_d = d["w_down"][0].rearrange("(f p) n -> p f n", p=P)

        def tiles_of(grp):
            return range(TG * grp, TG * grp + TG)

        def in_pairs(eng, body, q, between):
            cuts = sorted({1, NP - 1} | {p + 1 for p in between})
            body(q, 0, True, False)
            between.get(0, lambda: None)()
            for a, b in zip(cuts, cuts[1:]):
                with eng.Fori(a, b) as p:
                    body(q, p, False, False)
                between.get(b - 1, lambda: None)()
            body(q, NP - 1, False, True)

        @block.sync
        def _(sp):
            def load(n):
                half, p = n // NP, n % NP
                if half:
                    sp.wait_ge(s_lo, ((NG - 1) * NP + p + 1) * 2)
                sp.dma_start(w[:, 2 * p:2 * p + 2, :], w_d[:, 2 * p:2 * p + 2, half * HW:(half + 1) * HW]).then_inc(s_r[n % 4], 16)

            def loaded(n):
                sp.wait_ge(s_r[n % 4], 16 * (n // 4 + 1))
                sp.sem_inc(s_w, 1)

            for n in range(2 * NP):
                if n >= NP + 3 or 3 <= n < NP:
                    loaded(n - 3)
                if n == NP:
                    for m in range(NP - 3, NP):
                        loaded(m)
                load(n)
                if n == 3:
                    sp.dma_start(y[:, 0:NT, :], d["x1_d"][0:T, :].rearrange("(t p) n -> p t n", p=P)).then_inc(s_x, 16)
                    sp.dma_start(y[0:NS, NT, :], d["x1_d"][T:TT, :]).then_inc(s_x, 16)
                    sp.dma_start(g[:, :], d["final_norm_g"].rearrange("(a n) -> a n", a=1).to_broadcast([P, D])).then_inc(s_g, 16)
            for n in range(2 * NP - 3, 2 * NP):
                loaded(n)

        @block.tensor
        def _(pe):
            def pair(q, p, first, last):
                half, grp = passes[q]
                if first and q >= 2:
                    pe.wait_ge(s_v, q - 1)
                for b in range(2):
                    pe.wait_ge(s_lo, (q * NP + p) * 2 + b + 1)
                    for x, t in enumerate(tiles_of(grp)):
                        rows = ROWS[t]
                        ins = split_products(pe, acc[q % 2][x][0:rows, :], a_s[b], ws[b], np.s_[:, x * P:x * P + rows], np.s_[:, :],
                                             first and b == 0, last and b == 1)
                    ins.then_inc(s_pe, 1)

            for q in range(len(passes)):
                in_pairs(pe, pair, q, {})

        @block.scalar
        def _(act):
            act.sem_inc(s_pe, 2)

            def pair(q, p, first, last):
                half, grp = passes[q]
                n = sum(ROWS[t] for t in tiles_of(grp))
                if grp == 0:
                    act.wait_ge(s_w, half * NP + p + 1)
                for b in range(2):
                    act.wait_ge(s_pe, (q * NP + p) * 2 + b + 1)
                    f = ds(2 * p + b, 1)
                    act.activation(ws[b][0][:, :], w[:, f, :].rearrange("p a n -> p (a n)"), ACT.Copy).then_inc(s_hi, 1)
                    act.activation(a_s[b][0][:, 0:n], act_T[:, f, grp * TG * P:grp * TG * P + n].rearrange("p a n -> p (a n)"),
                                   ACT.Copy).then_inc(s_hi, 1)

            def squares(grp):
                act.wait_ge(s_v, NG + grp + 1)
                for t in tiles_of(grp):
                    if t:
                        act.wait_ge(s_sq, t)
                    act.activation(sq[0:ROWS[t], :], y[0:ROWS[t], t, :], ACT.Square, accum_out=ss[0:ROWS[t], 0, t:t + 1]).then_inc(s_sq, 1)

            def roots(grp):
                t = TG * grp
                act.wait_ge(s_ms, grp + 1)
                act.activation(ss[:, 2, t:t + TG], ss[:, 1, t:t + TG], ACT.Sqrt).then_inc(s_rt, 1)

            for q in range(len(passes)):
                between = {} if q <= NG else {3: lambda: squares(q - NG - 1), 5: lambda: roots(q - NG - 1)}
                in_pairs(act, pair, q, between)
            squares(NG - 1)
            roots(NG - 1)

        @block.vector
        def _(dve):
            dve.memset(ss[:, 0, :], 0.0).then_inc(s_z, 1)
            dve.wait_ge(s_z, 1)

            def pair(q, p, first, last):
                half, grp = passes[q]
                n = sum(ROWS[t] for t in tiles_of(grp))
                for b in range(2):
                    step = (q * NP + p) * 2 + b
                    dve.wait_ge(s_hi, 2 * step + 1)
                    f = ds(2 * p + b, 1)
                    dve.tensor_tensor(ws[b][1][:, :], w[:, f, :].rearrange("p a n -> p (a n)"), ws[b][0][:, :], ALU.subtract)
                    dve.wait_ge(s_hi, 2 * step + 2)
                    dve.tensor_tensor(a_s[b][1][:, 0:n], act_T[:, f, grp * TG * P:grp * TG * P + n].rearrange("p a n -> p (a n)"),
                                      a_s[b][0][:, 0:n], ALU.subtract).then_inc(s_lo, 1)

            def add(q):
                half, grp = passes[q]
                if q == 0:
                    dve.wait_ge(s_x, 32)
                dve.wait_ge(s_pe, (q + 1) * NF + 2)
                for x, t in enumerate(tiles_of(grp)):
                    dst = y[0:ROWS[t], t, half * HW:(half + 1) * HW]
                    ins = dve.tensor_tensor(dst, acc[q % 2][x][0:ROWS[t], :], dst, ALU.add)
                ins.then_inc(s_v, 1)

            def means(grp):
                t = TG * grp
                dve.wait_ge(s_sq, t + TG)
                dve.tensor_scalar(ss[:, 1, t:t + TG], ss[:, 0, t:t + TG], 1.0 / D, EPS, ALU.mult, ALU.add).then_inc(s_ms, 1)

            def inverses(grp):
                t = TG * grp
                dve.wait_ge(s_rt, grp + 1)
                dve.reciprocal(ss[:, 3, t:t + TG], ss[:, 2, t:t + TG]).then_inc(s_rr, 1)
                dve.wait_ge(s_rr, grp + 1)
                if grp == 0:
                    dve.wait_ge(s_g, 16)

            def scaled(t):
                rows = ROWS[t]
                dve.scalar_tensor_tensor(out=y[0:rows, t, :], in0=y[0:rows, t, :], scalar=ss[0:rows, 3, t:t + 1],
                                         in1=g[0:rows, :], op0=ALU.mult, op1=ALU.mult).then_inc(s_y, 1)

            for q in range(len(passes)):
                between = {0: lambda: add(q - 1)} if q else {}
                if q > NG:
                    grp = q - NG - 1
                    between.update({4: lambda: means(grp), 6: lambda: (inverses(grp), scaled(TG * grp)),
                                    7: lambda: scaled(TG * grp + 1), 8: lambda: scaled(TG * grp + 2)})
                in_pairs(dve, pair, q, between)
            add(len(passes) - 1)
            means(NG - 1)
            inverses(NG - 1)
            for t in tiles_of(NG - 1):
                scaled(t)

        @block.gpsimd
        def _(pool):
            for t, rows in enumerate(ROWS):
                pool.wait_ge(s_y, t + 1)
                dst = d["y_p"][0, t * P:(t + 1) * P, :] if t < NT else d["y_s"].rearrange("b q n -> (b q) n")
                pool.dma_start(dst, y[0:rows, t, :]).then_inc(s_st, 16)
            pool.wait_ge(s_st, 16 * 9)


def buckets(n):
    n = np.asarray(n)
    exact = NBK // 2
    far = exact + (np.log(np.maximum(n, 1) / exact) / math.log(128 / exact) * (NBK - exact) + 1e-9).astype(np.int64)
    return np.where(n < exact, np.maximum(n, 0), np.minimum(far, NBK - 1))


def one_hot(dist):
    dist = np.asarray(dist)
    b = buckets(dist)
    m = (np.arange(NBK).reshape((-1,) + (1,) * dist.ndim) == b[None]) & (dist >= 0)[None]
    return np.concatenate([m.astype(np.float32), np.where(dist < 0, np.float32(NEG), np.float32(0))[None]])


MISC = {}


def constants():
    c = {}
    c["c_oh"] = one_hot(255 - np.arange(383))
    m = np.arange(16) - 9
    c["c_cmp"] = one_hot(np.arange(P)[None, :] - (CLEN - 1) - NSTR * m[:, None])
    q = np.arange(NQ)[:, None]
    near = 768 + 2 * np.arange(P)[None, :] + np.arange(2)[:, None]
    smp = np.concatenate([
        T + q - near.reshape(1, -1),
        q - np.arange(NQ)[None, :],
        T + q - (T - P + np.arange(P))[None, :],
        T + q - (NSTR * np.arange(NC) + CLEN - 1)[None, :]], axis=1)
    c["c_smp"] = one_hot(smp)
    rel = np.zeros((NBK, NBK + 1), np.float32)
    rel[np.arange(NBK), np.arange(NBK)] = 1
    rel[NBK - 1, 0:NBK] -= 1
    c["c_rel"] = rel
    c["c_one"] = np.eye(NBK + 1, dtype=np.float32)[:, NBK:]
    parts = {}
    w = np.arange(P)
    parts["wmask"] = np.where(w[None, :] <= w[:, None], np.float32(NEG), np.float32(0))
    hq = np.arange(HQ)
    wm = np.zeros((P, P), np.float32)
    wm[:HQ] = np.where(w[None, :] <= (hq % NQ)[:, None], np.float32(NEG), np.float32(0))
    parts["wmask_s"] = wm
    ms = np.zeros((P, NSEL), np.float32)
    st, js = np.arange(NC) * NSTR, np.arange(NSEL) * HD
    ms[:NC] = (st[:, None] < js[None, :] + HD) & (st[:, None] + CLEN > js[None, :])
    parts["to_sel"] = ms
    gs = np.zeros((P, HQ), np.float32)
    gs[:HQ] = (hq[:, None] // (NQ * GH) == hq[None, :] // (NQ * GH)) & (hq[:, None] % NQ == hq[None, :] % NQ)
    parts["group_sum"] = gs
    bm = np.zeros((P, H * HD), np.float32)
    bm[:HQ] = np.repeat(hq[:, None] // NQ == np.arange(H)[None, :], HD, axis=1)
    parts["own_head"] = bm
    gm = np.zeros((P, G), np.float32)
    gm[:HQ] = hq[:, None] // (NQ * GH) == np.arange(G)[None, :]
    parts["own_group"] = gm
    parts["block_no"] = np.tile(np.arange(1, 15, dtype=np.float32), (P, 1))
    ne = np.zeros((P, HQ), np.float32)
    ne[:H] = -(np.arange(H)[:, None] == hq[None, :] // NQ).astype(np.float32)
    parts["neg_head"] = ne
    seen = np.ones((P, NT, H), np.float32)
    seen[0:CLEN - 1, 0] = 0
    parts["seen"] = seen.reshape(P, NT * H)
    cm = np.zeros((P, NQ), np.float32)
    cm[:HQ] = np.where(np.arange(NQ)[None, :] > (hq % NQ)[:, None], np.float32(NEG), np.float32(0))
    parts["causal_new"] = cm
    at = 0
    for k, v in parts.items():
        MISC[k] = (at, at + v.shape[1])
        at += v.shape[1]
    c["c_misc"] = np.concatenate(list(parts.values()), axis=1).astype(np.float32)
    return c


def build(nc, d):
    c = Ctx(nc, d)
    with Phase(nc) as top, nc.allow_non_contiguous_dma(reason="small tables of single elements"):
        c.passed = top.sem("passed")
        c.ident = top.sb("ident", [P, P])
        c.ident16 = top.sb("ident16", [P, P], BF16)
        c.causal16 = top.sb("causal16", [P, P], BF16)
        c.one = top.sb("one", [H, 1])
        c.zero = top.sb("zero", [P, 1])
        with Phase(nc) as mix:
            c.cb = mix.sb("cb", [P, H, 119])
            c.bias_s = mix.sb("bias_s", [HQ, 451])
            c.misc = mix.sb("misc", [P, d["c_misc"].shape[1]])
            c.pt = mix.sb("page_ids", [1, NB * PAGES], I32)
            c.gates = mix.sb("gates", [P, 9, 24])
            setup(c)
            c.q_smp = mix.sb("q_smp", [P, 2, 4, NS])
            c.kf_new = mix.sb("kf_new", [P, 4, NS])
            c.ks_new = mix.sb("ks_new", [P, 1, NS])
            c.kw_new = mix.sb("kw_new", [P, 1, NS])
            c.lf_new = mix.sb("lf_new", [H, NS])
            c.kc_p = mix.sb("kc_prompt", [P, NC])
            c.vc_p = mix.sb("vc_prompt", [NC, G * HD])
            with Phase(nc) as ph:
                hT = c.hT = split(ph, "h_T", [P, KD, TT])
                norm_transpose(c, "n1", lambda t: d["x_prompt"][0, t * P:(t + 1) * P, :] if t < NT
                               else d["x_sample"].rearrange("b q n -> (b q) n"),
                               d["norm1_g"][0:1, :].to_broadcast([P, D]), 1, hT)
                w_rows = [ph.sb(f"w_rows{i}", [P, KD, 512]) for i in range(2)]
                s_wr = [ph.sem(f"w_rows_loaded{i}") for i in range(4)]
                project_transposed(c, w_rows, s_wr)
                project_rows(c, w_rows, s_wr)
            with Phase(nc) as ph:
                pages = SamplePages(c, ph)
                c.w1 = ph.sb("cmp_w1_sb", [P, 2, 16, 256])
                c.w2 = ph.sb("cmp_w2_sb", [P, 2, 2, HD])
                c.b1 = ph.sb("cmp_b1_sb", [P, 2, 2])
                prompt_compress(c, pages)
                sample_attention(c, pages)
            with Phase(nc) as ph:
                c.o = ph.sb("o_prompt", [P, NT, D])
                with Phase(nc) as inputs:
                    pa = AttentionInputs(c, inputs)
                    compressed_attention(c, pa)
                    prompt_attention(c, pa)
                oT = split(ph, "o_T", [P, KD, TT])
                norm_transpose(c, "no", lambda t: d["os_d"], d["out_norm_g"][0:1, :].to_broadcast([P, D]), 2, oT, c.o)
                output_projection(c, oT)
        with Phase(nc) as ph:
            act_T = ph.sb("act_T", [P, NF, TT])
            with Phase(nc) as inner:
                h2T = split(inner, "h2_T", [P, KD, TT])
                norm_transpose(c, "n2", lambda t: d["x1_d"][t * P:t * P + ROWS[t], :],
                               d["norm2_g"][0:1, :].to_broadcast([P, D]), 1, h2T)
                gate_up(c, h2T, act_T)
            down(c, act_T)
    return c


_OUTS = [("y_p", (1, T, D)), ("y_s", (NB, NQ, D)),
         ("fox_kv_p", (1, 1, T, 2, H, HD)), ("fox_kv_s", (1, NB, NQ, 2, H, HD)),
         ("logf_p", (1, 1, T, H)), ("logf_s", (1, NB, NQ, H)),
         ("nsa_kv_p", (1, 1, T, 4, G, HD)), ("nsa_kv_s", (1, NB, NQ, 4, G, HD)),
         ("win_kv_p", (1, 1, WIN, 2, G, HD)), ("win_kv_s", (1, NB, WIN, 2, G, HD)),
         ("conv_p", (1, 1, 2, FF)), ("conv_s", (1, NB, 2, FF))]
_SCRATCH = [("qfs_d", (2, H, HD, T)), ("qns_d", (2, H, HD, T)), ("kf_d", (2, H, HD, T)), ("qn_d", (H, HD, T)),
            ("ks_d", (2, G, HD, T)), ("kw_d", (2, G, HD, T)), ("vw_d", (T, G * HD)),
            ("nc_d", (H, T)), ("rep_d", (H, P, 383)), ("tb_d", (H, P, 256)), ("os_d", (NS, D)), ("gs_d", (NS, 24)),
            ("x1_d", (TT, D))]


def declare(nc, inputs):
    arrays, d = {}, {}
    for name, a in {**inputs, **constants()}.items():
        a = np.ascontiguousarray(a)
        arrays[f"in_{name}"] = a
        d[name] = nc.dram_tensor(f"in_{name}", a.shape, mybir.dt.from_np(a.dtype), kind="ExternalInput").ap()
    for name, shape in _OUTS:
        d[name] = nc.dram_tensor(f"out_{name}", shape, F32, kind="ExternalOutput").ap()
    for name, shape in _SCRATCH:
        d[name] = nc.dram_tensor(f"scratch_{name}", shape, F32, kind="Internal").ap()
    return arrays, d


def kernel(**inputs):
    import concourse.bacc as bacc
    from concourse.bass_utils import run_bass_kernel_spmd

    nc = bacc.Bacc("TRN2", target_bir_lowering=False, num_devices=1)
    arrays, d = declare(nc, inputs)
    build(nc, d)
    r = run_bass_kernel_spmd(nc, [arrays], core_ids=[0])
    return tuple(r.results[0][f"out_{name}"] for name, _ in _OUTS)
```
